# Optimizing a Trainium2 kernel written in Bass

```python
import jax, jax.numpy as jnp
from jax import lax
import numpy as np

D_MODEL = 1024
BATCH = 1
SEQ = 1024
DEPTH = 1

RET_HEADS = 4
RET_QK_DIM = D_MODEL // RET_HEADS
RET_V_DIM = 2 * RET_QK_DIM
RET_QK_WIDTH = RET_HEADS * RET_QK_DIM
RET_V_WIDTH = RET_HEADS * RET_V_DIM
RET_CHUNK = 128
ROPE_BASE = 10000.0
LRU_WIDTH = D_MODEL
LRU_BLOCK = 256
LRU_BLOCKS = LRU_WIDTH // LRU_BLOCK
LRU_CONV = 4
LRU_C = 8.0
FFN_HIDDEN = ((8 * D_MODEL // 3 + 255) // 256) * 256
FFN_CONV = 3
NORM_EPS = 1e-6
GN_EPS = 1e-5

IN_SIZES = (RET_QK_WIDTH, RET_QK_WIDTH, RET_V_WIDTH, RET_V_WIDTH, LRU_WIDTH, LRU_WIDTH, D_MODEL, D_MODEL)
IN_WIDTH = sum(IN_SIZES)
SPLIT_POINTS = [int(v) for v in np.cumsum(IN_SIZES)[:-1]]

kernel_name = "hybrid_retention_rglru_convffn"

def rms_norm(x, g):
    xf = x.astype(jnp.float32)
    y = xf * lax.rsqrt(jnp.mean(jnp.square(xf), axis=-1, keepdims=True) + NORM_EPS)
    return (y * g.astype(jnp.float32)).astype(x.dtype)

def head_norm(o, g):
    b, s = o.shape[0], o.shape[1]
    of = o.astype(jnp.float32)
    mu = jnp.mean(of, axis=-1, keepdims=True)
    var = jnp.mean(jnp.square(of - mu), axis=-1, keepdims=True)
    y = ((of - mu) * lax.rsqrt(var + GN_EPS)).reshape(b, s, -1)
    return (y * g.astype(jnp.float32)).astype(o.dtype)

def rotary(t, cos, sin):
    t1, t2 = jnp.split(t, 2, axis=-1)
    c = cos[None, :, None, :]
    s = sin[None, :, None, :]
    return jnp.concatenate([t1 * c - t2 * s, t1 * s + t2 * c], axis=-1)

def causal_depthwise_conv(x, w, b):
    width, ch = w.shape
    y = lax.conv_general_dilated(x, w[:, None, :].astype(x.dtype), window_strides=(1,),
                                 padding=((width - 1, 0),), dimension_numbers=('NWC', 'WIO', 'NWC'),
                                 feature_group_count=ch)
    return y + b.astype(x.dtype)

def retention(q, k, v):
    b, s, h, dk = q.shape
    dv = v.shape[-1]
    nc = s // RET_CHUNK
    dt = q.dtype

    def chunks(t):
        return t.reshape(b, nc, RET_CHUNK, h, t.shape[-1]).transpose(1, 0, 3, 2, 4)

    log_g = jnp.log1p(-jnp.exp2(-5.0 - jnp.arange(h, dtype=jnp.float32)))
    pos = jnp.arange(RET_CHUNK, dtype=jnp.float32)
    rel = pos[:, None] - pos[None, :]
    decay_in = jnp.where(rel >= 0, jnp.exp(log_g[:, None, None] * jnp.maximum(rel, 0.0)), 0.0).astype(dt)
    decay_q = jnp.exp(log_g[:, None] * (pos + 1.0)).astype(dt)
    decay_k = jnp.exp(log_g[:, None] * (RET_CHUNK - 1.0 - pos)).astype(dt)
    decay_chunk = jnp.exp(log_g * RET_CHUNK).astype(dt)

    def step(state, qkv):
        qi, ki, vi = qkv
        scores = jnp.einsum('bhnd,bhmd->bhnm', qi, ki) * decay_in
        o = (jnp.einsum('bhnm,bhmv->bhnv', scores, vi)
             + jnp.einsum('bhnd,bhdv->bhnv', qi, state) * decay_q[:, :, None])
        state = (state * decay_chunk[:, None, None]
                 + jnp.einsum('bhmd,bhmv->bhdv', ki * decay_k[:, :, None], vi))
        return state, o

    init = jnp.zeros((b, h, dk, dv), dt)
    _, o = lax.scan(step, init, (chunks(q), chunks(k), chunks(v)))
    return o.transpose(1, 0, 3, 2, 4).reshape(b, s, h, dv)

def rg_lru(x, w_a, b_a, w_i, b_i, a_param):
    b, s, _ = x.shape
    xb = x.reshape(b, s, LRU_BLOCKS, LRU_BLOCK)
    r = jax.nn.sigmoid((jnp.einsum('bsnc,ncd->bsnd', xb, w_a) + b_a).reshape(b, s, LRU_WIDTH).astype(jnp.float32))
    i = jax.nn.sigmoid((jnp.einsum('bsnc,ncd->bsnd', xb, w_i) + b_i).reshape(b, s, LRU_WIDTH).astype(jnp.float32))
    log_a = -LRU_C * r * jax.nn.softplus(-a_param.astype(jnp.float32))
    a = jnp.exp(log_a)
    u = jnp.sqrt(-jnp.expm1(2.0 * log_a)) * i * x.astype(jnp.float32)

    def combine(left, right):
        return (left[0] * right[0], right[0] * left[1] + right[1])

    _, hs = lax.associative_scan(combine, (a, u), axis=1)
    return hs.astype(x.dtype)

def setup_inputs(seed: int = 0) -> dict:
    key = jax.random.key(seed)
    ks = jax.random.split(key, 24)
    f = jnp.float32

    def nrm(k, shape, scale):
        return jax.random.normal(k, shape, f) * scale

    u = jax.random.uniform(ks[12], (DEPTH, LRU_WIDTH), f, 0.9, 0.999)
    a0 = u ** (1.0 / LRU_C)
    return {
        "x": nrm(ks[0], (BATCH, SEQ, D_MODEL), 1.0),
        "in_norm_g": 1.0 + nrm(ks[1], (DEPTH, D_MODEL), 0.02),
        "w_in": nrm(ks[2], (DEPTH, D_MODEL, IN_WIDTH), D_MODEL ** -0.5),
        "ret_gn_g": 1.0 + nrm(ks[3], (DEPTH, RET_V_WIDTH), 0.02),
        "w_ret_o": nrm(ks[4], (DEPTH, RET_V_WIDTH, D_MODEL), RET_V_WIDTH ** -0.5),
        "lru_conv_w": nrm(ks[5], (DEPTH, LRU_CONV, LRU_WIDTH), LRU_CONV ** -0.5),
        "lru_conv_b": nrm(ks[6], (DEPTH, LRU_WIDTH), 0.02),
        "lru_w_a": nrm(ks[7], (DEPTH, LRU_BLOCKS, LRU_BLOCK, LRU_BLOCK), LRU_BLOCK ** -0.5),
        "lru_b_a": nrm(ks[8], (DEPTH, LRU_BLOCKS, LRU_BLOCK), 0.02),
        "lru_w_i": nrm(ks[9], (DEPTH, LRU_BLOCKS, LRU_BLOCK, LRU_BLOCK), LRU_BLOCK ** -0.5),
        "lru_b_i": nrm(ks[10], (DEPTH, LRU_BLOCKS, LRU_BLOCK), 0.02),
        "lru_a_param": jnp.log(a0) - jnp.log1p(-a0),
        "w_rnn_o": nrm(ks[13], (DEPTH, LRU_WIDTH, D_MODEL), LRU_WIDTH ** -0.5),
        "w_out": nrm(ks[14], (DEPTH, D_MODEL, D_MODEL), D_MODEL ** -0.5),
        "ffn_norm_g": 1.0 + nrm(ks[15], (DEPTH, D_MODEL), 0.02),
        "w_up": nrm(ks[16], (DEPTH, D_MODEL, 2 * FFN_HIDDEN), D_MODEL ** -0.5),
        "ffn_conv_w": nrm(ks[17], (DEPTH, FFN_CONV, 2 * FFN_HIDDEN), FFN_CONV ** -0.5),
        "ffn_conv_b": nrm(ks[18], (DEPTH, 2 * FFN_HIDDEN), 0.02),
        "w_down": nrm(ks[19], (DEPTH, FFN_HIDDEN, D_MODEL), FFN_HIDDEN ** -0.5),
        "final_norm_g": 1.0 + nrm(ks[20], (D_MODEL,), 0.02),
    }

def reference(x, in_norm_g, w_in, ret_gn_g, w_ret_o, lru_conv_w, lru_conv_b, lru_w_a, lru_b_a,
              lru_w_i, lru_b_i, lru_a_param, w_rnn_o, w_out, ffn_norm_g, w_up, ffn_conv_w,
              ffn_conv_b, w_down, final_norm_g):
    b, s, _ = x.shape
    pos = jnp.arange(s, dtype=jnp.float32)
    inv_freq = ROPE_BASE ** (-jnp.arange(0, RET_QK_DIM, 2, dtype=jnp.float32) / RET_QK_DIM)
    ang = pos[:, None] * inv_freq[None, :]
    cos = jnp.cos(ang).astype(x.dtype)
    sin = jnp.sin(ang).astype(x.dtype)

    for l in range(DEPTH):
        h = rms_norm(x, in_norm_g[l])
        proj = h @ w_in[l]
        q, k, v, g, xr, gr, m_ret, m_rnn = jnp.split(proj, SPLIT_POINTS, axis=-1)

        q = rotary(q.reshape(b, s, RET_HEADS, RET_QK_DIM), cos, sin)
        k = rotary(k.reshape(b, s, RET_HEADS, RET_QK_DIM), cos, sin) * (RET_QK_DIM ** -0.5)
        v = v.reshape(b, s, RET_HEADS, RET_V_DIM)
        o = head_norm(retention(q, k, v), ret_gn_g[l])
        y_ret = (jax.nn.silu(g) * o) @ w_ret_o[l]

        xr = causal_depthwise_conv(xr, lru_conv_w[l], lru_conv_b[l])
        hr = rg_lru(xr, lru_w_a[l], lru_b_a[l], lru_w_i[l], lru_b_i[l], lru_a_param[l])
        y_rnn = (hr * jax.nn.gelu(gr)) @ w_rnn_o[l]

        mixed = jax.nn.sigmoid(m_ret) * y_ret + jax.nn.sigmoid(m_rnn) * y_rnn
        x = x + mixed @ w_out[l]

        h = rms_norm(x, ffn_norm_g[l])
        up = causal_depthwise_conv(h @ w_up[l], ffn_conv_w[l], ffn_conv_b[l])
        gate, val = jnp.split(up, 2, axis=-1)
        x = x + (jax.nn.silu(gate) * val) @ w_down[l]

    return rms_norm(x, final_norm_g)


_drawn_inputs = setup_inputs


def setup_inputs(seed=0):
    import zlib

    import numpy as np

    out = dict(_drawn_inputs(seed))
    spreads = {}
    factors = {'in_norm_g': 3.117,
     'ret_gn_g': 8.0,
     'lru_b_a': 54.286,
     'lru_b_i': 40.632,
     'ffn_norm_g': 11.371,
     'ffn_conv_b': 11.302,
     'final_norm_g': 8.7,
     'lru_conv_b': 3.65}
    for name, (base, spread) in spreads.items():
        noise = np.random.default_rng([zlib.crc32(name.encode()), seed]).standard_normal(out[name].shape)
        drawn = base * np.exp(spread * noise) if base else spread * noise
        out[name] = __import__('jax').numpy.asarray(drawn.astype(out[name].dtype))
    for name, factor in factors.items():
        out[name] = (out[name] * factor).astype(out[name].dtype)
    return out
```

```python
import concourse.bass as bass
from concourse import mybir

F32 = mybir.dt.float32
F32R = mybir.dt.float32r
ALU = mybir.AluOpType
ACT = mybir.ActivationFunctionType

P = 128
D = 1024
S = 1024
KT = D // P
HALF = 512
HEADS = 4
CHUNK = 128
NCH = S // CHUNK
QK = 256
VD = 512
BC = 256
BE = KT * BC
IN_W = 10240
FFN = 2816
GROUPS = FFN // BC
LRU_BLOCKS = 4
NORM_EPS = 1e-6
GN_EPS = 1e-5
HI, LO = 0, 1

PAIR_IN = 0
PAIR_RETO = IN_W // BC // 2
PAIR_GATE = PAIR_RETO + HEADS
PAIR_RNNO = PAIR_GATE + LRU_BLOCKS // 2
PAIR_OUT = PAIR_RNNO + 2
PAIR_FFN = PAIR_OUT + 2

QK_PAIRS, V_PAIRS, G_PAIRS, XR_PAIRS, GR_PAIRS, M_PAIRS = (0, 4), (4, 8), (8, 12), (12, 14), (14, 16), (16, 20)

PRM = {}
_at = 0
for _name, _n in (("in_g", 8), ("ffn_g", 8), ("gn_g", 16), ("conv_w", 32), ("conv_b", 8), ("b_a", 8), ("b_i", 8),
                  ("a_param", 8), ("fconv_w", 3 * 44), ("fconv_b", 44)):
    PRM[_name] = _at
    _at += _n
PRM_W = _at
CON = {"vscale": 0, "gam": 4, "gam2": 8, "chunk": 12}
CON_W = 16


def build(nc, a):
    ds = bass.ds

    top = [nc.sbuf_base + (-nc.sbuf_base) % 64]

    def at(name, shape, dt, offset):
        n = 4
        for x in shape[1:]:
            n *= x
        assert offset + n <= nc.sbuf_top, (name, offset + n - nc.sbuf_top)
        return nc.alloc_sbuf_tensor_at(name, shape, dt, offset=offset), offset + n

    def fixed(name, shape, dt=F32):
        t, top[0] = at(name, shape, dt, top[0])
        return t

    raw = fixed("raw", [P, 2, BE])
    ws = fixed("ws", [P, 2, 2, BE], F32R)
    prm = fixed("prm", [P, PRM_W])
    con = fixed("con", [P, CON_W])
    ident = fixed("ident", [P, P])
    mask = fixed("mask", [P, P])
    rms_ss = fixed("rms_ss", [P, 8])
    rms_rs = fixed("rms_rs", [P, 8])
    sp = fixed("sp", [P, 8, 8])
    hn = fixed("hn", [P, 2, 16])
    A = top[0] + (-top[0]) % 64
    B = A + 64 * 1024
    C = B + 64 * 1024

    actv, _ = at("actv", [P, 2, KT, S], F32R, A)
    mix, _ = at("mix", [P, 2, KT, S], F32R, B)
    x_in, _ = at("x_in", [P, KT, D], F32, B)
    xn_in, e = at("xn_in", [P, KT, D], F32, B + 32 * 1024)
    cos, e = at("cos", [P, S], F32, e)
    sin, e = at("sin", [P, S], F32, e)
    ost, e = at("ost", [P, 2, 2, S], F32, B)
    rope, e = at("rope", [P, 4, HALF], F32, e)
    stage, e = at("stage", [P, 2, 4 + S], F32, e)
    yacc, e = at("yacc", [P, KT, S], F32, A)
    yh, e = at("yh", [P, 2, 2, 4, HALF], F32R, e)
    stt, e = at("state", [P, 2, HALF], F32, e)
    sts, e = at("state_s", [P, 2, 2, 2, HALF], F32R, e)
    qkv, e = at("qkv", [P, 2, 1024], F32, e)
    gch, e = at("gch", [P, 2, 4, CHUNK], F32, e)
    qkvs, e = at("qkvs", [P, 2, 2, 1024], F32R, e)
    ktm, e = at("ktm", [P, 2, 2, QK], F32R, e)
    sc, e = at("sc", [P, 2, CHUNK], F32, e)
    scs, e = at("scs", [P, 2, 2, CHUNK], F32R, e)
    on, e = at("on", [P, 2, VD], F32, e)
    ych, e = at("ych", [P, 2, 4, CHUNK], F32, e)
    sgm, e = at("sgm", [P, 2, S], F32, e)
    xc, e = at("xc", [P, 2, 2, S], F32, B)
    gel, e = at("gel", [P, 2, 2, S], F32, e)
    xcs, e = at("xcs", [P, 2, 2, S], F32R, e)
    ri, e = at("ri", [P, 2, 2, S], F32, e)
    ea, e = at("ea", [P, 2, S], F32, e)
    th, e = at("th", [P, 2, S], F32, e)
    t2, e = at("t2", [P, 2, S], F32, e)
    rbr, e = at("rbr", [P, 2, S], F32, C)
    sgr, e = at("sgr", [P, 2, S], F32, e)
    mxf, e = at("mxf", [P, 2, S], F32, e)
    x1, e = at("x1", [P, KT, D], F32, A)
    xn1, _ = at("xn1", [P, KT, D], F32, e)
    hact, e = at("hact", [P, 2, 2, 2, S], F32R, e)
    fst, e = at("fst", [P, 2, 4 + S], F32, C)
    gt, e = at("gt", [P, 2, S], F32, e)
    vt, e = at("vt", [P, 2, S], F32, e)
    gbc, _ = at("gbc", [P, D], F32, C)

    ps = nc.alloc_psum_tensor("ps", [P, 8, HALF], F32)

    scr = nc.dram_tensor("scr", [IN_W, S], F32, kind="Internal").ap()
    scr_v = nc.dram_tensor("scr_v", [S, HEADS * VD], F32, kind="Internal").ap()
    scr_r = nc.dram_tensor("scr_r", [D, S], F32, kind="Internal").ap()
    ROW_Q, ROW_K, ROW_G, ROW_XC, ROW_GR, ROW_MR, ROW_MN = 0, 1024, 4096, 6144, 7168, 8192, 9216

    names = """alone const_in xt0 xt1 xt2 xt3 xt4 xt5 xt6 xt7 raw0 raw1 whi0 whi1 wsp0 wsp1 blk0 blk1 ini
        ss_done std_done rs_done xn_done tr_ps nhi_done nsp_done
        job qk_evac evac rope_st rope_rd stage_full stage_free ost0 ost1 sto0 sto1 conv_st ost_mid
        yz qr0 qr1 gr0 gr1 qhi qsp sc_ps sc_mk sc_hi sc_sp kt_ps km_done o_done u_ps t_done s_hi s_sp
        h_st h_ag h_var h_std h_rec h_rs h_nb on_done ont_ps y_done y_hi y_sp reto acc sg0 sg1 r_done r_out
        sp_st rate xg0 xg1 x_hi x_sp g_evac tanh_done om_done sq_done l_st yr_done yr_hi yr_sp
        m_ld0 m_ld1 m_st m_f m_hi m_sp x_re x1_done ss2 std2 rs2 xn2 tr2_ps n2_hi n2_sp
        gv_job gv_evac fst_full conv_done f_st g_conv g_silu a_mul a_hi a_sp d_ps d_add gb_in
        ss3 std3 rs3 out_t out_done""".split()
    sem = {n: nc.alloc_semaphore(n) for n in names}
    raw_in, w_hi, w_split, blk = ([sem[n + "0"], sem[n + "1"]] for n in ("raw", "whi", "wsp", "blk"))
    ost_ready, stored = [sem["ost0"], sem["ost1"]], [sem["sto0"], sem["sto1"]]


    def load_block(sp_, pair, slot, first, second):
        sp_.wait_ge(w_split[slot], pair + 1)
        for dst, src in (first, second):
            sp_.dma_start(dst, src).then_inc(raw_in[slot], 16)

    def load_columns(sp_, pair, slot, w, col):
        r = raw[:, slot, :].rearrange("p (k c) -> p k c", k=KT)
        v = w.rearrange("(k p) n -> p k n", p=P)
        load_block(sp_, pair, slot, *((r[:, 4 * q:4 * q + 4, :], v[:, 4 * q:4 * q + 4, ds(col, BC)]) for q in range(2)))

    def load_rows(sp_, pair, slot, w, row):
        r = raw[:, slot, :].rearrange("p (k c) -> p k c", k=2)
        load_block(sp_, pair, slot, *((r[:, k, :], w[ds(row + k * P, P), :]) for k in range(2)))

    def split_hi(act, pair, slot, n=BE):
        act.wait_ge(raw_in[slot], pair * 32 + 32)
        act.wait_ge(blk[slot], pair + 1)
        act.activation(ws[:, slot, HI, 0:n], raw[:, slot, 0:n], ACT.Copy).then_inc(w_hi[slot], 1)

    def split_lo(dve, pair, slot, n=BE):
        dve.wait_ge(w_hi[slot], pair + 1)
        dve.tensor_tensor(ws[:, slot, LO, 0:n], raw[:, slot, 0:n], ws[:, slot, HI, 0:n].bitcast(F32),
                          ALU.subtract).then_inc(w_split[slot], 1)

    def alone(eng):
        eng.sem_inc(sem["alone"], 1)

    def block_ready(pe, pair, slot):
        pe.wait_ge(w_split[slot], pair + 2)

    def split_after(f, eng, pair, slot):
        f(eng, pair, 1) if slot == 0 else f(eng, pair + 1, 0)

    def mm3(pe, out, w, x, first, last):
        pe.matmul(out, w(HI), x(HI), start=first, stop=False, skip_group_check=True)
        pe.matmul(out, w(HI), x(LO), start=False, stop=False, skip_group_check=True)
        return pe.matmul(out, w(LO), x(HI), start=False, stop=last, skip_group_check=True)

    def feature_jobs(pe, slot, src, bank0, before, done):
        w = ws[:, slot, :, :].rearrange("p a (k c) -> p a k c", k=KT)
        for job in range(4):
            half, m = job // 2, job % 2
            before(job)
            for k in range(KT):
                last = mm3(pe, ps[:, bank0 + job, :], lambda q: w[:, q, k, m * P:(m + 1) * P],
                           lambda q: src[:, q, k, half * HALF:(half + 1) * HALF], k == 0, k == KT - 1)
            last.then_inc(done if job < 3 else blk[slot], 1)

    def token_jobs(pe, slot, src, bank0, before, done):
        w = ws[:, slot, :, :].rearrange("p a (k c) -> p a k c", k=KT)
        for job in range(4):
            before(job)
            for t in (2 * job, 2 * job + 1):
                for k in range(KT):
                    last = mm3(pe, ps[:, bank0 + job, (t % 2) * BC:(t % 2 + 1) * BC],
                               lambda q: src[:, q, k, t * P:(t + 1) * P], lambda q: w[:, q, k, :],
                               k == 0, k == KT - 1)
            last.then_inc(done if job < 3 else blk[slot], 1)


    def norm_scale_act(act, src, waits, ss, ss_sem, std_sem, out):
        for t in range(KT):
            waits(t)
            i = act.activation(out(t), src[:, t, :], ACT.Square, accum_out=ss[:, t:t + 1])
            i.then_inc(ss_sem, 1)
        act.wait_ge(ss_sem, KT)
        act.activation(rms_rs[:, :], ss[:, :], ACT.Sqrt, scale=1.0 / D, bias=eps_norm[:, 0:1]).then_inc(std_sem, 1)

    def norm_apply_dve(dve, src, dst, std_sem, rs_sem, xn_sem):
        dve.wait_ge(std_sem, 1)
        dve.reciprocal(rms_rs[:, :], rms_rs[:, :]).then_inc(rs_sem, 1)
        dve.wait_ge(rs_sem, 1)
        for t in range(KT):
            dve.tensor_scalar(dst[:, t, :], src[:, t, :], rms_rs[:, t:t + 1], None, ALU.mult).then_inc(xn_sem, 1)

    def turn_pe(pe, src, xn_sem, ps_sem, sp_sem):
        for n in range(16):
            half, k = n // 8, n % 8
            if k == 0:
                pe.wait_ge(xn_sem, 4 * half + 4)
            if n >= 8:
                pe.wait_ge(sp_sem, n - 7)
            for t in range(4):
                last = pe.transpose(ps[:, n % 8, t * P:(t + 1) * P], src[:, 4 * half + t, k * P:(k + 1) * P], ident[:, :])
            last.then_inc(ps_sem, 1)

    def turn_hi(act, n, dst, g, ps_sem, hi_sem):
        half, k = n // 8, n % 8
        act.wait_ge(ps_sem, n + 1)
        act.activation(dst[:, HI, k, half * HALF:(half + 1) * HALF], ps[:, n % 8, :], ACT.Copy,
                       scale=prm[:, g + k:g + k + 1]).then_inc(hi_sem, 1)

    def turn_lo(dve, n, dst, g, hi_sem, sp_sem):
        half, k = n // 8, n % 8
        cols = slice(half * HALF, (half + 1) * HALF)
        dve.wait_ge(hi_sem, n + 1)
        dve.scalar_tensor_tensor(out=dst[:, LO, k, cols], in0=ps[:, n % 8, :], scalar=prm[:, g + k:g + k + 1],
                                 in1=dst[:, HI, k, cols].bitcast(F32), op0=ALU.mult, op1=ALU.subtract).then_inc(sp_sem, 1)

    eps_norm = sp[:, 6, 0:1]
    eps_gn = sp[:, 6, 1:2]
    rate = [sp[:, 3, :], sp[:, 4, :], sp[:, 5, :]]


    def reto_parts(h, j):
        if j == 0:
            return [(h - 1, 0, t) for t in (6, 7)]
        if j < 5:
            return [(h - 1, 1, 2 * (j - 1) + q) for q in range(2)]
        return [(h, 0, 2 * (j - 5) + q) for q in range(2)]

    def reto_number(hh, seg, t):
        return hh * 16 + (seg * 8 + t)

    def previous(h, j):
        return (h, j - 1) if j else (h - 1, 7)

    block = nc.Block()
    with block:

        @block.sync
        def _(sp_):
            x_t = a["x"].rearrange("b (t p) d -> p (b t) d", p=P)
            for t in range(KT):
                sp_.dma_start(x_in[:, t, :], x_t[:, t, :]).then_inc(sem[f"xt{t}"], 16)
            for dst, src in ((prm, "prm"), (con, "con"), (ident, "ident"), (mask, "mask"), (cos, "cos"), (sin, "sin")):
                sp_.dma_start(dst[:, :], a[src]).then_inc(sem["const_in"], 16)
            w_in = a["w_in"][0]
            with sp_.Fori(0, PAIR_RETO) as i:
                for slot in range(2):
                    load_columns(sp_, i, slot, w_in, i * (2 * BC) + slot * BC)

            def load_reto(h):
                rows = a["w_ret_o"][0][ds(h * VD, VD), :].rearrange("(k p) n -> p k n", p=P)
                for slot in range(2):
                    r = raw[:, slot, :].rearrange("p (k c) -> p k c", k=4)
                    load_block(sp_, PAIR_RETO + h, slot,
                               *((r[:, 2 * q:2 * q + 2, :], rows[:, 2 * q:2 * q + 2, slot * HALF:(slot + 1) * HALF])
                                 for q in range(2)))

            load_reto(0)
            for slot in range(2):
                sp_.wait_ge(stored[slot], 16 * PAIR_RETO)
            tokens = scr_v.rearrange("(c p) n -> p c n", p=P)

            def chunk_loads(h, j):
                r = h * 8 + j
                slot = j % 2
                if not (isinstance(r, int) and r < 2):
                    sp_.wait_ge(sem["qsp"], r - 1)
                cols = slice(j * CHUNK, (j + 1) * CHUNK)
                for n, row in ((0, ROW_Q), (1, ROW_K)):
                    sp_.dma_start(qkv[:, slot, n * QK:(n + 1) * QK].rearrange("p (m c) -> p m c", m=2),
                                  scr[ds(h * QK + row, QK), cols].rearrange("(m p) c -> p m c", p=P)
                                  ).then_inc(sem[f"qr{slot}"], 16)
                sp_.dma_start(qkv[:, slot, 2 * QK:], tokens[:, j, ds(h * VD, VD)]).then_inc(sem[f"qr{slot}"], 16)
                if not (isinstance(r, int) and r < 2):
                    sp_.wait_ge(sem["y_done"], r - 1)
                sp_.dma_start(gch[:, slot, :, :], scr[ds(h * VD + ROW_G, VD), cols].rearrange("(m p) c -> p m c", p=P)
                              ).then_inc(sem[f"gr{slot}"], 16)

            for j in range(NCH):
                chunk_loads(0, j)
            with sp_.Fori(1, HEADS) as h:
                for j in range(NCH):
                    chunk_loads(h, j)
                    if j == 1:
                        load_reto(h)

            w_a, w_i = a["lru_w_a"][0], a["lru_w_i"][0]

            def load_gates(pair, slot, n):
                r = raw[:, slot, 0:2 * HALF].rearrange("p (g k c) -> p g k c", g=2, k=2)
                load_block(sp_, pair, slot, *((r[:, q, :, :], w[ds(n, 1), :, :].rearrange("b (k p) c -> p (b k) c", p=P))
                                              for q, w in enumerate((w_a, w_i))))

            for n in range(2):
                load_gates(PAIR_GATE, n, n)
            for t in range(KT):
                if t >= 2:
                    sp_.wait_ge(sem["r_done"], t - 1)
                sp_.dma_start(sgm[:, t % 2, :], scr[ROW_MR + t * P:ROW_MR + (t + 1) * P, :]).then_inc(sem[f"sg{t % 2}"], 16)
            sp_.wait_ge(sem["r_out"], 16)
            w_ro = a["w_rnn_o"][0]
            for n in range(LRU_BLOCKS):
                u = n % 2
                sp_.wait_ge(sem["yr_sp"], n + 1)
                for dst, row in ((xc, ROW_XC), (gel, ROW_GR)):
                    sp_.dma_start(dst[:, u, :, :], scr[row + n * BC:row + (n + 1) * BC, :].rearrange(
                        "(m p) s -> p m s", p=P)).then_inc(sem[f"xg{u}"], 16)
                if n == 1:
                    load_gates(PAIR_GATE + 1, 0, 2)
                if n == 2:
                    load_gates(PAIR_GATE + 1, 1, 3)
                    load_columns(sp_, PAIR_RNNO, 0, w_ro, 0)
            load_columns(sp_, PAIR_RNNO, 1, w_ro, BC)
            sp_.wait_ge(sem["yr_sp"], LRU_BLOCKS + 2)
            w_o = a["w_out"][0]
            for n in range(4):
                for m in range(2):
                    t = 2 * n + m
                    sp_.wait_ge(sem["m_sp"], t + 1)
                    for dst, src, row in ((rbr, scr_r, 0), (sgr, scr, ROW_MN)):
                        sp_.dma_start(dst[:, m, :], src[row + t * P:row + (t + 1) * P, :]).then_inc(sem[f"m_ld{m}"], 16)
                if n < 2:
                    load_columns(sp_, PAIR_RNNO + 1, n, w_ro, (2 + n) * BC)
                else:
                    load_columns(sp_, PAIR_OUT, n - 2, w_o, (n - 2) * BC)
            sp_.wait_ge(blk[1], PAIR_OUT + 1)
            for t in range(0, KT, 4):
                sp_.dma_start(x1[:, t:t + 4, :], x_t[:, t:t + 4, :]).then_inc(sem["x_re"], 16)
            for n in range(2, 4):
                load_columns(sp_, PAIR_OUT + 1, n % 2, w_o, n * BC)
            w_up, w_dn = a["w_up"][0], a["w_down"][0]
            load_columns(sp_, PAIR_FFN, 0, w_up, 0)
            load_columns(sp_, PAIR_FFN, 1, w_up, FFN)
            with sp_.Fori(0, (GROUPS - 1) // 2) as i:
                for c in range(6):
                    pair, slot = i * 3 + (PAIR_FFN + 1 + c // 2), c % 2
                    g = i * 2 + (1 + c // 3)
                    if c % 3 == 0:
                        load_columns(sp_, pair, slot, w_up, g * BC)
                    elif c % 3 == 1:
                        load_columns(sp_, pair, slot, w_up, g * BC + FFN)
                    else:
                        load_rows(sp_, pair, slot, w_dn, g * BC - BC)
            load_rows(sp_, PAIR_FFN + 16, 0, w_dn, (GROUPS - 1) * BC)
            sp_.wait_ge(sem["a_sp"], GROUPS)
            sp_.dma_start(gbc[:, :], a["final_g"]).then_inc(sem["gb_in"], 16)
            out_t = a["out"].rearrange("b (t p) d -> p (b t) d", p=P)
            for t in range(KT):
                sp_.wait_ge(sem["out_t"], t + 1)
                sp_.dma_start(out_t[:, t, :], x1[:, t, :]).then_inc(sem["out_done"], 16)
            sp_.wait_ge(sem["out_done"], 16 * KT)

        @block.gpsimd
        def _(pool):
            pool.memset(sp[:, 6, 0:1], NORM_EPS).then_inc(sem["ini"], 1)
            pool.memset(sp[:, 6, 1:2], GN_EPS).then_inc(sem["ini"], 1)
            def store(pair, slot, dst):
                pool.wait_ge(ost_ready[slot], pair + 1)
                pool.dma_start(dst, ost[:, slot, :, :] if len(dst.shape) == 3 and dst.shape[1] == 2 else
                               ost[:, slot, :, :].rearrange("p m (t c) -> p (m t) c", c=BC)).then_inc(stored[slot], 16)

            def rows(lo, hi):
                with pool.Fori(lo, hi) as i:
                    for slot in range(2):
                        store(i, slot, scr[ds(i * (2 * BC) + slot * BC, BC), :].rearrange("(m p) s -> p m s", p=P))

            rows(*QK_PAIRS)
            tokens = scr_v.rearrange("(t p) n -> p t n", p=P)
            with pool.Fori(*V_PAIRS) as i:
                for slot in range(2):
                    store(i, slot, tokens[:, :, ds(i * (2 * BC) + (slot * BC - V_PAIRS[0] * 2 * BC), BC)])
            rows(G_PAIRS[0], M_PAIRS[1])
            for slot in range(2):
                pool.wait_ge(stored[slot], 16 * PAIR_RETO)
            pool.memset(yacc[:, :, :], 0.0).then_inc(sem["yz"], 1)

            def lo_parts(h, j):
                r, slot = h * 8 + j, j % 2
                pool.wait_ge(sem["qhi"], r + 1)
                pool.tensor_tensor(qkvs[:, slot, LO, :], qkv[:, slot, :], qkvs[:, slot, HI, :].bitcast(F32),
                                   ALU.subtract).then_inc(sem["qsp"], 1)

            for j in range(NCH):
                lo_parts(0, j)
            with pool.Fori(1, HEADS) as h:
                for j in range(NCH):
                    lo_parts(h, j)
            pool.wait_ge(sem["r_done"], KT)
            pool.dma_start(scr_r.rearrange("(k p) s -> p k s", p=P), yacc[:, :, :]).then_inc(sem["r_out"], 16)
            pool.wait_ge(sem["r_out"], 16)

        @block.tensor
        def _(pe):
            for slot in range(2):
                pe.sem_inc(blk[slot], 1)
            pe.wait_ge(sem["const_in"], 16 * 6)
            turn_pe(pe, xn_in, sem["xn_done"], sem["tr_ps"], sem["nsp_done"])
            pe.wait_ge(sem["nsp_done"], 16)

            with pe.Fori(*QK_PAIRS) as i:
                for slot in range(2):
                    block_ready(pe, i, slot)
                    feature_jobs(pe, slot, actv, 4 * slot,
                                 lambda job: pe.wait_ge(sem["qk_evac"], i * 4 + (2 * slot + job // 2 + 1)), sem["job"])
            pe.wait_ge(sem["qk_evac"], 4 * QK_PAIRS[1] + 4)
            for lo, hi, jobs in ((*V_PAIRS, token_jobs), (G_PAIRS[0], M_PAIRS[1], feature_jobs)):
                with pe.Fori(lo, hi) as i:
                    for slot in range(2):
                        block_ready(pe, i, slot)
                        jobs(pe, slot, actv, 4 * slot,
                             lambda job: pe.wait_ge(sem["evac"], i * 8 + (4 * slot + job + 1 - 8 * V_PAIRS[0])),
                             sem["job"])
            pe.wait_ge(sem["evac"], 8 * (M_PAIRS[1] - V_PAIRS[0]) + 8)

            def q_(slot, m):
                return lambda p: qkvs[:, slot, p, m * P:(m + 1) * P]

            def k_(slot, m):
                return lambda p: qkvs[:, slot, p, QK + m * P:QK + (m + 1) * P]

            def v_(slot):
                return lambda p: qkvs[:, slot, p, 2 * QK:]

            def scores(h, j):
                r, slot = h * 8 + j, j % 2
                pe.wait_ge(sem["qsp"], r + 1)
                if not (isinstance(r, int) and r < 2):
                    pe.wait_ge(sem["sc_mk"], r - 1)
                for m in range(2):
                    last = mm3(pe, ps[:, 0, slot * P:(slot + 1) * P], k_(slot, m), q_(slot, m), m == 0, m == 1)
                last.then_inc(sem["sc_ps"], 1)
                if not (isinstance(r, int) and r < 1):
                    pe.wait_ge(sem["km_done"], r)
                for p in range(2):
                    for m in range(2):
                        last = pe.transpose(ps[:, 1, p * QK + m * P:p * QK + (m + 1) * P],
                                            k_(slot, m)(p).bitcast(F32), ident[:, :])
                last.then_inc(sem["kt_ps"], 1)

            def outs(h, j):
                r, slot = h * 8 + j, j % 2
                pe.wait_ge(sem["sc_sp"], r + 1)
                if not (isinstance(r, int) and r < 1):
                    pe.wait_ge(sem["on_done"], r)
                last = mm3(pe, ps[:, 2, :], lambda p: scs[:, slot, p, :], v_(slot), True, j == 0)
                if j:
                    pe.wait_ge(sem["s_sp"], h * 7 + j)
                    for m in range(2):
                        last = mm3(pe, ps[:, 2, :], q_(slot, m), lambda p: sts[:, 1 - slot, p, m, :], False, m == 1)
                last.then_inc(sem["o_done"], 1)

            def update(h, j):
                r, slot = h * 8 + j, j % 2
                pe.wait_ge(sem["km_done"], r + 1)
                if not (isinstance(r, int) and r < 1):
                    pe.wait_ge(sem["t_done"], h * 7 + j)
                for m in range(2):
                    last = mm3(pe, ps[:, 3 + m, :], lambda p: ktm[:, slot, p, m * P:(m + 1) * P], v_(slot), True, True)
                last.then_inc(sem["u_ps"], 1)

            def reto(hh, seg, t):
                n = reto_number(hh, seg, t)
                slot = t // 4
                if t == 0:
                    pe.wait_ge(sem["y_sp"], hh * 8 + (4 * seg + 4))
                if t % 4 == 0 and seg == 0:
                    block_ready(pe, hh + PAIR_RETO, slot)
                if not (isinstance(n, int) and n < 2):
                    pe.wait_ge(sem["acc"], n - 1)
                w = ws[:, slot, :, :].rearrange("p a (k c) -> p a k c", k=4)
                for k in range(4):
                    last = mm3(pe, ps[:, 6 + t % 2, :], lambda p: w[:, p, k, (t % 4) * P:(t % 4 + 1) * P],
                               lambda p: yh[:, seg, p, k, :], k == 0, k == 3)
                last.then_inc(blk[slot] if seg == 1 and t % 4 == 3 else sem["reto"], 1)

            def turn_out(h, j):
                r, slot = h * 8 + j, j % 2
                pe.wait_ge(sem["on_done"], r + 1)
                if not (isinstance(r, int) and r < 1):
                    pe.wait_ge(sem["y_done"], r)
                for m in range(4):
                    last = pe.transpose(ps[:, 5, m * P:(m + 1) * P], on[:, slot, m * P:(m + 1) * P], ident[:, :])
                last.then_inc(sem["ont_ps"], 1)

            def step(h, j):
                first = isinstance(h, int)
                scores(h, j)
                if not (first and j == 0):
                    outs(*previous(h, j))
                if j < 7:
                    update(h, j)
                parts = [] if first and j < 5 else reto_parts(h, j)
                for n in parts[:1]:
                    reto(*n)
                if not (first and j == 0):
                    turn_out(*previous(h, j))
                for n in parts[1:]:
                    reto(*n)

            for j in range(NCH):
                step(0, j)
            with pe.Fori(1, HEADS) as h:
                for j in range(NCH):
                    step(h, j)
            outs(HEADS - 1, 7)
            reto(HEADS - 1, 0, 6)
            reto(HEADS - 1, 0, 7)
            turn_out(HEADS - 1, 7)
            for t in range(8):
                reto(HEADS - 1, 1, t)
            pe.wait_ge(sem["acc"], 16 * HEADS)

            with pe.Fori(0, LRU_BLOCKS // 2) as i:
                for u in range(2):
                    n = i * 2 + u
                    block_ready(pe, i + PAIR_GATE, u)
                    pe.wait_ge(sem["x_sp"], n + 1)
                    pe.wait_ge(sem["g_evac"], n + 1)
                    w = ws[:, u, :, 0:4 * BC].rearrange("p a (g k c) -> p a g k c", g=2, k=2)
                    for g in range(2):
                        for half in range(2):
                            for m in range(2):
                                for k in range(2):
                                    last = mm3(pe, ps[:, 4 * g + 2 * m + half, :],
                                               lambda p: w[:, p, g, k, m * P:(m + 1) * P],
                                               lambda p: xcs[:, p, k, half * HALF:(half + 1) * HALF], k == 0, k == 1)
                    last.then_inc(blk[u], 1)
            pe.wait_ge(sem["g_evac"], LRU_BLOCKS + 1)
            pe.wait_ge(sem["yr_sp"], LRU_BLOCKS + 2)

            with pe.Fori(0, 2) as i:
                for slot in range(2):
                    block_ready(pe, i + PAIR_RNNO, slot)
                    feature_jobs(pe, slot, actv, 4 * slot,
                                 lambda job: pe.wait_ge(sem["m_f"], i * 8 + (4 * slot + job + 1)), sem["job"])
            pe.wait_ge(sem["m_f"], 16 + 8)
            pe.wait_ge(sem["m_sp"], KT + 2)

            with pe.Fori(0, 2) as i:
                for slot in range(2):
                    block_ready(pe, i + PAIR_OUT, slot)
                    token_jobs(pe, slot, mix, 4 * slot,
                               lambda job: pe.wait_ge(sem["x1_done"], i * 8 + (4 * slot + job + 1)), sem["job"])
            pe.wait_ge(sem["x1_done"], 16 + 8)
            turn_pe(pe, xn1, sem["xn2"], sem["tr2_ps"], sem["n2_sp"])
            pe.wait_ge(sem["n2_sp"], 16)

            def up(g, pair, slot, val):
                block_ready(pe, pair, slot)

                def before(job):
                    if not (isinstance(g, int) and g < 2):
                        pe.wait_ge(sem["d_add"], g * 16 + (8 + 4 * val + job + 1 - 32))
                feature_jobs(pe, slot, mix, 4 * val, before, sem["gv_job"])

            def down(g, pair, slot, hslot):
                block_ready(pe, pair, slot)
                pe.wait_ge(sem["a_sp"], g + 1)
                w = ws[:, slot, :, :].rearrange("p a (k c) -> p a k c", k=2)
                for job in range(16):
                    t, half = job // 2, job % 2
                    if job < 8:
                        if isinstance(g, int) and g == GROUPS - 1:
                            pe.wait_ge(sem["d_add"], g * 16 - 7 + job)
                        else:
                            pe.wait_ge(sem["gv_evac"], g * 8 + (8 + job + 1))
                    else:
                        pe.wait_ge(sem["d_add"], g * 16 + (job - 7))
                    for k in range(2):
                        last = mm3(pe, ps[:, job % 8, :], lambda p: hact[:, hslot, p, k, t * P:(t + 1) * P],
                                   lambda p: w[:, p, k, half * HALF:(half + 1) * HALF], k == 0, k == 1)
                    last.then_inc(sem["d_ps"] if job < 15 else blk[slot], 1)

            def group(i, u):
                g = i * 2 + (1 + u) if not isinstance(i, int) else 2 * i + 1 + u
                c = 3 * u
                ps_ = [(i * 3 + (PAIR_FFN + 1 + (c + q) // 2), (c + q) % 2) for q in range(3)]
                up(g, *ps_[0], 0)
                up(g, *ps_[1], 1)
                down(g - 1, *ps_[2], u)

            up(0, PAIR_FFN, 0, 0)
            up(0, PAIR_FFN, 1, 1)
            group(0, 0)
            group(0, 1)
            with pe.Fori(1, (GROUPS - 1) // 2) as i:
                group(i, 0)
                group(i, 1)
            down(GROUPS - 1, PAIR_FFN + 16, 0, 0)

        @block.scalar
        def _(act):
            act.wait_ge(sem["ini"], 2)
            act.sem_inc(sem["evac"], 8)
            act.sem_inc(sem["g_evac"], 1)
            norm_scale_act(act, x_in, lambda t: act.wait_ge(sem[f"xt{t}"], 16), rms_ss, sem["ss_done"], sem["std_done"],
                           lambda t: xn_in[:, t, :])
            split_hi(act, 0, 0)
            act.wait_ge(sem["const_in"], 16 * 6)
            for n in range(16):
                turn_hi(act, n, actv, PRM["in_g"], sem["tr_ps"], sem["nhi_done"])

            def job_wait(pair, slot, job):
                if job < 3:
                    act.wait_ge(sem["job"], pair * 6 + (3 * slot + job + 1))
                else:
                    act.wait_ge(blk[slot], pair + 2)

            with act.Fori(*QK_PAIRS) as i:
                for slot in range(2):
                    split_after(split_hi, act, i, slot)
            with act.Fori(*V_PAIRS) as i:
                for slot in range(2):
                    split_after(split_hi, act, i, slot)
                    act.wait_ge(stored[slot], i * 16)
                    for job in range(4):
                        job_wait(i, slot, job)
                        o = ost[:, slot, job // 2, (job % 2) * HALF:(job % 2 + 1) * HALF]
                        alone(act)
                        act.activation(o, ps[:, 4 * slot + job, :], ACT.Copy,
                                       scale=con[:, ds(i - V_PAIRS[0], 1)]).then_inc(sem["evac"], 1)
                    act.wait_ge(sem["evac"], i * 8 + (4 * slot + 4 + 8 - 8 * V_PAIRS[0]))
                    act.sem_inc(ost_ready[slot], 1)

            def to_stage(lo, hi, func):
                with act.Fori(lo, hi) as i:
                    for slot in range(2):
                        split_after(split_hi, act, i, slot)
                        for job in range(4):
                            half, m = job // 2, job % 2
                            if half == 0:
                                act.wait_ge(sem["stage_free"], i * 4 + (2 * slot + m + 1 - 4 * G_PAIRS[0]))
                            job_wait(i, slot, job)
                            act.activation(stage[:, m, 4 + half * HALF:4 + (half + 1) * HALF], ps[:, 4 * slot + job, :],
                                           func).then_inc(sem["evac"], 1)

            def to_ost(lo, hi, func):
                with act.Fori(lo, hi) as i:
                    for slot in range(2):
                        split_after(split_hi, act, i, slot)
                        act.wait_ge(stored[slot], i * 16)
                        for job in range(4):
                            half, m = job // 2, job % 2
                            job_wait(i, slot, job)
                            act.activation(ost[:, slot, m, half * HALF:(half + 1) * HALF], ps[:, 4 * slot + job, :],
                                           func).then_inc(sem["evac"], 1)
                        act.wait_ge(sem["evac"], i * 8 + (4 * slot + 4 + 8 - 8 * V_PAIRS[0]))
                        act.sem_inc(ost_ready[slot], 1)

            to_stage(*G_PAIRS, ACT.Silu)
            to_stage(*XR_PAIRS, ACT.Copy)
            to_ost(*GR_PAIRS, ACT.Gelu_apprx_tanh)
            to_ost(*M_PAIRS, ACT.Sigmoid)
            for slot in range(2):
                act.wait_ge(stored[slot], 16 * PAIR_RETO)

            def hi_parts(h, j):
                r, slot = h * 8 + j, j % 2
                act.wait_ge(sem[f"qr{slot}"], h * (48 * 4) + 48 * (j // 2 + 1))
                if not (isinstance(r, int) and r < 2):
                    act.wait_ge(sem["o_done"], r - 1)
                act.activation(qkvs[:, slot, HI, :], qkv[:, slot, :], ACT.Copy).then_inc(sem["qhi"], 1)

            def normalise(h, j):
                r, slot = h * 8 + j, j % 2
                act.wait_ge(sem["h_var"], r + 1)
                act.activation(hn[:, slot, 9:10], hn[:, slot, 8:9], ACT.Sqrt).then_inc(sem["h_std"], 1)
                if not (isinstance(r, int) and r < 2):
                    act.wait_ge(sem["ont_ps"], r - 1)
                act.wait_ge(sem["h_nb"], r + 1)
                act.activation(on[:, slot, :], ps[:, 2, :], ACT.Identity, scale=hn[:, slot, 11:12],
                               bias=hn[:, slot, 12:13]).then_inc(sem["on_done"], 1)

            def y_hi(h, j):
                r, slot = h * 8 + j, j % 2
                seg = j // 4
                act.wait_ge(sem["y_done"], r + 1)
                if j % 4 == 0 and not isinstance(h, int):
                    act.wait_ge(sem["acc"], h * 16 + (8 * seg - 8))
                if j % 4 == 0 and isinstance(h, int) and h > 0:
                    act.wait_ge(sem["acc"], h * 16 + 8 * seg - 8)
                act.activation(yh[:, seg, HI, :, (j % 4) * CHUNK:(j % 4 + 1) * CHUNK], ych[:, slot, :, :],
                               ACT.Copy).then_inc(sem["y_hi"], 1)

            def step(h, j):
                r, slot = h * 8 + j, j % 2
                first = isinstance(h, int)
                if j == 0:
                    hi_parts(h, 0)
                act.wait_ge(sem["kt_ps"], r + 1)
                act.activation(ktm[:, slot, :, :], ps[:, 1, :].rearrange("p (a c) -> p a c", a=2),
                               ACT.Copy).then_inc(sem["km_done"], 1)
                act.wait_ge(sem["sc_mk"], r + 1)
                act.activation(scs[:, slot, HI, :], sc[:, slot, :], ACT.Copy).then_inc(sem["sc_hi"], 1)
                if not (first and j == 0):
                    normalise(*previous(h, j))
                if j < 7:
                    hi_parts(h, j + 1)
                if (j == 3 and not first) or j == 5:
                    split_hi(act, h + PAIR_RETO, 0 if j == 3 else 1)
                if j < 7:
                    act.wait_ge(sem["t_done"], h * 7 + (j + 1))
                    alone(act)
                    act.activation(sts[:, slot, HI, :, :], stt[:, :, :], ACT.Copy,
                                   scale=con[:, ds(h + CON["chunk"], 1)]).then_inc(sem["s_hi"], 1)
                if not (first and j == 0):
                    y_hi(*previous(h, j))

            for j in range(NCH):
                step(0, j)
            with act.Fori(1, HEADS) as h:
                for j in range(NCH):
                    step(h, j)
            normalise(HEADS - 1, 7)
            y_hi(HEADS - 1, 7)

            split_hi(act, PAIR_GATE, 0, 4 * BC)
            act.wait_ge(sem["sp_st"], 1)
            act.activation(sp[:, 1, :], sp[:, 0, :], ACT.Exp).then_inc(sem["sp_st"], 1)
            act.wait_ge(sem["rate"], 3)
            act.wait_ge(sem["r_out"], 16)
            with act.Fori(0, LRU_BLOCKS // 2) as i:
                for u in range(2):
                    n = i * 2 + u
                    act.wait_ge(sem[f"xg{u}"], i * 32 + 32)
                    act.wait_ge(sem["g_evac"], n + 1)
                    act.activation(xcs[:, HI, :, :], xc[:, u, :, :], ACT.Copy).then_inc(sem["x_hi"], 1)
                    if u == 0:
                        split_hi(act, i + PAIR_GATE, 1, 4 * BC)
                    act.wait_ge(blk[u], i + (PAIR_GATE + 2))
                    act.wait_ge(sem["yr_done"], n + 1)
                    for g, b in ((0, "b_a"), (1, "b_i")):
                        for m in range(2):
                            alone(act)
                            last = act.activation(ri[:, g, m, :], ps[:, 4 * g + 2 * m:4 * g + 2 * m + 2, :],
                                                  ACT.Sigmoid, bias=prm[:, ds(n * 2 + (PRM[b] + m), 1)])
                    last.then_inc(sem["g_evac"], 1)
                    act.wait_ge(sem["g_evac"], n + 2)
                    for m in range(2):
                        alone(act)
                        act.activation(ea[:, m, :], ri[:, 0, m, :], ACT.Exp, scale=sp[:, 3, ds(n * 2 + m, 1)])
                        act.activation(th[:, m, :], ri[:, 0, m, :], ACT.Tanh, scale=sp[:, 4, ds(n * 2 + m, 1)])
                        last = act.activation(t2[:, m, :], ri[:, 0, m, :], ACT.Tanh, scale=sp[:, 5, ds(n * 2 + m, 1)])
                    last.then_inc(sem["tanh_done"], 1)
                    act.wait_ge(sem["om_done"], n + 1)
                    act.activation(t2[:, :, :], t2[:, :, :], ACT.Sqrt).then_inc(sem["sq_done"], 1)
                    act.wait_ge(sem["yr_done"], n + 2)
                    alone(act)
                    act.activation(actv[:, HI, ds(n * 2, 2), :], gel[:, u, :, :], ACT.Copy).then_inc(sem["yr_hi"], 1)
                    if u == 1:
                        split_hi(act, i + (PAIR_GATE + 1), 0)

            with act.Fori(0, 2) as i:
                for slot in range(2):
                    split_after(split_hi, act, i + PAIR_RNNO, slot)
                    for m in range(2):
                        t = i * 4 + (2 * slot + m)
                        act.wait_ge(sem["m_f"], i * 8 + (4 * slot + 3 + m + 8))
                        alone(act)
                        act.activation(mix[:, HI, ds(t, 1), :], mxf[:, m:m + 1, :], ACT.Copy).then_inc(sem["m_hi"], 1)

            with act.Fori(0, 2) as i:
                for slot in range(2):
                    split_after(split_hi, act, i + PAIR_OUT, slot)
            norm_scale_act(act, x1, lambda t: act.wait_ge(sem["x1_done"], 16 + 8) if t == 0 else None, rms_ss,
                           sem["ss2"], sem["std2"], lambda t: xn1[:, t, :])
            for n in range(16):
                turn_hi(act, n, mix, PRM["ffn_g"], sem["tr2_ps"], sem["n2_hi"])

            def evac_up(g, pair, slot, val):
                for job in range(4):
                    half, m = job // 2, job % 2
                    if half == 0 and not (isinstance(g, int) and g == 0 and val == 0):
                        act.wait_ge(sem["conv_done"], g * 4 + (2 * val + m - 1))
                    if job < 3:
                        act.wait_ge(sem["gv_job"], g * 6 + (3 * val + job + 1))
                    else:
                        act.wait_ge(blk[slot], pair + 2)
                    act.activation(fst[:, m, 4 + half * HALF:4 + (half + 1) * HALF], ps[:, 4 * val + job, :],
                                   ACT.Copy).then_inc(sem["gv_evac"], 1)

            def silu_gate(g):
                for m in range(2):
                    act.wait_ge(sem["conv_done"], g * 4 + (m + 1))
                    act.activation(gt[:, m, :], gt[:, m, :], ACT.Silu).then_inc(sem["g_silu"], 1)

            def act_hi(g, hslot):
                act.wait_ge(sem["a_mul"], g + 1)
                if not (isinstance(g, int) and g < 2):
                    act.wait_ge(sem["d_add"], g * 16 - 16)
                act.activation(hact[:, hslot, HI, :, :], vt[:, :, :], ACT.Copy).then_inc(sem["a_hi"], 1)

            def group(i, u):
                g = i * 2 + (1 + u)
                c = 3 * u
                pp = [(i * 3 + (PAIR_FFN + 1 + (c + q) // 2), (c + q) % 2) for q in range(3)]
                split_after(split_hi, act, *pp[0])
                evac_up(g, *pp[0], 0)
                split_after(split_hi, act, *pp[1])
                silu_gate(g)
                evac_up(g, *pp[1], 1)
                split_after(split_hi, act, *pp[2])
                act_hi(g, 1 - u)

            split_hi(act, PAIR_FFN, 1)
            evac_up(0, PAIR_FFN, 0, 0)
            split_hi(act, PAIR_FFN + 1, 0)
            silu_gate(0)
            evac_up(0, PAIR_FFN, 1, 1)
            act_hi(0, 0)
            group(0, 0)
            group(0, 1)
            with act.Fori(1, (GROUPS - 1) // 2) as i:
                group(i, 0)
                group(i, 1)

            def row_complete(t):
                act.wait_ge(sem["d_add"], 16 * (GROUPS - 1) + 2 * t + 2)
                if t >= 2:
                    act.wait_ge(sem["ss3"], t - 1)

            norm_scale_act(act, x1, row_complete, rms_ss,
                           sem["ss3"], sem["std3"], lambda t: vt[:, t % 2, :])

        @block.vector
        def _(dve):
            for slot in range(2):
                dve.sem_inc(w_split[slot], 1)
            for name, n in (("qk_evac", 4), ("rope_rd", 1), ("stage_free", 2), ("yr_sp", 2), ("yr_done", 1), ("m_sp", 2), ("m_f", 8),
                            ("x1_done", 8)):
                dve.sem_inc(sem[name], n)
            norm_apply_dve(dve, x_in, xn_in, sem["std_done"], sem["rs_done"], sem["xn_done"])
            split_lo(dve, 0, 0)
            dve.wait_ge(sem["const_in"], 16 * 6)
            for n in range(16):
                turn_lo(dve, n, actv, PRM["in_g"], sem["nhi_done"], sem["nsp_done"])
            dve.wait_ge(sem["tr_ps"], 16)

            def job_wait(pair, slot, job):
                if job < 3:
                    dve.wait_ge(sem["job"], pair * 6 + (3 * slot + job + 1))
                else:
                    dve.wait_ge(blk[slot], pair + 2)

            def rotary(i):
                for slot in range(2):
                    split_after(split_lo, dve, i, slot)
                    if not isinstance(i, int):
                        dve.wait_ge(stored[slot], i * 16)
                    for half in range(2):
                        job_wait(i, slot, 2 * half + 1)
                        dve.wait_ge(sem["rope_rd"], i * 4 + (2 * slot + half + 1))
                        cols = slice(half * HALF, (half + 1) * HALF)
                        t1, tt2 = ps[:, 4 * slot + 2 * half, :], ps[:, 4 * slot + 2 * half + 1, :]
                        dve.tensor_tensor(rope[:, 0, :], t1, cos[:, cols], ALU.mult)
                        dve.tensor_tensor(rope[:, 1, :], tt2, sin[:, cols], ALU.mult)
                        dve.tensor_tensor(rope[:, 2, :], t1, sin[:, cols], ALU.mult).then_inc(sem["rope_st"], 1)
                        dve.tensor_tensor(rope[:, 3, :], tt2, cos[:, cols], ALU.mult).then_inc(sem["qk_evac"], 1)
                        dve.wait_ge(sem["rope_st"], i * 4 + (2 * slot + half + 1))
                        dve.wait_ge(sem["qk_evac"], i * 4 + (2 * slot + half + 1 + 4))
                        dve.tensor_tensor(ost[:, slot, 0, cols], rope[:, 0, :], rope[:, 1, :], ALU.subtract)
                        dve.tensor_tensor(ost[:, slot, 1, cols], rope[:, 2, :], rope[:, 3, :],
                                          ALU.add).then_inc(sem["rope_rd"], 1)
                    dve.wait_ge(sem["rope_rd"], i * 4 + (2 * slot + 3))
                    dve.sem_inc(ost_ready[slot], 1)

            rotary(0)
            with dve.Fori(1, QK_PAIRS[1]) as i:
                rotary(i)
            with dve.Fori(*V_PAIRS) as i:
                for slot in range(2):
                    split_after(split_lo, dve, i, slot)

            def stage_ready(i, slot, m):
                dve.wait_ge(sem["evac"], i * 8 + (4 * slot + 3 + m + 8 - 8 * V_PAIRS[0]))

            with dve.Fori(*G_PAIRS) as i:
                for slot in range(2):
                    split_after(split_lo, dve, i, slot)
                    dve.wait_ge(stored[slot], i * 16)
                    for m in range(2):
                        stage_ready(i, slot, m)
                        dve.tensor_scalar(ost[:, slot, m, :], stage[:, m, 4:],
                                          prm[:, ds(i * 4 + (2 * slot + m + PRM["gn_g"] - 4 * G_PAIRS[0]), 1)], None,
                                          ALU.mult).then_inc(sem["stage_free"], 1)
                    dve.wait_ge(sem["stage_free"], i * 4 + (2 * slot + 4 - 4 * G_PAIRS[0]))
                    dve.sem_inc(ost_ready[slot], 1)
            dve.memset(stage[:, :, 0:4], 0.0).then_inc(sem["conv_st"], 1)
            dve.wait_ge(sem["conv_st"], 1)

            def conv(dst, src, taps, w_col, b_col, st, st_count):
                for q in range(taps):
                    tap = taps - 1 - q
                    s_ = src[:, 4 - q:4 - q + S]
                    w = prm[:, ds(w_col + tap, 1)]
                    if q == 0:
                        ins = dve.tensor_scalar(dst, s_, w, prm[:, ds(b_col, 1)], ALU.mult, ALU.add)
                    else:
                        dve.wait_ge(st, st_count + q)
                        ins = dve.scalar_tensor_tensor(out=dst, in0=s_, scalar=w, in1=dst, op0=ALU.mult, op1=ALU.add)
                    if q < taps - 1:
                        ins.then_inc(st, 1)
                return ins

            with dve.Fori(*XR_PAIRS) as i:
                for slot in range(2):
                    split_after(split_lo, dve, i, slot)
                    dve.wait_ge(stored[slot], i * 16)
                    for m in range(2):
                        stage_ready(i, slot, m)
                        c = i * 4 + (2 * slot + m - 4 * XR_PAIRS[0])
                        conv(ost[:, slot, m, :], stage[:, m, :], 4, c * 4 + PRM["conv_w"], c + PRM["conv_b"],
                             sem["conv_st"], c * 3 + 1).then_inc(sem["stage_free"], 1)
                    dve.wait_ge(sem["stage_free"], i * 4 + (2 * slot + 4 - 4 * G_PAIRS[0]))
                    dve.sem_inc(ost_ready[slot], 1)
            with dve.Fori(GR_PAIRS[0], M_PAIRS[1]) as i:
                for slot in range(2):
                    split_after(split_lo, dve, i, slot)
            for slot in range(2):
                dve.wait_ge(stored[slot], 16 * PAIR_RETO)

            def stats(h, j):
                r, slot = h * 8 + j, j % 2
                dve.wait_ge(sem["o_done"], r + 1)
                dve.bn_stats(hn[:, slot, 0:6], ps[:, 2, :]).then_inc(sem["h_st"], 1)
                dve.wait_ge(sem["h_st"], r + 1)
                alone(dve)
                dve.bn_aggr(hn[:, slot, 6:8], hn[:, slot, 0:6]).then_inc(sem["h_ag"], 1)
                dve.wait_ge(sem["h_ag"], r + 1)
                dve.tensor_scalar(hn[:, slot, 8:9], hn[:, slot, 7:8], con[:, ds(h + CON["gam2"], 1)], eps_gn[:, 0:1],
                                  ALU.mult, ALU.add).then_inc(sem["h_var"], 1)

            def coefficients(h, j):
                r, slot = h * 8 + j, j % 2
                dve.wait_ge(sem["h_std"], r + 1)
                dve.reciprocal(hn[:, slot, 10:11], hn[:, slot, 9:10]).then_inc(sem["h_rec"], 1)
                dve.wait_ge(sem["h_rec"], r + 1)
                dve.tensor_scalar(hn[:, slot, 11:12], hn[:, slot, 10:11], con[:, ds(h + CON["gam"], 1)], None,
                                  ALU.mult).then_inc(sem["h_rs"], 1)
                dve.wait_ge(sem["h_rs"], r + 1)
                dve.scalar_tensor_tensor(out=hn[:, slot, 12:13], in0=hn[:, slot, 6:7], scalar=-1.0,
                                         in1=hn[:, slot, 11:12], op0=ALU.mult, op1=ALU.mult).then_inc(sem["h_nb"], 1)

            def gate(h, j):
                r, slot = h * 8 + j, j % 2
                if not (isinstance(r, int) and r < 2):
                    dve.wait_ge(sem["y_sp"], r - 1)
                dve.wait_ge(sem["ont_ps"], r + 1)
                dve.wait_ge(sem[f"gr{slot}"], h * 64 + 16 * (j // 2 + 1))
                dve.tensor_tensor(ych[:, slot, :, :], ps[:, 5, :].rearrange("p (m c) -> p m c", m=4), gch[:, slot, :, :],
                                  ALU.mult).then_inc(sem["y_done"], 1)

            def gate_lo(h, j):
                r, slot = h * 8 + j, j % 2
                seg, cols = j // 4, slice((j % 4) * CHUNK, (j % 4 + 1) * CHUNK)
                dve.wait_ge(sem["y_hi"], r + 1)
                dve.tensor_tensor(yh[:, seg, LO, :, cols], ych[:, slot, :, :], yh[:, seg, HI, :, cols].bitcast(F32),
                                  ALU.subtract).then_inc(sem["y_sp"], 1)

            def accumulate(hh, seg, t):
                if seg == 1 and t % 4 == 3:
                    dve.wait_ge(blk[t // 4], hh + (PAIR_RETO + 2))
                else:
                    dve.wait_ge(sem["reto"], hh * 14 + (8 * seg + t + 1 - (seg == 1 and t > 3)))
                cols = slice(seg * HALF, (seg + 1) * HALF)
                dve.tensor_tensor(yacc[:, t, cols], yacc[:, t, cols], ps[:, 6 + t % 2, :], ALU.add).then_inc(sem["acc"], 1)

            def step(h, j):
                r, slot = h * 8 + j, j % 2
                first = isinstance(h, int)
                before = not (first and j == 0)
                parts = [] if first and j < 5 else reto_parts(h, j)
                dve.wait_ge(sem["sc_ps"], r + 1)
                if not (first and j < 2):
                    dve.wait_ge(sem["sc_sp"], r - 1)
                dve.tensor_tensor(sc[:, slot, :], ps[:, 0, slot * P:(slot + 1) * P], mask[:, :],
                                  ALU.mult).then_inc(sem["sc_mk"], 1)
                dve.wait_ge(sem["sc_hi"], r + 1)
                dve.tensor_tensor(scs[:, slot, LO, :], sc[:, slot, :], scs[:, slot, HI, :].bitcast(F32),
                                  ALU.subtract).then_inc(sem["sc_sp"], 1)
                if before:
                    stats(*previous(h, j))
                    coefficients(*previous(h, j))
                if j < 7:
                    if not (first and j == 0):
                        dve.wait_ge(sem["s_sp"], h * 7 + j)
                    dve.wait_ge(sem["u_ps"], h * 7 + (j + 1))
                    if j:
                        for m in range(2):
                            last = dve.scalar_tensor_tensor(out=stt[:, m, :], in0=stt[:, m, :],
                                                            scalar=con[:, ds(h + CON["chunk"], 1)],
                                                            in1=ps[:, 3 + m, :], op0=ALU.mult, op1=ALU.add)
                    else:
                        last = dve.tensor_copy(stt[:, :, :], ps[:, 3:5, :])
                    last.then_inc(sem["t_done"], 1)
                for n in parts[:1]:
                    accumulate(*n)
                if (j == 3 and not first) or j == 5:
                    split_lo(dve, h + PAIR_RETO, 0 if j == 3 else 1)
                if j < 7:
                    dve.wait_ge(sem["s_hi"], h * 7 + (j + 1))
                    dve.scalar_tensor_tensor(out=sts[:, slot, LO, :, :], in0=stt[:, :, :],
                                             scalar=con[:, ds(h + CON["chunk"], 1)],
                                             in1=sts[:, slot, HI, :, :].bitcast(F32), op0=ALU.mult,
                                             op1=ALU.subtract).then_inc(sem["s_sp"], 1)
                if before:
                    gate(*previous(h, j))
                for n in parts[1:]:
                    accumulate(*n)
                if before:
                    gate_lo(*previous(h, j))

            dve.wait_ge(sem["yz"], 1)
            for j in range(NCH):
                step(0, j)
            with dve.Fori(1, HEADS) as h:
                for j in range(NCH):
                    step(h, j)
            stats(HEADS - 1, 7)
            coefficients(HEADS - 1, 7)
            accumulate(HEADS - 1, 0, 6)
            accumulate(HEADS - 1, 0, 7)
            gate(HEADS - 1, 7)
            gate_lo(HEADS - 1, 7)
            for t in range(8):
                accumulate(HEADS - 1, 1, t)
            dve.wait_ge(sem["acc"], 16 * HEADS)
            split_lo(dve, PAIR_GATE, 0, 4 * BC)
            for t in range(KT):
                dve.wait_ge(sem[f"sg{t % 2}"], 16 * (t // 2 + 1))
                dve.tensor_tensor(yacc[:, t, :], yacc[:, t, :], sgm[:, t % 2, :], ALU.mult).then_inc(sem["r_done"], 1)

            a_p = prm[:, PRM["a_param"]:PRM["a_param"] + 8]
            spn = [0]

            def small(ins):
                ins.then_inc(sem["l_st"], 1)
                spn[0] += 1
                dve.wait_ge(sem["l_st"], spn[0])

            small(dve.tensor_scalar(sp[:, 2, :], a_p, -1.0, None, ALU.mult))
            dve.tensor_tensor(sp[:, 0, :], a_p, sp[:, 2, :], ALU.min).then_inc(sem["sp_st"], 1)
            dve.wait_ge(sem["sp_st"], 2)
            small(dve.tensor_scalar(sp[:, 3, :], sp[:, 1, :], 2.0, None, ALU.add))
            small(dve.reciprocal(sp[:, 3, :], sp[:, 3, :]))
            small(dve.tensor_tensor(sp[:, 1, :], sp[:, 1, :], sp[:, 3, :], ALU.mult))
            small(dve.tensor_tensor(sp[:, 4, :], sp[:, 1, :], sp[:, 1, :], ALU.mult))
            small(dve.tensor_scalar(sp[:, 5, :], sp[:, 4, :], 2.0 / 17, 2.0 / 15, ALU.mult, ALU.add))
            for odd in (13, 11, 9, 7, 5, 3, 1):
                small(dve.tensor_tensor(sp[:, 5, :], sp[:, 5, :], sp[:, 4, :], ALU.mult))
                small(dve.tensor_scalar(sp[:, 5, :], sp[:, 5, :], 2.0 / odd, None, ALU.add))
            small(dve.tensor_tensor(sp[:, 5, :], sp[:, 5, :], sp[:, 1, :], ALU.mult))
            small(dve.tensor_scalar(sp[:, 2, :], sp[:, 2, :], 0.0, None, ALU.max))
            small(dve.tensor_tensor(sp[:, 7, :], sp[:, 2, :], sp[:, 5, :], ALU.add))
            for q, f in ((3, -8.0), (4, 4.0), (5, 8.0)):
                dve.tensor_scalar(sp[:, q, :], sp[:, 7, :], f, None, ALU.mult).then_inc(sem["rate"], 1)
            dve.wait_ge(sem["r_out"], 16)
            lsteps = spn[0]

            with dve.Fori(0, LRU_BLOCKS // 2) as i:
                for u in range(2):
                    n = i * 2 + u
                    dve.wait_ge(sem["x_hi"], n + 1)
                    dve.tensor_tensor(xcs[:, LO, :, :], xc[:, u, :, :], xcs[:, HI, :, :].bitcast(F32),
                                      ALU.subtract).then_inc(sem["x_sp"], 1)
                    if u == 0:
                        split_lo(dve, i + PAIR_GATE, 1, 4 * BC)
                    step_no = [0]

                    def chained(ins):
                        ins.then_inc(sem["l_st"], 1)
                        step_no[0] += 1
                        dve.wait_ge(sem["l_st"], n * 6 + (lsteps + step_no[0]))

                    dve.wait_ge(sem["tanh_done"], n + 1)
                    chained(dve.scalar_tensor_tensor(out=th[:, :, :], in0=ea[:, :, :], scalar=1.0, in1=th[:, :, :],
                                                     op0=ALU.add, op1=ALU.mult))
                    chained(dve.tensor_scalar(ea[:, :, :], th[:, :, :], -1.0, 1.0, ALU.mult, ALU.add))
                    chained(dve.tensor_tensor(th[:, :, :], ea[:, :, :], ea[:, :, :], ALU.mult))
                    dve.scalar_tensor_tensor(out=t2[:, :, :], in0=th[:, :, :], scalar=1.0, in1=t2[:, :, :],
                                             op0=ALU.add, op1=ALU.mult).then_inc(sem["om_done"], 1)
                    chained(dve.tensor_tensor(ri[:, 1, :, :], ri[:, 1, :, :], xc[:, u, :, :], ALU.mult))
                    dve.wait_ge(sem["sq_done"], n + 1)
                    chained(dve.tensor_tensor(ri[:, 1, :, :], ri[:, 1, :, :], t2[:, :, :], ALU.mult))
                    dve.tensor_tensor_scan(th[:, 0, :], ea[:, 0, :], ri[:, 1, 0, :], 0.0, ALU.mult, ALU.add)
                    chained(dve.tensor_tensor_scan(th[:, 1, :], ea[:, 1, :], ri[:, 1, 1, :], 0.0, ALU.mult, ALU.add))
                    dve.tensor_tensor(gel[:, u, :, :], gel[:, u, :, :], th[:, :, :], ALU.mult).then_inc(sem["yr_done"], 1)
                    dve.wait_ge(sem["yr_hi"], n + 1)
                    dve.tensor_tensor(actv[:, LO, ds(n * 2, 2), :], gel[:, u, :, :],
                                      actv[:, HI, ds(n * 2, 2), :].bitcast(F32), ALU.subtract).then_inc(sem["yr_sp"], 1)
                    if u == 1:
                        split_lo(dve, i + (PAIR_GATE + 1), 0)

            with dve.Fori(0, 2) as i:
                for slot in range(2):
                    split_after(split_lo, dve, i + PAIR_RNNO, slot)
                    for job in range(4):
                        half, m = job // 2, job % 2
                        t = i * 4 + (2 * slot + m)
                        cols = slice(half * HALF, (half + 1) * HALF)
                        if half == 0:
                            dve.wait_ge(sem[f"m_ld{m}"], i * 64 + (32 * slot + 32))
                        if job < 3:
                            dve.wait_ge(sem["job"], i * 6 + (6 * PAIR_RETO + 3 * slot + job + 1))
                        else:
                            dve.wait_ge(blk[slot], i + (PAIR_RNNO + 2))
                        dve.tensor_tensor(sgr[:, m, cols], sgr[:, m, cols], ps[:, 4 * slot + job, :],
                                          ALU.mult).then_inc(sem["m_st"], 1)
                        dve.wait_ge(sem["m_st"], i * 8 + (4 * slot + job + 1))
                        dve.tensor_tensor(mxf[:, m, cols], sgr[:, m, cols], rbr[:, m, cols],
                                          ALU.add).then_inc(sem["m_f"], 1)
                    for m in range(2):
                        t = i * 4 + (2 * slot + m)
                        dve.wait_ge(sem["m_hi"], t + 1)
                        dve.tensor_tensor(mix[:, LO, ds(t, 1), :], mxf[:, m:m + 1, :],
                                          mix[:, HI, ds(t, 1), :].bitcast(F32), ALU.subtract).then_inc(sem["m_sp"], 1)

            dve.wait_ge(sem["x_re"], 32)
            with dve.Fori(0, 2) as i:
                for slot in range(2):
                    split_after(split_lo, dve, i + PAIR_OUT, slot)
                    for job in range(4):
                        if job < 3:
                            dve.wait_ge(sem["job"], i * 6 + (6 * PAIR_RETO + 12 + 3 * slot + job + 1))
                        else:
                            dve.wait_ge(blk[slot], i + (PAIR_OUT + 2))
                        o = x1[:, 2 * job:2 * job + 2, ds(i * (2 * BC) + slot * BC, BC)]
                        dve.tensor_tensor(o, o, ps[:, 4 * slot + job, :].rearrange("p (t c) -> p t c", t=2),
                                          ALU.add).then_inc(sem["x1_done"], 1)
            norm_apply_dve(dve, x1, xn1, sem["std2"], sem["rs2"], sem["xn2"])
            for n in range(16):
                turn_lo(dve, n, mix, PRM["ffn_g"], sem["n2_hi"], sem["n2_sp"])
            dve.memset(fst[:, :, 0:4], 0.0).then_inc(sem["f_st"], 1)
            dve.wait_ge(sem["f_st"], 1)

            def conv_tile(g, val, m):
                dve.wait_ge(sem["gv_evac"], g * 8 + (4 * val + 3 + m))
                c = g * 2 + (22 * val + m)
                if val == 0 and not (isinstance(g, int) and g == 0):
                    dve.wait_ge(sem["a_mul"], g)
                if val == 1 and not (isinstance(g, int) and g == 0):
                    dve.wait_ge(sem["a_sp"], g)
                conv((vt if val else gt)[:, m, :], fst[:, m, :], 3, c * 3 + PRM["fconv_w"], c + PRM["fconv_b"],
                     sem["f_st"], g * 8 + (4 * val + 2 * m + 1)).then_inc(sem["conv_done"], 1)

            def multiply(g):
                dve.wait_ge(sem["g_silu"], g * 2 + 2)
                dve.wait_ge(sem["conv_done"], g * 4 + 4)
                dve.tensor_tensor(vt[:, :, :], vt[:, :, :], gt[:, :, :], ALU.mult).then_inc(sem["a_mul"], 1)

            def act_lo(g, hslot):
                dve.wait_ge(sem["a_hi"], g + 1)
                dve.tensor_tensor(hact[:, hslot, LO, :, :], vt[:, :, :], hact[:, hslot, HI, :, :].bitcast(F32),
                                  ALU.subtract).then_inc(sem["a_sp"], 1)

            def add_down(g, pair, slot, jobs):
                for job in jobs:
                    t, half = job // 2, job % 2
                    cols = slice(half * HALF, (half + 1) * HALF)
                    if job < 15:
                        dve.wait_ge(sem["d_ps"], g * 15 + (job + 1))
                    else:
                        dve.wait_ge(blk[slot], pair + 2)
                    dve.tensor_tensor(x1[:, t, cols], x1[:, t, cols], ps[:, job % 8, :], ALU.add).then_inc(sem["d_add"], 1)

            def group(i, u):
                g = i * 2 + (1 + u)
                c = 3 * u
                pp = [(i * 3 + (PAIR_FFN + 1 + (c + q) // 2), (c + q) % 2) for q in range(3)]
                split_after(split_lo, dve, *pp[0])
                conv_tile(g, 0, 0)
                conv_tile(g, 0, 1)
                split_after(split_lo, dve, *pp[1])
                conv_tile(g, 1, 0)
                add_down(g - 1, *pp[2], range(0, 4))
                conv_tile(g, 1, 1)
                add_down(g - 1, *pp[2], range(4, 8))
                multiply(g)
                split_after(split_lo, dve, *pp[2])
                add_down(g - 1, *pp[2], range(8, 12))
                act_lo(g, 1 - u)
                add_down(g - 1, *pp[2], range(12, 16))

            split_lo(dve, PAIR_FFN, 1)
            conv_tile(0, 0, 0)
            conv_tile(0, 0, 1)
            split_lo(dve, PAIR_FFN + 1, 0)
            conv_tile(0, 1, 0)
            conv_tile(0, 1, 1)
            multiply(0)
            act_lo(0, 0)
            group(0, 0)
            group(0, 1)
            with dve.Fori(1, (GROUPS - 1) // 2) as i:
                group(i, 0)
                group(i, 1)
            add_down(GROUPS - 1, PAIR_FFN + 16, 0, range(16))

            dve.wait_ge(sem["std3"], 1)
            dve.reciprocal(rms_rs[:, :], rms_rs[:, :]).then_inc(sem["rs3"], 1)
            dve.wait_ge(sem["rs3"], 1)
            dve.wait_ge(sem["gb_in"], 16)
            for t in range(KT):
                dve.scalar_tensor_tensor(out=x1[:, t, :], in0=x1[:, t, :], scalar=rms_rs[:, t:t + 1], in1=gbc[:, :],
                                         op0=ALU.mult, op1=ALU.mult).then_inc(sem["out_t"], 1)


def kernel(**inputs):
    import numpy as np
    import concourse.bacc as bacc
    from concourse.bass_utils import run_bass_kernel_spmd

    nc = bacc.Bacc("TRN2", target_bir_lowering=False, num_devices=1)
    get = {k: np.asarray(v) for k, v in inputs.items()}
    arrays, aps = {}, {}

    def dram_in(name, array):
        arrays[name] = np.ascontiguousarray(array)
        aps[name] = nc.dram_tensor(name, array.shape, F32, kind="ExternalInput").ap()

    for name in ("x", "w_in", "w_ret_o", "lru_w_a", "lru_w_i", "w_rnn_o", "w_out", "w_up", "w_down"):
        dram_in(name, get[name])

    def columns(v):
        return v.reshape(-1, P).T

    def tap_columns(w):
        taps, ch = w.shape
        return w.reshape(taps, ch // P, P).transpose(2, 1, 0).reshape(P, -1)

    dram_in("prm", np.concatenate(
        [columns(get["in_norm_g"][0]), columns(get["ffn_norm_g"][0]), columns(get["ret_gn_g"][0]),
         tap_columns(get["lru_conv_w"][0]), columns(get["lru_conv_b"][0]), columns(get["lru_b_a"][0]),
         columns(get["lru_b_i"][0]), columns(get["lru_a_param"][0]), tap_columns(get["ffn_conv_w"][0]),
         columns(get["ffn_conv_b"][0])], axis=1))
    dram_in("final_g", np.broadcast_to(get["final_norm_g"], (P, D)))

    log_g = np.log1p(-np.exp2(-5.0 - np.arange(HEADS, dtype=np.float64)))
    pos1 = np.arange(1, CHUNK + 1, dtype=np.float64)[:, None]
    con = np.concatenate([np.exp(-log_g * pos1) / 16.0, np.exp(log_g * pos1), np.exp(2 * log_g * pos1),
                          np.exp(log_g * CHUNK) + 0 * pos1], axis=1)
    dram_in("con", con.astype(np.float32))
    f = np.float32
    inv_freq = f(10000.0) ** (-np.arange(0, QK, 2, dtype=f) / f(QK))
    ang = (inv_freq.astype(f)[:, None] * np.arange(S, dtype=f)[None, :]).astype(f).astype(np.float64)
    dram_in("cos", np.cos(ang).astype(f))
    dram_in("sin", np.sin(ang).astype(f))
    dram_in("ident", np.eye(P, dtype=f))
    dram_in("mask", np.triu(np.ones((P, P), dtype=f)))
    aps["out"] = nc.dram_tensor("out", (1, S, D), F32, kind="ExternalOutput").ap()

    build(nc, aps)
    r = run_bass_kernel_spmd(nc, [arrays], core_ids=[0])
    return r.results[0]["out"]
```

```python
import concourse.bass as bass
from concourse import mybir

F32 = mybir.dt.float32
F32R = mybir.dt.float32r
ALU = mybir.AluOpType
ACT = mybir.ActivationFunctionType

P = 128
D = 1024
S = 1024
KT = D // P
HALF = 512
HEADS = 4
CHUNK = 128
NCH = S // CHUNK
QK = 256
VD = 512
BC = 256
BE = KT * BC
IN_W = 10240
FFN = 2816
GROUPS = FFN // BC
LRU_BLOCKS = 4
NORM_EPS = 1e-6
GN_EPS = 1e-5
HI, LO = 0, 1

XR_PAIRS, GR_PAIRS, V_PAIRS, QK_PAIRS, G_PAIRS, M_PAIRS = (0, 2), (2, 4), (4, 8), (8, 12), (12, 16), (16, 20)
PAIR_RNNO = IN_W // BC // 2
PAIR_RETO = PAIR_RNNO + 2
PAIR_OUT = PAIR_RETO + HEADS
PAIR_FFN = PAIR_OUT + 2
COL = {XR_PAIRS: 6144, GR_PAIRS: 6144, V_PAIRS: 0, QK_PAIRS: -4096, G_PAIRS: -2048, M_PAIRS: 0}

PRM = {}
_at = 0
for _name, _n in (("in_g", 8), ("ffn_g", 8), ("gn_g", 16), ("conv_w", 32), ("conv_b", 8), ("b_a", 8), ("b_i", 8),
                  ("a_param", 8), ("fconv_w", 3 * 44), ("fconv_b", 44)):
    PRM[_name] = _at
    _at += _n
PRM_W = _at
CON = {"vscale": 0, "gam": 4, "gam2": 8, "chunk": 12}
CON_W = 16


def build(nc, a):
    ds = bass.ds

    top = [nc.sbuf_base + (-nc.sbuf_base) % 64]

    def at(name, shape, dt, offset):
        n = 4
        for x in shape[1:]:
            n *= x
        assert offset + n <= nc.sbuf_top, (name, offset + n - nc.sbuf_top)
        return nc.alloc_sbuf_tensor_at(name, shape, dt, offset=offset), offset + n

    def fixed(name, shape, dt=F32):
        t, top[0] = at(name, shape, dt, top[0])
        return t

    raw = fixed("raw", [P, 2, BE])
    ws = fixed("ws", [P, 2, 2, BE], F32R)
    prm = fixed("prm", [P, PRM_W])
    con = fixed("con", [P, CON_W])
    ident = fixed("ident", [P, P])
    mask = fixed("mask", [P, P])
    rms_ss = fixed("rms_ss", [P, 8])
    rms_rs = fixed("rms_rs", [P, 8])
    sp = fixed("sp", [P, 8, 8])
    hn = fixed("hn", [P, 2, 16])
    A = top[0] + (-top[0]) % 64
    B = A + 64 * 1024
    C = B + 64 * 1024

    K1 = 1024
    x_in, _ = at("x_in", [P, KT, D], F32, B)
    xn_in, _ = at("xn_in", [P, KT, D], F32, B + 32 * K1)
    actv, _ = at("actv", [P, 2, KT, S], F32R, A)
    ost, e = at("ost", [P, 2, 2, S], F32, C)
    graw, e = at("graw", [P, 4 * BC], F32, e)
    gws, _ = at("gws", [P, 2, 4 * BC], F32R, e)
    stage, _ = at("stage", [P, 2, 4 + S], F32, e)
    stg, _ = at("stg", [P, 2, S], F32, e)
    rope, e = at("rope", [P, 4, HALF], F32, B)
    cos, e = at("cos", [P, S], F32, e)
    sin, e = at("sin", [P, S], F32, e)
    yr, _ = at("yr", [P, 2, KT, S], F32R, B)
    xc, e = at("xc", [P, 2, 2, S], F32, B)
    gel, e = at("gel", [P, 2, 2, S], F32, e)
    xcs, _ = at("xcs", [P, 2, 2, S], F32R, e)
    ea, e = at("ea", [P, 2, S], F32, e)
    th, e = at("th", [P, 2, S], F32, e)
    ri, e = at("ri", [P, 2, 2, S], F32, e)
    yacc, _ = at("yacc", [P, KT, S], F32, A)
    qkv, e = at("qkv", [P, 2, 1024], F32, A + 32 * K1)
    gch, e = at("gch", [P, 2, 4, CHUNK], F32, e)
    qkvs, e = at("qkvs", [P, 2, 2, 1024], F32R, e)
    ych, e = at("ych", [P, 2, 4, CHUNK], F32, e)
    stt, e = at("state", [P, 2, HALF], F32, B)
    sts, e = at("state_s", [P, 2, 2, 2, HALF], F32R, e)
    ktm, e = at("ktm", [P, 2, 2, QK], F32R, e)
    sc, e = at("sc", [P, 2, CHUNK], F32, e)
    scs, e = at("scs", [P, 2, 2, CHUNK], F32R, e)
    on, e = at("on", [P, 2, VD], F32, e)
    yh, _ = at("yh", [P, 2, 2, 4, HALF], F32R, B + 32 * K1)
    mix, _ = at("mix", [P, 2, KT, S], F32R, A + 32 * K1)
    msg, e = at("msg", [P, 4, HALF], F32, C)
    mrb, e = at("mrb", [P, 4, HALF], F32, e)
    mxf, e = at("mxf", [P, 2, HALF], F32, e)
    x1, _ = at("x1", [P, KT, D], F32, B + 32 * K1)
    xn1, _ = at("xn1", [P, KT, D], F32, A)
    hact, _ = at("hact", [P, 2, 2, 2, S], F32R, A)
    fst, e = at("fst", [P, 2, 4 + S], F32, C)
    gt, e = at("gt", [P, 2, S], F32, e)
    vt, e = at("vt", [P, 2, S], F32, e)
    gbc, _ = at("gbc", [P, D], F32, C)

    ps = nc.alloc_psum_tensor("ps", [P, 8, HALF], F32)

    scr = nc.dram_tensor("scr", [IN_W, S], F32, kind="Internal").ap()
    scr_v = nc.dram_tensor("scr_v", [S, HEADS * VD], F32, kind="Internal").ap()
    scr_y = nc.dram_tensor("scr_y", [D, S], F32, kind="Internal").ap()
    scr_r = nc.dram_tensor("scr_r", [D, S], F32, kind="Internal").ap()
    ROW_Q, ROW_K, ROW_G, ROW_XC, ROW_GR, ROW_MR, ROW_MN = 0, 1024, 4096, 6144, 7168, 8192, 9216

    names = """alone const_in cs_in xt0 xt1 xt2 xt3 xt4 xt5 xt6 xt7 raw0 raw1 whi0 whi1 wsp0 wsp1 blk0 blk1 ini
        ss_done std_done rs_done xn_done tr_ps nhi_done nsp_done
        job qk_evac v_evac evac rope_st rope_rd stage_full stage_free ost0 ost1 sto0 sto1 conv_st
        yz qr0 qr1 gr0 gr1 qhi qsp sc_ps sc_mk sc_hi sc_sp kt_ps km_done o_done u_ps t_done s_hi s_sp
        h_st h_ag h_var h_std h_rec h_rs h_nb on_done ont_ps y_done y_hi y_sp reto acc
        sp_st rate xg0 xg1 x_hi x_sp gw_in gw_hi gw_sp gr_ps gi_ps gr_evac gi_evac tanh_done om_done sq_done l_st
        yr_done ysto0 ysto1 ys_in0 ys_in1 ys_hi ys_sp sg_in sg_used
        mx_in0 mx_in1 mx_in2 mx_in3 mx_mul mx_f mx_hi mx_sp x_re x1_done ss2 std2 rs2 xn2 tr2_ps n2_hi n2_sp
        gv_job gv_evac conv_done f_st g_silu a_mul a_hi a_sp d_ps d_add gb_in
        ss3 std3 rs3 out_t out_done""".split()
    sem = {n: nc.alloc_semaphore(n) for n in names}
    raw_in, w_hi, w_split, blk = ([sem[n + "0"], sem[n + "1"]] for n in ("raw", "whi", "wsp", "blk"))
    ost_ready, stored = [sem["ost0"], sem["ost1"]], [sem["sto0"], sem["sto1"]]


    def load_block(sp_, pair, slot, first, second):
        sp_.wait_ge(w_split[slot], pair + 1)
        for dst, src in (first, second):
            sp_.dma_start(dst, src).then_inc(raw_in[slot], 16)

    def load_columns(sp_, pair, slot, w, col):
        r = raw[:, slot, :].rearrange("p (k c) -> p k c", k=KT)
        v = w.rearrange("(k p) n -> p k n", p=P)
        load_block(sp_, pair, slot, *((r[:, 4 * q:4 * q + 4, :], v[:, 4 * q:4 * q + 4, ds(col, BC)]) for q in range(2)))

    def load_rows(sp_, pair, slot, w, row):
        r = raw[:, slot, :].rearrange("p (k c) -> p k c", k=2)
        load_block(sp_, pair, slot, *((r[:, k, :], w[ds(row + k * P, P), :]) for k in range(2)))

    def split_hi(act, pair, slot, n=BE):
        act.wait_ge(raw_in[slot], pair * 32 + 32)
        act.wait_ge(blk[slot], pair + 1)
        act.activation(ws[:, slot, HI, 0:n], raw[:, slot, 0:n], ACT.Copy).then_inc(w_hi[slot], 1)

    def split_lo(dve, pair, slot, n=BE):
        dve.wait_ge(w_hi[slot], pair + 1)
        dve.tensor_tensor(ws[:, slot, LO, 0:n], raw[:, slot, 0:n], ws[:, slot, HI, 0:n].bitcast(F32),
                          ALU.subtract).then_inc(w_split[slot], 1)

    def alone(eng):
        eng.sem_inc(sem["alone"], 1)

    def block_ready(pe, pair, slot):
        pe.wait_ge(w_split[slot], pair + 2)

    def split_after(f, eng, pair, slot):
        f(eng, pair, 1) if slot == 0 else f(eng, pair + 1, 0)

    def mm3(pe, out, w, x, first, last):
        pe.matmul(out, w(HI), x(HI), start=first, stop=False, skip_group_check=True)
        pe.matmul(out, w(HI), x(LO), start=False, stop=False, skip_group_check=True)
        return pe.matmul(out, w(LO), x(HI), start=False, stop=last, skip_group_check=True)

    def feature_jobs(pe, slot, src, bank0, before, done):
        w = ws[:, slot, :, :].rearrange("p a (k c) -> p a k c", k=KT)
        for job in range(4):
            half, m = job // 2, job % 2
            before(job)
            for k in range(KT):
                last = mm3(pe, ps[:, bank0 + job, :], lambda q: w[:, q, k, m * P:(m + 1) * P],
                           lambda q: src[:, q, k, half * HALF:(half + 1) * HALF], k == 0, k == KT - 1)
            last.then_inc(done if job < 3 else blk[slot], 1)

    def token_jobs(pe, slot, src, bank0, before, done):
        w = ws[:, slot, :, :].rearrange("p a (k c) -> p a k c", k=KT)
        for job in range(4):
            before(job)
            for t in (2 * job, 2 * job + 1):
                for k in range(KT):
                    last = mm3(pe, ps[:, bank0 + job, (t % 2) * BC:(t % 2 + 1) * BC],
                               lambda q: src[:, q, k, t * P:(t + 1) * P], lambda q: w[:, q, k, :],
                               k == 0, k == KT - 1)
            last.then_inc(done if job < 3 else blk[slot], 1)


    def norm_scale_act(act, src, waits, ss_sem, std_sem, out, half):
        for t in range(4 * half, 4 * half + 4):
            waits(t)
            act.activation(out(t), src[:, t, :], ACT.Square, accum_out=rms_ss[:, t:t + 1]).then_inc(ss_sem, 1)
        act.wait_ge(ss_sem, 4 * half + 4)
        cols = slice(4 * half, 4 * half + 4)
        act.activation(rms_rs[:, cols], rms_ss[:, cols], ACT.Sqrt, scale=1.0 / D,
                       bias=eps_norm[:, 0:1]).then_inc(std_sem, 1)

    def norm_apply_dve(dve, src, dst, std_sem, rs_sem, xn_sem, half):
        cols = slice(4 * half, 4 * half + 4)
        dve.wait_ge(std_sem, half + 1)
        dve.reciprocal(rms_rs[:, cols], rms_rs[:, cols]).then_inc(rs_sem, 1)
        dve.wait_ge(rs_sem, half + 1)
        for t in range(4 * half, 4 * half + 4):
            dve.tensor_scalar(dst[:, t, :], src[:, t, :], rms_rs[:, t:t + 1], None, ALU.mult).then_inc(xn_sem, 1)

    def turn_bank(n):
        return n if n < 8 else 4 + n % 4

    def turn_pe(pe, jobs, src, xn_sem, ps_sem, sp_sem):
        for n in jobs:
            half, k = n // 8, n % 8
            if k == 0:
                pe.wait_ge(xn_sem, 4 * half + 4)
            if n >= 8:
                pe.wait_ge(sp_sem, n - 3)
            for t in range(4):
                last = pe.transpose(ps[:, turn_bank(n), t * P:(t + 1) * P],
                                    src[:, 4 * half + t, k * P:(k + 1) * P], ident[:, :])
            last.then_inc(ps_sem, 1)

    def first_block(pe, slot_jobs, src_turn, sems):
        def before(job):
            if job == 0:
                pe.wait_ge(sems[2], 8)
            if job == 2:
                turn_pe(pe, range(8, 16), src_turn, *sems)
                pe.wait_ge(sems[2], 16)
        slot_jobs(before)

    def turn_hi(act, n, dst, g, ps_sem, hi_sem):
        half, k = n // 8, n % 8
        act.wait_ge(ps_sem, n + 1)
        act.activation(dst[:, HI, k, half * HALF:(half + 1) * HALF], ps[:, turn_bank(n), :], ACT.Copy,
                       scale=prm[:, g + k:g + k + 1]).then_inc(hi_sem, 1)

    def turn_lo(dve, n, dst, g, hi_sem, sp_sem):
        half, k = n // 8, n % 8
        cols = slice(half * HALF, (half + 1) * HALF)
        dve.wait_ge(hi_sem, n + 1)
        dve.scalar_tensor_tensor(out=dst[:, LO, k, cols], in0=ps[:, turn_bank(n), :], scalar=prm[:, g + k:g + k + 1],
                                 in1=dst[:, HI, k, cols].bitcast(F32), op0=ALU.mult, op1=ALU.subtract).then_inc(sp_sem, 1)

    eps_norm = sp[:, 6, 0:1]
    eps_gn = sp[:, 6, 1:2]
    rate = [sp[:, 3, :], sp[:, 4, :], sp[:, 5, :]]


    def reto_parts(h, j):
        if j == 0:
            return [(h - 1, 0, t) for t in (6, 7)]
        if j < 5:
            return [(h - 1, 1, 2 * (j - 1) + q) for q in range(2)]
        return [(h, 0, 2 * (j - 5) + q) for q in range(2)]

    def reto_number(hh, seg, t):
        return hh * 16 + (seg * 8 + t)

    def stage_base(lo):
        return 0 if lo == XR_PAIRS[0] else 4 * (G_PAIRS[0] - XR_PAIRS[1])

    def previous(h, j):
        return (h, j - 1) if j else (h - 1, 7)

    block = nc.Block()
    with block:

        @block.sync
        def _(sp_):
            x_t = a["x"].rearrange("b (t p) d -> p (b t) d", p=P)
            for t in range(KT):
                sp_.dma_start(x_in[:, t, :], x_t[:, t, :]).then_inc(sem[f"xt{t}"], 16)
                if t == 3:
                    load_columns(sp_, 0, 0, a["w_in"][0], COL[XR_PAIRS])
                    for dst, src in ((prm, "prm"), (con, "con"), (ident, "ident"), (mask, "mask")):
                        sp_.dma_start(dst[:, :], a[src]).then_inc(sem["const_in"], 16)
            w_in = a["w_in"][0]

            def section(pairs, lo=None):
                with sp_.Fori(pairs[0] if lo is None else lo, pairs[1]) as i:
                    for slot in range(2):
                        load_columns(sp_, i, slot, w_in, i * (2 * BC) + (slot * BC + COL[pairs]))

            load_columns(sp_, 0, 1, w_in, COL[XR_PAIRS] + BC)
            section(XR_PAIRS, 1)
            section(GR_PAIRS)
            w_a, w_i = a["lru_w_a"][0], a["lru_w_i"][0]
            for n in range(LRU_BLOCKS):
                i, u = V_PAIRS[0] + n, n % 2
                load_columns(sp_, i, 0, w_in, i * 2 * BC)
                sp_.wait_ge(sem["gw_sp"], n + 1)
                for q, w in enumerate((w_a, w_i)):
                    sp_.dma_start(graw[:, q * 2 * BC:(q + 1) * 2 * BC].rearrange("p (k c) -> p k c", k=2),
                                  w[n, :, :].rearrange("(k p) c -> p k c", p=P)).then_inc(sem["gw_in"], 16)
                if n == 0:
                    for slot in range(2):
                        sp_.wait_ge(stored[slot], 16 * GR_PAIRS[1])
                if n >= 2:
                    sp_.wait_ge(sem[f"ysto{u}"], 16)
                for dst, row in ((xc, ROW_XC), (gel, ROW_GR)):
                    sp_.dma_start(dst[:, u, :, :], scr[row + n * BC:row + (n + 1) * BC, :].rearrange(
                        "(m p) s -> p m s", p=P)).then_inc(sem[f"xg{u}"], 16)
                load_columns(sp_, i, 1, w_in, i * 2 * BC + BC)
            for slot in range(2):
                load_columns(sp_, QK_PAIRS[0], slot, w_in, slot * BC)
            for u in range(2):
                sp_.wait_ge(sem[f"ysto{u}"], 32)
            for dst, src in ((cos, "cos"), (sin, "sin")):
                sp_.dma_start(dst[:, :], a[src]).then_inc(sem["cs_in"], 16)
            section(QK_PAIRS, QK_PAIRS[0] + 1)
            section(G_PAIRS)
            with sp_.Fori(*M_PAIRS) as i:
                for slot in range(2):
                    load_columns(sp_, i, slot, w_in, i * (2 * BC) + slot * BC)
                    t = i * 2 + (slot - 2 * M_PAIRS[0])
                    sp_.wait_ge(sem["ys_sp"], t + 1)
                    sp_.wait_ge(sem["stage_free"], 2 + 8 + 16)
                    sp_.dma_start(stg[:, slot, :], scr_y[ds(t * P, P), :]).then_inc(sem[f"ys_in{slot}"], 16)
            w_ro = a["w_rnn_o"][0]
            for n in range(4):
                load_columns(sp_, PAIR_RNNO + n // 2, n % 2, w_ro, n * BC)
                if n == 0:
                    sp_.wait_ge(sem["ys_sp"], KT + 2)
                    for slot in range(2):
                        sp_.wait_ge(stored[slot], 16 * PAIR_RNNO)
                else:
                    sp_.wait_ge(sem["sg_used"], 4 * n)
                sp_.dma_start(stg[:, :, :], scr[ROW_MN + n * BC:ROW_MN + (n + 1) * BC, :].rearrange(
                    "(m p) s -> p m s", p=P)).then_inc(sem["sg_in"], 16)

            def load_reto(h):
                rows = a["w_ret_o"][0][ds(h * VD, VD), :].rearrange("(k p) n -> p k n", p=P)
                for slot in range(2):
                    r = raw[:, slot, :].rearrange("p (k c) -> p k c", k=4)
                    load_block(sp_, PAIR_RETO + h, slot,
                               *((r[:, 2 * q:2 * q + 2, :], rows[:, 2 * q:2 * q + 2, slot * HALF:(slot + 1) * HALF])
                                 for q in range(2)))

            for slot in range(2):
                sp_.wait_ge(blk[slot], PAIR_RNNO + 1)
            tokens = scr_v.rearrange("(c p) n -> p c n", p=P)

            def chunk_loads(h, j):
                r = h * 8 + j
                slot = j % 2
                if not (isinstance(r, int) and r < 2):
                    sp_.wait_ge(sem["qsp"], r - 1)
                cols = slice(j * CHUNK, (j + 1) * CHUNK)
                for n, row in ((0, ROW_Q), (1, ROW_K)):
                    sp_.dma_start(qkv[:, slot, n * QK:(n + 1) * QK].rearrange("p (m c) -> p m c", m=2),
                                  scr[ds(h * QK + row, QK), cols].rearrange("(m p) c -> p m c", p=P)
                                  ).then_inc(sem[f"qr{slot}"], 16)
                sp_.dma_start(qkv[:, slot, 2 * QK:], tokens[:, j, ds(h * VD, VD)]).then_inc(sem[f"qr{slot}"], 16)
                if not (isinstance(r, int) and r < 2):
                    sp_.wait_ge(sem["y_done"], r - 1)
                sp_.dma_start(gch[:, slot, :, :], scr[ds(h * VD + ROW_G, VD), cols].rearrange("(m p) c -> p m c", p=P)
                              ).then_inc(sem[f"gr{slot}"], 16)

            chunk_loads(0, 0)
            load_reto(0)
            for j in range(1, NCH):
                chunk_loads(0, j)
            with sp_.Fori(1, HEADS) as h:
                for j in range(NCH):
                    chunk_loads(h, j)
                    if j == 1:
                        load_reto(h)

            for slot in range(2):
                sp_.wait_ge(stored[slot], 16 * PAIR_RETO)
            w_o = a["w_out"][0]
            for n in range(16):
                half, t = n // 8, n % 8
                cols = slice(half * HALF, (half + 1) * HALF)
                if n >= 4:
                    sp_.wait_ge(sem["mx_f"], n - 3)
                for dst, src, row in ((msg, scr, ROW_MR), (mrb, scr_r, 0)):
                    sp_.dma_start(dst[:, n % 4, :], src[row + t * P:row + (t + 1) * P, cols]
                                  ).then_inc(sem[f"mx_in{n % 4}"], 16)
                if n == 3:
                    load_columns(sp_, PAIR_OUT, 0, w_o, 0)
                if n == 5:
                    load_columns(sp_, PAIR_OUT, 1, w_o, BC)
            sp_.wait_ge(sem["acc"], 16 * HEADS)
            for t in range(0, KT, 4):
                sp_.dma_start(x1[:, t:t + 4, :], x_t[:, t:t + 4, :]).then_inc(sem["x_re"], 16)
            for n in range(2, 4):
                load_columns(sp_, PAIR_OUT + 1, n % 2, w_o, n * BC)
            w_up, w_dn = a["w_up"][0], a["w_down"][0]
            load_columns(sp_, PAIR_FFN, 0, w_up, 0)
            load_columns(sp_, PAIR_FFN, 1, w_up, FFN)
            with sp_.Fori(0, (GROUPS - 1) // 2) as i:
                for c in range(6):
                    pair, slot = i * 3 + (PAIR_FFN + 1 + c // 2), c % 2
                    g = i * 2 + (1 + c // 3)
                    if c % 3 == 0:
                        load_columns(sp_, pair, slot, w_up, g * BC)
                    elif c % 3 == 1:
                        load_columns(sp_, pair, slot, w_up, g * BC + FFN)
                    else:
                        load_rows(sp_, pair, slot, w_dn, g * BC - BC)
            load_rows(sp_, PAIR_FFN + 16, 0, w_dn, (GROUPS - 1) * BC)
            sp_.wait_ge(sem["a_sp"], GROUPS)
            sp_.dma_start(gbc[:, :], a["final_g"]).then_inc(sem["gb_in"], 16)
            out_t = a["out"].rearrange("b (t p) d -> p (b t) d", p=P)
            for t in range(KT):
                sp_.wait_ge(sem["out_t"], t + 1)
                sp_.dma_start(out_t[:, t, :], x1[:, t, :]).then_inc(sem["out_done"], 16)
            sp_.wait_ge(sem["out_done"], 16 * KT)

        @block.gpsimd
        def _(pool):
            pool.memset(sp[:, 6, 0:1], NORM_EPS).then_inc(sem["ini"], 1)
            pool.memset(sp[:, 6, 1:2], GN_EPS).then_inc(sem["ini"], 1)
            def store(pair, slot, dst):
                pool.wait_ge(ost_ready[slot], pair + 1)
                pool.dma_start(dst, ost[:, slot, :, :] if len(dst.shape) == 3 and dst.shape[1] == 2 else
                               ost[:, slot, :, :].rearrange("p m (t c) -> p (m t) c", c=BC)).then_inc(stored[slot], 16)

            def rows(pairs):
                with pool.Fori(*pairs) as i:
                    for slot in range(2):
                        store(i, slot, scr[ds(i * (2 * BC) + (slot * BC + COL[pairs]), BC), :].rearrange(
                            "(m p) s -> p m s", p=P))

            rows(XR_PAIRS)
            rows(GR_PAIRS)
            tokens = scr_v.rearrange("(t p) n -> p t n", p=P)
            for i in range(*V_PAIRS):
                n = i - V_PAIRS[0]
                for slot in range(2):
                    store(i, slot, tokens[:, :, n * 2 * BC + slot * BC:n * 2 * BC + (slot + 1) * BC])
                pool.wait_ge(sem["yr_done"], n + 1)
                pool.dma_start(scr_y[n * BC:(n + 1) * BC, :].rearrange("(m p) s -> p m s", p=P), gel[:, n % 2, :, :]
                               ).then_inc(sem[f"ysto{n % 2}"], 16)
            rows(QK_PAIRS)
            rows(G_PAIRS)
            rows(M_PAIRS)
            for slot in range(2):
                pool.wait_ge(blk[slot], PAIR_RNNO + 1)
            pool.memset(yacc[:, :, :], 0.0).then_inc(sem["yz"], 1)
            for n in range(4):
                store(PAIR_RNNO + n // 2, n % 2, scr_r[n * BC:(n + 1) * BC, :].rearrange("(m p) s -> p m s", p=P))

            def lo_parts(h, j):
                r, slot = h * 8 + j, j % 2
                pool.wait_ge(sem["qhi"], r + 1)
                pool.tensor_tensor(qkvs[:, slot, LO, :], qkv[:, slot, :], qkvs[:, slot, HI, :].bitcast(F32),
                                   ALU.subtract).then_inc(sem["qsp"], 1)

            for j in range(NCH):
                lo_parts(0, j)
            with pool.Fori(1, HEADS) as h:
                for j in range(NCH):
                    lo_parts(h, j)
            for n in range(16):
                half, t = n // 8, n % 8
                pool.wait_ge(sem[f"mx_in{n % 4}"], 32 * (n // 4 + 1))
                pool.wait_ge(sem["acc"], 16 * (HEADS - 1) + 8 * half + t + 1)
                pool.tensor_tensor(msg[:, n % 4, :], msg[:, n % 4, :], yacc[:, t, half * HALF:(half + 1) * HALF],
                                   ALU.mult).then_inc(sem["mx_mul"], 1)

        @block.tensor
        def _(pe):
            for slot in range(2):
                pe.sem_inc(blk[slot], 1)
            pe.wait_ge(sem["const_in"], 16 * 4)
            in_sems = (sem["xn_done"], sem["tr_ps"], sem["nsp_done"])
            turn_pe(pe, range(8), xn_in, *in_sems)

            def evac_wait(pairs, i, slot):
                base = 0 if pairs in (XR_PAIRS, GR_PAIRS) else 8 * (G_PAIRS[0] - GR_PAIRS[1])
                return lambda job: pe.wait_ge(sem["evac"], i * 8 + (4 * slot + job + 1 - base))

            def section(pairs, lo=None):
                with pe.Fori(pairs[0] if lo is None else lo, pairs[1]) as i:
                    for slot in range(2):
                        block_ready(pe, i, slot)
                        feature_jobs(pe, slot, actv, 4 * slot, evac_wait(pairs, i, slot), sem["job"])

            block_ready(pe, 0, 0)
            first_block(pe, lambda before: feature_jobs(pe, 0, actv, 0, before, sem["job"]), xn_in, in_sems)
            block_ready(pe, 0, 1)
            feature_jobs(pe, 1, actv, 4, lambda job: None, sem["job"])
            section(XR_PAIRS, 1)
            section(GR_PAIRS)
            pe.wait_ge(sem["evac"], 8 * GR_PAIRS[1] + 8)

            gw = gws[:, :, :].rearrange("p a (g k c) -> p a g k c", g=2, k=2)
            with pe.Fori(*V_PAIRS) as i:
                for slot in range(2):
                    block_ready(pe, i, slot)
                    token_jobs(pe, slot, actv, 0,
                               lambda job: pe.wait_ge(sem["v_evac"], i * 8 + (4 * slot + job + 1 - 8 * V_PAIRS[0])),
                               sem["job"])
                    if slot == 1:
                        continue
                    n4 = i * 4 - 4 * V_PAIRS[0]
                    pe.wait_ge(sem["gw_sp"], i + (2 - V_PAIRS[0]))
                    pe.wait_ge(sem["x_sp"], i + (1 - V_PAIRS[0]))
                    for g in range(2):
                        for q in range(4):
                            m, half = q // 2, q % 2
                            pe.wait_ge(sem["gr_evac" if g else "gi_evac"], n4 + (q + 1))
                            for k in range(2):
                                last = mm3(pe, ps[:, 4 + q, :], lambda p: gw[:, p, g, k, m * P:(m + 1) * P],
                                           lambda p: xcs[:, p, k, half * HALF:(half + 1) * HALF], k == 0, k == 1)
                            last.then_inc(sem["gi_ps" if g else "gr_ps"], 1)
            pe.wait_ge(sem["v_evac"], 8 * LRU_BLOCKS + 4)
            pe.wait_ge(sem["gi_evac"], 4 * LRU_BLOCKS + 4)
            with pe.Fori(*QK_PAIRS) as i:
                for slot in range(2):
                    block_ready(pe, i, slot)
                    feature_jobs(pe, slot, actv, 4 * slot,
                                 lambda job: pe.wait_ge(sem["qk_evac"],
                                                        i * 4 + (2 * slot + job // 2 + 1 - 4 * QK_PAIRS[0])), sem["job"])
            pe.wait_ge(sem["qk_evac"], 4 * 4 + 4)
            section(G_PAIRS)
            section(M_PAIRS)

            pe.wait_ge(sem["ys_sp"], KT + 2)
            pe.wait_ge(sem["evac"], 8 * 12 + 8)
            for n in range(4):
                slot = n % 2
                block_ready(pe, PAIR_RNNO + n // 2, slot)
                feature_jobs(pe, slot, yr, 4 * slot,
                             lambda job: pe.wait_ge(sem["sg_used"], 4 * n - 7 + job) if n >= 2 else None, sem["job"])
            pe.wait_ge(sem["sg_used"], 16)

            def q_(slot, m):
                return lambda p: qkvs[:, slot, p, m * P:(m + 1) * P]

            def k_(slot, m):
                return lambda p: qkvs[:, slot, p, QK + m * P:QK + (m + 1) * P]

            def v_(slot):
                return lambda p: qkvs[:, slot, p, 2 * QK:]

            def scores(h, j):
                r, slot = h * 8 + j, j % 2
                pe.wait_ge(sem["qsp"], r + 1)
                if not (isinstance(r, int) and r < 2):
                    pe.wait_ge(sem["sc_mk"], r - 1)
                for m in range(2):
                    last = mm3(pe, ps[:, 0, slot * P:(slot + 1) * P], k_(slot, m), q_(slot, m), m == 0, m == 1)
                last.then_inc(sem["sc_ps"], 1)
                if not (isinstance(r, int) and r < 1):
                    pe.wait_ge(sem["km_done"], r)
                for p in range(2):
                    for m in range(2):
                        last = pe.transpose(ps[:, 1, p * QK + m * P:p * QK + (m + 1) * P],
                                            k_(slot, m)(p).bitcast(F32), ident[:, :])
                last.then_inc(sem["kt_ps"], 1)

            def outs(h, j):
                r, slot = h * 8 + j, j % 2
                pe.wait_ge(sem["sc_sp"], r + 1)
                if not (isinstance(r, int) and r < 1):
                    pe.wait_ge(sem["on_done"], r)
                last = mm3(pe, ps[:, 2, :], lambda p: scs[:, slot, p, :], v_(slot), True, j == 0)
                if j:
                    pe.wait_ge(sem["s_sp"], h * 7 + j)
                    for m in range(2):
                        last = mm3(pe, ps[:, 2, :], q_(slot, m), lambda p: sts[:, 1 - slot, p, m, :], False, m == 1)
                last.then_inc(sem["o_done"], 1)

            def update(h, j):
                r, slot = h * 8 + j, j % 2
                pe.wait_ge(sem["km_done"], r + 1)
                if not (isinstance(r, int) and r < 1):
                    pe.wait_ge(sem["t_done"], h * 7 + j)
                for m in range(2):
                    last = mm3(pe, ps[:, 3 + m, :], lambda p: ktm[:, slot, p, m * P:(m + 1) * P], v_(slot), True, True)
                last.then_inc(sem["u_ps"], 1)

            def reto(hh, seg, t):
                n = reto_number(hh, seg, t)
                slot = t // 4
                if t == 0:
                    pe.wait_ge(sem["y_sp"], hh * 8 + (4 * seg + 4))
                if t % 4 == 0 and seg == 0:
                    block_ready(pe, hh + PAIR_RETO, slot)
                if not (isinstance(n, int) and n < 2):
                    pe.wait_ge(sem["acc"], n - 1)
                w = ws[:, slot, :, :].rearrange("p a (k c) -> p a k c", k=4)
                for k in range(4):
                    last = mm3(pe, ps[:, 6 + t % 2, :], lambda p: w[:, p, k, (t % 4) * P:(t % 4 + 1) * P],
                               lambda p: yh[:, seg, p, k, :], k == 0, k == 3)
                last.then_inc(blk[slot] if seg == 1 and t % 4 == 3 else sem["reto"], 1)

            def turn_out(h, j):
                r, slot = h * 8 + j, j % 2
                pe.wait_ge(sem["on_done"], r + 1)
                if not (isinstance(r, int) and r < 1):
                    pe.wait_ge(sem["y_done"], r)
                for m in range(4):
                    last = pe.transpose(ps[:, 5, m * P:(m + 1) * P], on[:, slot, m * P:(m + 1) * P], ident[:, :])
                last.then_inc(sem["ont_ps"], 1)

            def step(h, j):
                first = isinstance(h, int)
                scores(h, j)
                if not (first and j == 0):
                    outs(*previous(h, j))
                if j < 7:
                    update(h, j)
                parts = [] if first and j < 5 else reto_parts(h, j)
                for n in parts[:1]:
                    reto(*n)
                if not (first and j == 0):
                    turn_out(*previous(h, j))
                for n in parts[1:]:
                    reto(*n)

            for j in range(NCH):
                step(0, j)
            with pe.Fori(1, HEADS) as h:
                for j in range(NCH):
                    step(h, j)
            outs(HEADS - 1, 7)
            reto(HEADS - 1, 0, 6)
            reto(HEADS - 1, 0, 7)
            turn_out(HEADS - 1, 7)
            for t in range(8):
                reto(HEADS - 1, 1, t)
            pe.wait_ge(sem["acc"], 16 * HEADS)

            for n in range(4):
                slot = n % 2
                block_ready(pe, PAIR_OUT + n // 2, slot)

                def before(job):
                    if n == 0 and job in (0, 2):
                        pe.wait_ge(sem["mx_sp"], 8 + 4 * job)
                    if n >= 2:
                        pe.wait_ge(sem["x1_done"], 4 * n - 7 + job)
                token_jobs(pe, slot, mix, 4 * slot, before, sem["job"])
            pe.wait_ge(sem["x1_done"], 16)
            ffn_sems = (sem["xn2"], sem["tr2_ps"], sem["n2_sp"])
            turn_pe(pe, range(8), xn1, *ffn_sems)

            def up(g, pair, slot, val):
                block_ready(pe, pair, slot)

                def before(job):
                    if not (isinstance(g, int) and g < 2):
                        pe.wait_ge(sem["d_add"], g * 16 + (8 + 4 * val + job + 1 - 32))
                feature_jobs(pe, slot, mix, 4 * val, before, sem["gv_job"])

            def down(g, pair, slot, hslot):
                block_ready(pe, pair, slot)
                pe.wait_ge(sem["a_sp"], g + 1)
                w = ws[:, slot, :, :].rearrange("p a (k c) -> p a k c", k=2)
                for job in range(16):
                    t, half = job // 2, job % 2
                    if job < 8:
                        if isinstance(g, int) and g == GROUPS - 1:
                            pe.wait_ge(sem["d_add"], g * 16 - 7 + job)
                        else:
                            pe.wait_ge(sem["gv_evac"], g * 8 + (8 + job + 1))
                    else:
                        pe.wait_ge(sem["d_add"], g * 16 + (job - 7))
                    for k in range(2):
                        last = mm3(pe, ps[:, job % 8, :], lambda p: hact[:, hslot, p, k, t * P:(t + 1) * P],
                                   lambda p: w[:, p, k, half * HALF:(half + 1) * HALF], k == 0, k == 1)
                    last.then_inc(sem["d_ps"] if job < 15 else blk[slot], 1)

            def group(i, u):
                g = i * 2 + (1 + u) if not isinstance(i, int) else 2 * i + 1 + u
                c = 3 * u
                ps_ = [(i * 3 + (PAIR_FFN + 1 + (c + q) // 2), (c + q) % 2) for q in range(3)]
                up(g, *ps_[0], 0)
                up(g, *ps_[1], 1)
                down(g - 1, *ps_[2], u)

            block_ready(pe, PAIR_FFN, 0)
            first_block(pe, lambda before: feature_jobs(pe, 0, mix, 0, before, sem["gv_job"]), xn1, ffn_sems)
            up(0, PAIR_FFN, 1, 1)
            group(0, 0)
            group(0, 1)
            with pe.Fori(1, (GROUPS - 1) // 2) as i:
                group(i, 0)
                group(i, 1)
            down(GROUPS - 1, PAIR_FFN + 16, 0, 0)

        @block.scalar
        def _(act):
            act.wait_ge(sem["ini"], 2)
            act.sem_inc(sem["evac"], 8)
            act.sem_inc(sem["v_evac"], 4)
            act.sem_inc(sem["gi_evac"], 4)
            norm_scale_act(act, x_in, lambda t: act.wait_ge(sem[f"xt{t}"], 16), sem["ss_done"], sem["std_done"],
                           lambda t: xn_in[:, t, :], 0)
            split_hi(act, 0, 0)
            act.wait_ge(sem["const_in"], 16 * 4)
            for n in range(8):
                turn_hi(act, n, actv, PRM["in_g"], sem["tr_ps"], sem["nhi_done"])
            norm_scale_act(act, x_in, lambda t: act.wait_ge(sem[f"xt{t}"], 16), sem["ss_done"], sem["std_done"],
                           lambda t: xn_in[:, t, :], 1)
            for n in range(8, 16):
                turn_hi(act, n, actv, PRM["in_g"], sem["tr_ps"], sem["nhi_done"])

            def job_wait(pair, slot, job):
                if job < 3:
                    act.wait_ge(sem["job"], pair * 6 + (3 * slot + job + 1))
                else:
                    act.wait_ge(blk[slot], pair + 2)

            def to_stage(lo, hi, func):
                with act.Fori(lo, hi) as i:
                    for slot in range(2):
                        split_after(split_hi, act, i, slot)
                        for job in range(4):
                            half, m = job // 2, job % 2
                            if half == 0:
                                act.wait_ge(sem["stage_free"], i * 4 + (2 * slot + m + 1 - stage_base(lo)))
                            job_wait(i, slot, job)
                            act.activation(stage[:, m, 4 + half * HALF:4 + (half + 1) * HALF], ps[:, 4 * slot + job, :],
                                           func).then_inc(sem["evac"], 1)

            def evac_ost(i, slot, func, base):
                act.wait_ge(stored[slot], i * 16)
                for job in range(4):
                    half, m = job // 2, job % 2
                    job_wait(i, slot, job)
                    act.activation(ost[:, slot, m, half * HALF:(half + 1) * HALF], ps[:, 4 * slot + job, :],
                                   func).then_inc(sem["evac"], 1)
                act.wait_ge(sem["evac"], i * 8 + (4 * slot + 4 + 8 + base))
                act.sem_inc(ost_ready[slot], 1)

            def to_ost(lo, hi, func):
                with act.Fori(lo, hi) as i:
                    for slot in range(2):
                        split_after(split_hi, act, i, slot)
                        evac_ost(i, slot, func, 0)

            to_stage(*XR_PAIRS, ACT.Copy)
            to_ost(*GR_PAIRS, ACT.Gelu_apprx_tanh)

            act.wait_ge(sem["sp_st"], 1)
            act.activation(sp[:, 1, :], sp[:, 0, :], ACT.Exp).then_inc(sem["sp_st"], 1)

            def evac_v(i, slot, jobs):
                n = i - V_PAIRS[0]
                for job in jobs:
                    job_wait(i, slot, job)
                    act.activation(ost[:, slot, job // 2, (job % 2) * HALF:(job % 2 + 1) * HALF], ps[:, job, :], ACT.Copy,
                                   scale=con[:, n:n + 1]).then_inc(sem["v_evac"], 1)
                if 3 in jobs:
                    act.wait_ge(sem["v_evac"], 8 * n + 4 * slot + 4 + 4)
                    act.sem_inc(ost_ready[slot], 1)

            for n in range(LRU_BLOCKS):
                i, u = V_PAIRS[0] + n, n % 2
                split_after(split_hi, act, i, 0)
                act.wait_ge(sem["gw_in"], 32 * n + 32)
                if n:
                    act.wait_ge(sem["gi_ps"], 4 * n)
                else:
                    act.wait_ge(sem["stage_free"], 2 + 8)
                act.activation(gws[:, HI, :], graw[:, :], ACT.Copy).then_inc(sem["gw_hi"], 1)
                act.wait_ge(sem[f"xg{u}"], 32 * (n // 2) + 32)
                if n:
                    act.wait_ge(sem["yr_done"], n)
                act.activation(xcs[:, HI, :, :], xc[:, u, :, :], ACT.Copy).then_inc(sem["x_hi"], 1)
                act.wait_ge(stored[0], 16 * i)
                evac_v(i, 0, range(4))
                for g, b in ((0, "b_a"), (1, "b_i")):
                    for q in range(4):
                        m, half = q // 2, q % 2
                        act.wait_ge(sem["gi_ps" if g else "gr_ps"], 4 * n + q + 1)
                        col = PRM[b] + 2 * n + m
                        act.activation(ri[:, g, m, half * HALF:(half + 1) * HALF], ps[:, 4 + q, :], ACT.Sigmoid,
                                       bias=prm[:, col:col + 1]).then_inc(sem["gi_evac" if g else "gr_evac"], 1)
                act.wait_ge(sem["gr_evac"], 4 * n + 4)
                if n == 0:
                    act.wait_ge(sem["rate"], 3)
                for m in range(2):
                    c = 2 * n + m
                    act.activation(ea[:, m, :], ri[:, 0, m, :], ACT.Exp, scale=sp[:, 3, c:c + 1])
                    act.activation(th[:, m, :], ri[:, 0, m, :], ACT.Tanh, scale=sp[:, 4, c:c + 1]).then_inc(
                        sem["tanh_done"], 1)
                    act.wait_ge(sem["tanh_done"], 4 * n + 2 * m + 1)
                    act.activation(ri[:, 0, m, :], ri[:, 0, m, :], ACT.Tanh, scale=sp[:, 5, c:c + 1]).then_inc(
                        sem["tanh_done"], 1)
                split_after(split_hi, act, i, 1)
                act.wait_ge(stored[1], 16 * i)
                evac_v(i, 1, range(0, 2))
                act.wait_ge(sem["om_done"], n + 1)
                act.activation(ri[:, 0, :, :], ri[:, 0, :, :], ACT.Sqrt).then_inc(sem["sq_done"], 1)
                evac_v(i, 1, range(2, 4))

            with act.Fori(*QK_PAIRS) as i:
                for slot in range(2):
                    split_after(split_hi, act, i, slot)
            to_stage(*G_PAIRS, ACT.Silu)
            with act.Fori(*M_PAIRS) as i:
                for slot in range(2):
                    split_after(split_hi, act, i, slot)
                    t = i * 2 + (slot - 2 * M_PAIRS[0])
                    act.wait_ge(sem[f"ys_in{slot}"], i * 16 + (16 - 16 * M_PAIRS[0]))
                    alone(act)
                    act.activation(yr[:, HI, ds(t, 1), :], stg[:, slot:slot + 1, :], ACT.Copy).then_inc(sem["ys_hi"], 1)
                    evac_ost(i, slot, ACT.Sigmoid, -8 * 8)
            for n in range(4):
                split_after(split_hi, act, PAIR_RNNO + n // 2, n % 2)

            def hi_parts(h, j):
                r, slot = h * 8 + j, j % 2
                act.wait_ge(sem[f"qr{slot}"], h * (48 * 4) + 48 * (j // 2 + 1))
                if not (isinstance(r, int) and r < 2):
                    act.wait_ge(sem["o_done"], r - 1)
                act.activation(qkvs[:, slot, HI, :], qkv[:, slot, :], ACT.Copy).then_inc(sem["qhi"], 1)

            def normalise(h, j):
                r, slot = h * 8 + j, j % 2
                act.wait_ge(sem["h_var"], r + 1)
                act.activation(hn[:, slot, 9:10], hn[:, slot, 8:9], ACT.Sqrt).then_inc(sem["h_std"], 1)
                if not (isinstance(r, int) and r < 2):
                    act.wait_ge(sem["ont_ps"], r - 1)
                act.wait_ge(sem["h_nb"], r + 1)
                act.activation(on[:, slot, :], ps[:, 2, :], ACT.Identity, scale=hn[:, slot, 11:12],
                               bias=hn[:, slot, 12:13]).then_inc(sem["on_done"], 1)

            def y_hi(h, j):
                r, slot = h * 8 + j, j % 2
                seg = j // 4
                act.wait_ge(sem["y_done"], r + 1)
                if j % 4 == 0 and not isinstance(h, int):
                    act.wait_ge(sem["acc"], h * 16 + (8 * seg - 8))
                if j % 4 == 0 and isinstance(h, int) and h > 0:
                    act.wait_ge(sem["acc"], h * 16 + 8 * seg - 8)
                act.activation(yh[:, seg, HI, :, (j % 4) * CHUNK:(j % 4 + 1) * CHUNK], ych[:, slot, :, :],
                               ACT.Copy).then_inc(sem["y_hi"], 1)

            def step(h, j, following):
                r, slot = h * 8 + j, j % 2
                first = isinstance(h, int)
                act.wait_ge(sem["kt_ps"], r + 1)
                act.activation(ktm[:, slot, :, :], ps[:, 1, :].rearrange("p (a c) -> p a c", a=2),
                               ACT.Copy).then_inc(sem["km_done"], 1)
                act.wait_ge(sem["sc_mk"], r + 1)
                act.activation(scs[:, slot, HI, :], sc[:, slot, :], ACT.Copy).then_inc(sem["sc_hi"], 1)
                if following:
                    hi_parts(*following)
                if not (first and j == 0):
                    normalise(*previous(h, j))
                if (j == 3 and not first) or j == 5:
                    split_hi(act, h + PAIR_RETO, 0 if j == 3 else 1)
                if j < 7:
                    act.wait_ge(sem["t_done"], h * 7 + (j + 1))
                    alone(act)
                    act.activation(sts[:, slot, HI, :, :], stt[:, :, :], ACT.Copy,
                                   scale=con[:, ds(h + CON["chunk"], 1)]).then_inc(sem["s_hi"], 1)
                if not (first and j == 0):
                    y_hi(*previous(h, j))

            hi_parts(0, 0)
            for j in range(7):
                step(0, j, (0, j + 1))
            with act.Fori(1, HEADS) as h:
                step(h - 1, 7, (h, 0))
                for j in range(7):
                    step(h, j, (h, j + 1))
            step(HEADS - 1, 7, None)
            normalise(HEADS - 1, 7)
            y_hi(HEADS - 1, 7)

            split_hi(act, PAIR_OUT, 0)
            for n in range(16):
                half, t = n // 8, n % 8
                act.wait_ge(sem["mx_f"], n + 1)
                act.activation(mix[:, HI, t, half * HALF:(half + 1) * HALF], mxf[:, n % 2, :],
                               ACT.Copy).then_inc(sem["mx_hi"], 1)
                if n == 7:
                    split_hi(act, PAIR_OUT, 1)
            for n in range(1, 4):
                split_after(split_hi, act, PAIR_OUT + n // 2, n % 2)
            for half in range(2):
                norm_scale_act(act, x1, lambda t: act.wait_ge(sem["x1_done"], 12 + t // 2 + 1), sem["ss2"], sem["std2"],
                               lambda t: xn1[:, t, :], half)
                for n in range(8 * half, 8 * half + 8):
                    turn_hi(act, n, mix, PRM["ffn_g"], sem["tr2_ps"], sem["n2_hi"])

            def evac_up(g, pair, slot, val):
                for job in range(4):
                    half, m = job // 2, job % 2
                    if half == 0 and not (isinstance(g, int) and g == 0 and val == 0):
                        act.wait_ge(sem["conv_done"], g * 4 + (2 * val + m - 1))
                    if job < 3:
                        act.wait_ge(sem["gv_job"], g * 6 + (3 * val + job + 1))
                    else:
                        act.wait_ge(blk[slot], pair + 2)
                    act.activation(fst[:, m, 4 + half * HALF:4 + (half + 1) * HALF], ps[:, 4 * val + job, :],
                                   ACT.Copy).then_inc(sem["gv_evac"], 1)

            def silu_gate(g):
                for m in range(2):
                    act.wait_ge(sem["conv_done"], g * 4 + (m + 1))
                    act.activation(gt[:, m, :], gt[:, m, :], ACT.Silu).then_inc(sem["g_silu"], 1)

            def act_hi(g, hslot):
                act.wait_ge(sem["a_mul"], g + 1)
                if not (isinstance(g, int) and g < 2):
                    act.wait_ge(sem["d_add"], g * 16 - 16)
                act.activation(hact[:, hslot, HI, :, :], vt[:, :, :], ACT.Copy).then_inc(sem["a_hi"], 1)

            def group(i, u):
                g = i * 2 + (1 + u)
                c = 3 * u
                pp = [(i * 3 + (PAIR_FFN + 1 + (c + q) // 2), (c + q) % 2) for q in range(3)]
                split_after(split_hi, act, *pp[0])
                evac_up(g, *pp[0], 0)
                split_after(split_hi, act, *pp[1])
                silu_gate(g)
                evac_up(g, *pp[1], 1)
                split_after(split_hi, act, *pp[2])
                act_hi(g, 1 - u)

            split_hi(act, PAIR_FFN, 1)
            evac_up(0, PAIR_FFN, 0, 0)
            split_hi(act, PAIR_FFN + 1, 0)
            silu_gate(0)
            evac_up(0, PAIR_FFN, 1, 1)
            act_hi(0, 0)
            group(0, 0)
            group(0, 1)
            with act.Fori(1, (GROUPS - 1) // 2) as i:
                group(i, 0)
                group(i, 1)

            def row_complete(t):
                act.wait_ge(sem["d_add"], 16 * (GROUPS - 1) + 2 * t + 2)
                if t >= 2:
                    act.wait_ge(sem["ss3"], t - 1)

            for t in range(KT):
                row_complete(t)
                act.activation(vt[:, t % 2, :], x1[:, t, :], ACT.Square, accum_out=rms_ss[:, t:t + 1]).then_inc(sem["ss3"], 1)
                act.wait_ge(sem["ss3"], t + 1)
                act.activation(rms_rs[:, t:t + 1], rms_ss[:, t:t + 1], ACT.Sqrt, scale=1.0 / D,
                               bias=eps_norm[:, 0:1]).then_inc(sem["std3"], 1)

        @block.vector
        def _(dve):
            for slot in range(2):
                dve.sem_inc(w_split[slot], 1)
            for name, n in (("qk_evac", 4), ("rope_rd", 1), ("stage_free", 2), ("gw_sp", 1), ("ys_sp", 2)):
                dve.sem_inc(sem[name], n)
            norm_apply_dve(dve, x_in, xn_in, sem["std_done"], sem["rs_done"], sem["xn_done"], 0)
            split_lo(dve, 0, 0)
            dve.wait_ge(sem["const_in"], 16 * 4)
            for n in range(8):
                turn_lo(dve, n, actv, PRM["in_g"], sem["nhi_done"], sem["nsp_done"])
            norm_apply_dve(dve, x_in, xn_in, sem["std_done"], sem["rs_done"], sem["xn_done"], 1)
            for n in range(8, 16):
                turn_lo(dve, n, actv, PRM["in_g"], sem["nhi_done"], sem["nsp_done"])

            def job_wait(pair, slot, job):
                if job < 3:
                    dve.wait_ge(sem["job"], pair * 6 + (3 * slot + job + 1))
                else:
                    dve.wait_ge(blk[slot], pair + 2)

            def stage_ready(i, slot, m, base):
                dve.wait_ge(sem["evac"], i * 8 + (4 * slot + 3 + m + 8 - base))

            dve.memset(stage[:, :, 0:4], 0.0).then_inc(sem["conv_st"], 1)
            dve.wait_ge(sem["conv_st"], 1)

            def conv(dst, src, taps, w_col, b_col, st, st_count):
                for q in range(taps):
                    tap = taps - 1 - q
                    s_ = src[:, 4 - q:4 - q + S]
                    w = prm[:, ds(w_col + tap, 1)]
                    if q == 0:
                        ins = dve.tensor_scalar(dst, s_, w, prm[:, ds(b_col, 1)], ALU.mult, ALU.add)
                    else:
                        dve.wait_ge(st, st_count + q)
                        ins = dve.scalar_tensor_tensor(out=dst, in0=s_, scalar=w, in1=dst, op0=ALU.mult, op1=ALU.add)
                    if q < taps - 1:
                        ins.then_inc(st, 1)
                return ins

            def x_rnn(i):
                for slot in range(2):
                    split_after(split_lo, dve, i, slot)
                    if not (isinstance(i, int) and i == 0):
                        dve.wait_ge(stored[slot], i * 16)
                    for m in range(2):
                        stage_ready(i, slot, m, 0)
                        c = i * 4 + (2 * slot + m - 4 * XR_PAIRS[0])
                        conv(ost[:, slot, m, :], stage[:, m, :], 4, c * 4 + PRM["conv_w"], c + PRM["conv_b"],
                             sem["conv_st"], c * 3 + 1).then_inc(sem["stage_free"], 1)
                    dve.wait_ge(sem["stage_free"], i * 4 + (2 * slot + 4))
                    dve.sem_inc(ost_ready[slot], 1)

            x_rnn(0)
            with dve.Fori(1, XR_PAIRS[1]) as i:
                x_rnn(i)
            with dve.Fori(*GR_PAIRS) as i:
                for slot in range(2):
                    split_after(split_lo, dve, i, slot)
            a_p = prm[:, PRM["a_param"]:PRM["a_param"] + 8]
            spn = [0]

            def small(ins):
                ins.then_inc(sem["l_st"], 1)
                spn[0] += 1
                dve.wait_ge(sem["l_st"], spn[0])

            small(dve.tensor_scalar(sp[:, 2, :], a_p, -1.0, None, ALU.mult))
            dve.tensor_tensor(sp[:, 0, :], a_p, sp[:, 2, :], ALU.min).then_inc(sem["sp_st"], 1)
            dve.wait_ge(sem["sp_st"], 2)
            small(dve.tensor_scalar(sp[:, 3, :], sp[:, 1, :], 2.0, None, ALU.add))
            small(dve.reciprocal(sp[:, 3, :], sp[:, 3, :]))
            small(dve.tensor_tensor(sp[:, 1, :], sp[:, 1, :], sp[:, 3, :], ALU.mult))
            small(dve.tensor_tensor(sp[:, 4, :], sp[:, 1, :], sp[:, 1, :], ALU.mult))
            small(dve.tensor_scalar(sp[:, 5, :], sp[:, 4, :], 2.0 / 17, 2.0 / 15, ALU.mult, ALU.add))
            for odd in (13, 11, 9, 7, 5, 3, 1):
                small(dve.tensor_tensor(sp[:, 5, :], sp[:, 5, :], sp[:, 4, :], ALU.mult))
                small(dve.tensor_scalar(sp[:, 5, :], sp[:, 5, :], 2.0 / odd, None, ALU.add))
            small(dve.tensor_tensor(sp[:, 5, :], sp[:, 5, :], sp[:, 1, :], ALU.mult))
            small(dve.tensor_scalar(sp[:, 2, :], sp[:, 2, :], 0.0, None, ALU.max))
            small(dve.tensor_tensor(sp[:, 7, :], sp[:, 2, :], sp[:, 5, :], ALU.add))
            for q, f in ((3, -8.0), (4, 4.0), (5, 8.0)):
                dve.tensor_scalar(sp[:, q, :], sp[:, 7, :], f, None, ALU.mult).then_inc(sem["rate"], 1)
            lsteps = spn[0]


            for n in range(LRU_BLOCKS):
                i, u = V_PAIRS[0] + n, n % 2
                split_after(split_lo, dve, i, 0)
                dve.wait_ge(sem["gw_hi"], n + 1)
                dve.tensor_tensor(gws[:, LO, :], graw[:, :], gws[:, HI, :].bitcast(F32), ALU.subtract).then_inc(
                    sem["gw_sp"], 1)
                dve.wait_ge(sem["x_hi"], n + 1)
                dve.tensor_tensor(xcs[:, LO, :, :], xc[:, u, :, :], xcs[:, HI, :, :].bitcast(F32),
                                  ALU.subtract).then_inc(sem["x_sp"], 1)
                dve.wait_ge(sem["tanh_done"], 4 * n + 4)
                small(dve.scalar_tensor_tensor(out=th[:, :, :], in0=ea[:, :, :], scalar=1.0, in1=th[:, :, :],
                                               op0=ALU.add, op1=ALU.mult))
                small(dve.tensor_scalar(ea[:, :, :], th[:, :, :], -1.0, 1.0, ALU.mult, ALU.add))
                small(dve.tensor_tensor(th[:, :, :], ea[:, :, :], ea[:, :, :], ALU.mult))
                dve.scalar_tensor_tensor(out=ri[:, 0, :, :], in0=th[:, :, :], scalar=1.0, in1=ri[:, 0, :, :],
                                         op0=ALU.add, op1=ALU.mult).then_inc(sem["om_done"], 1)
                dve.wait_ge(sem["gi_evac"], 4 * n + 4 + 4)
                small(dve.tensor_tensor(ri[:, 1, :, :], ri[:, 1, :, :], xc[:, u, :, :], ALU.mult))
                split_after(split_lo, dve, i, 1)
                dve.wait_ge(sem["sq_done"], n + 1)
                small(dve.tensor_tensor(ri[:, 1, :, :], ri[:, 1, :, :], ri[:, 0, :, :], ALU.mult))
                dve.tensor_tensor_scan(th[:, 0, :], ea[:, 0, :], ri[:, 1, 0, :], 0.0, ALU.mult, ALU.add)
                small(dve.tensor_tensor_scan(th[:, 1, :], ea[:, 1, :], ri[:, 1, 1, :], 0.0, ALU.mult, ALU.add))
                dve.tensor_tensor(gel[:, u, :, :], gel[:, u, :, :], th[:, :, :], ALU.mult).then_inc(sem["yr_done"], 1)

            def rotary(i):
                for slot in range(2):
                    split_after(split_lo, dve, i, slot)
                    dve.wait_ge(stored[slot], i * 16)
                    for half in range(2):
                        job_wait(i, slot, 2 * half + 1)
                        dve.wait_ge(sem["rope_rd"], i * 4 + (2 * slot + half + 1 - 4 * QK_PAIRS[0]))
                        cols = slice(half * HALF, (half + 1) * HALF)
                        t1, tt2 = ps[:, 4 * slot + 2 * half, :], ps[:, 4 * slot + 2 * half + 1, :]
                        dve.tensor_tensor(rope[:, 0, :], t1, cos[:, cols], ALU.mult)
                        dve.tensor_tensor(rope[:, 1, :], tt2, sin[:, cols], ALU.mult)
                        dve.tensor_tensor(rope[:, 2, :], t1, sin[:, cols], ALU.mult).then_inc(sem["rope_st"], 1)
                        dve.tensor_tensor(rope[:, 3, :], tt2, cos[:, cols], ALU.mult).then_inc(sem["qk_evac"], 1)
                        dve.wait_ge(sem["rope_st"], i * 4 + (2 * slot + half + 1 - 4 * QK_PAIRS[0]))
                        dve.wait_ge(sem["qk_evac"], i * 4 + (2 * slot + half + 1 + 4 - 4 * QK_PAIRS[0]))
                        dve.tensor_tensor(ost[:, slot, 0, cols], rope[:, 0, :], rope[:, 1, :], ALU.subtract)
                        dve.tensor_tensor(ost[:, slot, 1, cols], rope[:, 2, :], rope[:, 3, :],
                                          ALU.add).then_inc(sem["rope_rd"], 1)
                    dve.wait_ge(sem["rope_rd"], i * 4 + (2 * slot + 3 - 4 * QK_PAIRS[0]))
                    dve.sem_inc(ost_ready[slot], 1)

            dve.wait_ge(sem["cs_in"], 32)
            with dve.Fori(*QK_PAIRS) as i:
                rotary(i)
            with dve.Fori(*G_PAIRS) as i:
                for slot in range(2):
                    split_after(split_lo, dve, i, slot)
                    dve.wait_ge(stored[slot], i * 16)
                    for m in range(2):
                        stage_ready(i, slot, m, 8 * 8)
                        dve.tensor_scalar(ost[:, slot, m, :], stage[:, m, 4:],
                                          prm[:, ds(i * 4 + (2 * slot + m + PRM["gn_g"] - 4 * G_PAIRS[0]), 1)], None,
                                          ALU.mult).then_inc(sem["stage_free"], 1)
                    dve.wait_ge(sem["stage_free"], i * 4 + (2 * slot + 4 - stage_base(G_PAIRS[0])))
                    dve.sem_inc(ost_ready[slot], 1)
            with dve.Fori(*M_PAIRS) as i:
                for slot in range(2):
                    split_after(split_lo, dve, i, slot)
                    t = i * 2 + (slot - 2 * M_PAIRS[0])
                    dve.wait_ge(sem["ys_hi"], t + 1)
                    dve.tensor_tensor(yr[:, LO, ds(t, 1), :], stg[:, slot:slot + 1, :],
                                      yr[:, HI, ds(t, 1), :].bitcast(F32), ALU.subtract).then_inc(sem["ys_sp"], 1)

            for n in range(4):
                pair, slot = PAIR_RNNO + n // 2, n % 2
                split_after(split_lo, dve, pair, slot)
                dve.wait_ge(stored[slot], 16 * pair)
                dve.wait_ge(sem["sg_in"], 16 * n + 16)
                for job in range(4):
                    half, m = job // 2, job % 2
                    cols = slice(half * HALF, (half + 1) * HALF)
                    job_wait(pair, slot, job)
                    dve.tensor_tensor(ost[:, slot, m, cols], stg[:, m, cols], ps[:, 4 * slot + job, :],
                                      ALU.mult).then_inc(sem["sg_used"], 1)
                dve.wait_ge(sem["sg_used"], 4 * n + 4)
                dve.sem_inc(ost_ready[slot], 1)

            def stats(h, j):
                r, slot = h * 8 + j, j % 2
                dve.wait_ge(sem["o_done"], r + 1)
                dve.bn_stats(hn[:, slot, 0:6], ps[:, 2, :]).then_inc(sem["h_st"], 1)
                dve.wait_ge(sem["h_st"], r + 1)
                alone(dve)
                dve.bn_aggr(hn[:, slot, 6:8], hn[:, slot, 0:6]).then_inc(sem["h_ag"], 1)
                dve.wait_ge(sem["h_ag"], r + 1)
                dve.tensor_scalar(hn[:, slot, 8:9], hn[:, slot, 7:8], con[:, ds(h + CON["gam2"], 1)], eps_gn[:, 0:1],
                                  ALU.mult, ALU.add).then_inc(sem["h_var"], 1)

            def coefficients(h, j):
                r, slot = h * 8 + j, j % 2
                dve.wait_ge(sem["h_std"], r + 1)
                dve.reciprocal(hn[:, slot, 10:11], hn[:, slot, 9:10]).then_inc(sem["h_rec"], 1)
                dve.wait_ge(sem["h_rec"], r + 1)
                dve.tensor_scalar(hn[:, slot, 11:12], hn[:, slot, 10:11], con[:, ds(h + CON["gam"], 1)], None,
                                  ALU.mult).then_inc(sem["h_rs"], 1)
                dve.wait_ge(sem["h_rs"], r + 1)
                dve.scalar_tensor_tensor(out=hn[:, slot, 12:13], in0=hn[:, slot, 6:7], scalar=-1.0,
                                         in1=hn[:, slot, 11:12], op0=ALU.mult, op1=ALU.mult).then_inc(sem["h_nb"], 1)

            def gate(h, j):
                r, slot = h * 8 + j, j % 2
                if not (isinstance(r, int) and r < 2):
                    dve.wait_ge(sem["y_sp"], r - 1)
                dve.wait_ge(sem["ont_ps"], r + 1)
                dve.wait_ge(sem[f"gr{slot}"], h * 64 + 16 * (j // 2 + 1))
                dve.tensor_tensor(ych[:, slot, :, :], ps[:, 5, :].rearrange("p (m c) -> p m c", m=4), gch[:, slot, :, :],
                                  ALU.mult).then_inc(sem["y_done"], 1)

            def gate_lo(h, j):
                r, slot = h * 8 + j, j % 2
                seg, cols = j // 4, slice((j % 4) * CHUNK, (j % 4 + 1) * CHUNK)
                dve.wait_ge(sem["y_hi"], r + 1)
                dve.tensor_tensor(yh[:, seg, LO, :, cols], ych[:, slot, :, :], yh[:, seg, HI, :, cols].bitcast(F32),
                                  ALU.subtract).then_inc(sem["y_sp"], 1)

            def accumulate(hh, seg, t):
                if seg == 1 and t % 4 == 3:
                    dve.wait_ge(blk[t // 4], hh + (PAIR_RETO + 2))
                else:
                    dve.wait_ge(sem["reto"], hh * 14 + (8 * seg + t + 1 - (seg == 1 and t > 3)))
                cols = slice(seg * HALF, (seg + 1) * HALF)
                dve.tensor_tensor(yacc[:, t, cols], yacc[:, t, cols], ps[:, 6 + t % 2, :], ALU.add).then_inc(sem["acc"], 1)

            def step(h, j):
                r, slot = h * 8 + j, j % 2
                first = isinstance(h, int)
                before = not (first and j == 0)
                parts = [] if first and j < 5 else reto_parts(h, j)
                dve.wait_ge(sem["sc_ps"], r + 1)
                if not (first and j < 2):
                    dve.wait_ge(sem["sc_sp"], r - 1)
                dve.tensor_tensor(sc[:, slot, :], ps[:, 0, slot * P:(slot + 1) * P], mask[:, :],
                                  ALU.mult).then_inc(sem["sc_mk"], 1)
                dve.wait_ge(sem["sc_hi"], r + 1)
                dve.tensor_tensor(scs[:, slot, LO, :], sc[:, slot, :], scs[:, slot, HI, :].bitcast(F32),
                                  ALU.subtract).then_inc(sem["sc_sp"], 1)
                if before:
                    stats(*previous(h, j))
                    coefficients(*previous(h, j))
                if j < 7:
                    if not (first and j == 0):
                        dve.wait_ge(sem["s_sp"], h * 7 + j)
                    dve.wait_ge(sem["u_ps"], h * 7 + (j + 1))
                    if j:
                        for m in range(2):
                            last = dve.scalar_tensor_tensor(out=stt[:, m, :], in0=stt[:, m, :],
                                                            scalar=con[:, ds(h + CON["chunk"], 1)],
                                                            in1=ps[:, 3 + m, :], op0=ALU.mult, op1=ALU.add)
                    else:
                        last = dve.tensor_copy(stt[:, :, :], ps[:, 3:5, :])
                    last.then_inc(sem["t_done"], 1)
                for n in parts[:1]:
                    accumulate(*n)
                if (j == 3 and not first) or j == 5:
                    split_lo(dve, h + PAIR_RETO, 0 if j == 3 else 1)
                if j < 7:
                    dve.wait_ge(sem["s_hi"], h * 7 + (j + 1))
                    dve.scalar_tensor_tensor(out=sts[:, slot, LO, :, :], in0=stt[:, :, :],
                                             scalar=con[:, ds(h + CON["chunk"], 1)],
                                             in1=sts[:, slot, HI, :, :].bitcast(F32), op0=ALU.mult,
                                             op1=ALU.subtract).then_inc(sem["s_sp"], 1)
                if before:
                    gate(*previous(h, j))
                for n in parts[1:]:
                    accumulate(*n)
                if before:
                    gate_lo(*previous(h, j))

            dve.wait_ge(sem["yz"], 1)
            for j in range(NCH):
                step(0, j)
            with dve.Fori(1, HEADS) as h:
                for j in range(NCH):
                    step(h, j)
            stats(HEADS - 1, 7)
            coefficients(HEADS - 1, 7)
            accumulate(HEADS - 1, 0, 6)
            accumulate(HEADS - 1, 0, 7)
            gate(HEADS - 1, 7)
            gate_lo(HEADS - 1, 7)
            def mixed(n):
                dve.wait_ge(sem["mx_mul"], n + 1)
                if n >= 2:
                    dve.wait_ge(sem["mx_sp"], n - 1)
                dve.tensor_tensor(mxf[:, n % 2, :], msg[:, n % 4, :], mrb[:, n % 4, :], ALU.add).then_inc(sem["mx_f"], 1)

            def mixed_lo(n):
                half, t = n // 8, n % 8
                cols = slice(half * HALF, (half + 1) * HALF)
                dve.wait_ge(sem["mx_hi"], n + 1)
                dve.tensor_tensor(mix[:, LO, t, cols], mxf[:, n % 2, :], mix[:, HI, t, cols].bitcast(F32),
                                  ALU.subtract).then_inc(sem["mx_sp"], 1)

            for t in range(8):
                accumulate(HEADS - 1, 1, t)
                mixed(t)
                if t:
                    mixed_lo(t - 1)
            split_lo(dve, PAIR_OUT, 0)
            for n in range(8, 16):
                mixed(n)
                mixed_lo(n - 1)
                if n == 9:
                    split_lo(dve, PAIR_OUT, 1)
            mixed_lo(15)

            dve.wait_ge(sem["x_re"], 32)
            for n in range(4):
                pair, slot = PAIR_OUT + n // 2, n % 2
                if n:
                    split_after(split_lo, dve, pair, slot)
                for job in range(4):
                    if job < 3:
                        dve.wait_ge(sem["job"], 6 * PAIR_RETO + 3 * n + job + 1)
                    else:
                        dve.wait_ge(blk[slot], pair + 2)
                    o = x1[:, 2 * job:2 * job + 2, n * BC:(n + 1) * BC]
                    dve.tensor_tensor(o, o, ps[:, 4 * slot + job, :].rearrange("p (t c) -> p t c", t=2),
                                      ALU.add).then_inc(sem["x1_done"], 1)
            for half in range(2):
                norm_apply_dve(dve, x1, xn1, sem["std2"], sem["rs2"], sem["xn2"], half)
                if half == 0:
                    for n in range(8):
                        turn_lo(dve, n, mix, PRM["ffn_g"], sem["n2_hi"], sem["n2_sp"])
            for n in range(8, 16):
                turn_lo(dve, n, mix, PRM["ffn_g"], sem["n2_hi"], sem["n2_sp"])
            dve.memset(fst[:, :, 0:4], 0.0).then_inc(sem["f_st"], 1)
            dve.wait_ge(sem["f_st"], 1)

            def conv_tile(g, val, m):
                dve.wait_ge(sem["gv_evac"], g * 8 + (4 * val + 3 + m))
                c = g * 2 + (22 * val + m)
                if val == 0 and not (isinstance(g, int) and g == 0):
                    dve.wait_ge(sem["a_mul"], g)
                if val == 1 and not (isinstance(g, int) and g == 0):
                    dve.wait_ge(sem["a_sp"], g)
                conv((vt if val else gt)[:, m, :], fst[:, m, :], 3, c * 3 + PRM["fconv_w"], c + PRM["fconv_b"],
                     sem["f_st"], g * 8 + (4 * val + 2 * m + 1)).then_inc(sem["conv_done"], 1)

            def multiply(g):
                dve.wait_ge(sem["g_silu"], g * 2 + 2)
                dve.wait_ge(sem["conv_done"], g * 4 + 4)
                dve.tensor_tensor(vt[:, :, :], vt[:, :, :], gt[:, :, :], ALU.mult).then_inc(sem["a_mul"], 1)

            def act_lo(g, hslot):
                dve.wait_ge(sem["a_hi"], g + 1)
                dve.tensor_tensor(hact[:, hslot, LO, :, :], vt[:, :, :], hact[:, hslot, HI, :, :].bitcast(F32),
                                  ALU.subtract).then_inc(sem["a_sp"], 1)

            def add_down(g, pair, slot, jobs):
                for job in jobs:
                    t, half = job // 2, job % 2
                    cols = slice(half * HALF, (half + 1) * HALF)
                    if job < 15:
                        dve.wait_ge(sem["d_ps"], g * 15 + (job + 1))
                    else:
                        dve.wait_ge(blk[slot], pair + 2)
                    dve.tensor_tensor(x1[:, t, cols], x1[:, t, cols], ps[:, job % 8, :], ALU.add).then_inc(sem["d_add"], 1)

            def group(i, u):
                g = i * 2 + (1 + u)
                c = 3 * u
                pp = [(i * 3 + (PAIR_FFN + 1 + (c + q) // 2), (c + q) % 2) for q in range(3)]
                split_after(split_lo, dve, *pp[0])
                conv_tile(g, 0, 0)
                conv_tile(g, 0, 1)
                split_after(split_lo, dve, *pp[1])
                conv_tile(g, 1, 0)
                add_down(g - 1, *pp[2], range(0, 4))
                conv_tile(g, 1, 1)
                add_down(g - 1, *pp[2], range(4, 8))
                multiply(g)
                split_after(split_lo, dve, *pp[2])
                add_down(g - 1, *pp[2], range(8, 12))
                act_lo(g, 1 - u)
                add_down(g - 1, *pp[2], range(12, 16))

            split_lo(dve, PAIR_FFN, 1)
            conv_tile(0, 0, 0)
            conv_tile(0, 0, 1)
            split_lo(dve, PAIR_FFN + 1, 0)
            conv_tile(0, 1, 0)
            conv_tile(0, 1, 1)
            multiply(0)
            act_lo(0, 0)
            group(0, 0)
            group(0, 1)
            with dve.Fori(1, (GROUPS - 1) // 2) as i:
                group(i, 0)
                group(i, 1)

            def finish(t):
                dve.wait_ge(sem["std3"], t + 1)
                dve.reciprocal(rms_rs[:, t:t + 1], rms_rs[:, t:t + 1]).then_inc(sem["rs3"], 1)
                dve.wait_ge(sem["rs3"], t + 1)
                dve.scalar_tensor_tensor(out=x1[:, t, :], in0=x1[:, t, :], scalar=rms_rs[:, t:t + 1], in1=gbc[:, :],
                                         op0=ALU.mult, op1=ALU.mult).then_inc(sem["out_t"], 1)

            dve.wait_ge(sem["gb_in"], 16)
            for t in range(KT):
                add_down(GROUPS - 1, PAIR_FFN + 16, 0, (2 * t, 2 * t + 1))
                if t:
                    finish(t - 1)
            finish(KT - 1)


def kernel(**inputs):
    import numpy as np
    import concourse.bacc as bacc
    from concourse.bass_utils import run_bass_kernel_spmd

    nc = bacc.Bacc("TRN2", target_bir_lowering=False, num_devices=1)
    get = {k: np.asarray(v) for k, v in inputs.items()}
    arrays, aps = {}, {}

    def dram_in(name, array):
        arrays[name] = np.ascontiguousarray(array)
        aps[name] = nc.dram_tensor(name, array.shape, F32, kind="ExternalInput").ap()

    for name in ("x", "w_in", "w_ret_o", "lru_w_a", "lru_w_i", "w_rnn_o", "w_out", "w_up", "w_down"):
        dram_in(name, get[name])

    def columns(v):
        return v.reshape(-1, P).T

    def tap_columns(w):
        taps, ch = w.shape
        return w.reshape(taps, ch // P, P).transpose(2, 1, 0).reshape(P, -1)

    dram_in("prm", np.concatenate(
        [columns(get["in_norm_g"][0]), columns(get["ffn_norm_g"][0]), columns(get["ret_gn_g"][0]),
         tap_columns(get["lru_conv_w"][0]), columns(get["lru_conv_b"][0]), columns(get["lru_b_a"][0]),
         columns(get["lru_b_i"][0]), columns(get["lru_a_param"][0]), tap_columns(get["ffn_conv_w"][0]),
         columns(get["ffn_conv_b"][0])], axis=1))
    dram_in("final_g", np.broadcast_to(get["final_norm_g"], (P, D)))

    log_g = np.log1p(-np.exp2(-5.0 - np.arange(HEADS, dtype=np.float64)))
    pos1 = np.arange(1, CHUNK + 1, dtype=np.float64)[:, None]
    con = np.concatenate([np.exp(-log_g * pos1) / 16.0, np.exp(log_g * pos1), np.exp(2 * log_g * pos1),
                          np.exp(log_g * CHUNK) + 0 * pos1], axis=1)
    dram_in("con", con.astype(np.float32))
    f = np.float32
    inv_freq = f(10000.0) ** (-np.arange(0, QK, 2, dtype=f) / f(QK))
    ang = (inv_freq.astype(f)[:, None] * np.arange(S, dtype=f)[None, :]).astype(f).astype(np.float64)
    dram_in("cos", np.cos(ang).astype(f))
    dram_in("sin", np.sin(ang).astype(f))
    dram_in("ident", np.eye(P, dtype=f))
    dram_in("mask", np.triu(np.ones((P, P), dtype=f)))
    aps["out"] = nc.dram_tensor("out", (1, S, D), F32, kind="ExternalOutput").ap()

    build(nc, aps)
    r = run_bass_kernel_spmd(nc, [arrays], core_ids=[0])
    return r.results[0]["out"]
```

```python
import concourse.bass as bass
from concourse import mybir

F32 = mybir.dt.float32
F32R = mybir.dt.float32r
ALU = mybir.AluOpType
ACT = mybir.ActivationFunctionType

P = 128
D = 1024
S = 1024
KT = D // P
HALF = 512
HEADS = 4
CHUNK = 128
NCH = S // CHUNK
QK = 256
VD = 512
BC = 256
BE = KT * BC
IN_W = 10240
FFN = 2816
GROUPS = FFN // BC
LRU_BLOCKS = 4
NORM_EPS = 1e-6
GN_EPS = 1e-5
HI, LO = 0, 1

XR_PAIRS, GR_PAIRS, V_PAIRS, QK_PAIRS, G_PAIRS, M_PAIRS = (0, 2), (2, 4), (4, 8), (8, 12), (12, 16), (16, 20)
PAIR_RNNO = IN_W // BC // 2
PAIR_RETO = PAIR_RNNO + 2
PAIR_OUT = PAIR_RETO + HEADS
PAIR_FFN = PAIR_OUT + 2
COL = {XR_PAIRS: 6144, GR_PAIRS: 6144, V_PAIRS: 0, QK_PAIRS: -4096, G_PAIRS: -2048, M_PAIRS: 0}

PRM = {}
_at = 0
for _name, _n in (("in_g", 8), ("ffn_g", 8), ("gn_g", 16), ("conv_w", 32), ("conv_b", 8), ("b_a", 8), ("b_i", 8),
                  ("a_param", 8), ("fconv_w", 3 * 44), ("fconv_b", 44)):
    PRM[_name] = _at
    _at += _n
PRM_W = _at
CON = {"vscale": 0, "gam": 4, "gam2": 8, "chunk": 12, "unchunk": 16}
CON_W = 20


def build(nc, a):
    ds = bass.ds

    top = [nc.sbuf_base + (-nc.sbuf_base) % 64]

    def at(name, shape, dt, offset):
        n = 4
        for x in shape[1:]:
            n *= x
        assert offset + n <= nc.sbuf_top, (name, offset + n - nc.sbuf_top)
        return nc.alloc_sbuf_tensor_at(name, shape, dt, offset=offset), offset + n

    def fixed(name, shape, dt=F32):
        t, top[0] = at(name, shape, dt, top[0] + (-top[0]) % 32)
        return t

    raw = fixed("raw", [P, 2, BE])
    ws = fixed("ws", [P, 2, 2, BE], F32R)
    prm = fixed("prm", [P, PRM_W])
    con = fixed("con", [P, CON_W])
    ident = fixed("ident", [P, P])
    mask = fixed("mask", [P, P])
    rms_ss = fixed("rms_ss", [P, 8])
    rms_rs = fixed("rms_rs", [P, 8])
    sp = fixed("sp", [P, 8, 8])
    hn = fixed("hn", [P, 2, 16])
    A = top[0] + (-top[0]) % 64
    B = A + 64 * 1024
    C = B + 64 * 1024

    K1 = 1024
    x_in, _ = at("x_in", [P, KT, D], F32, B)
    xn_in, _ = at("xn_in", [P, KT, D], F32, B + 32 * K1)
    actv, _ = at("actv", [P, 2, KT, S], F32R, A)
    ost, e = at("ost", [P, 2, 2, S], F32, C)
    graw, e = at("graw", [P, 4 * BC], F32, e)
    gws, _ = at("gws", [P, 2, 4 * BC], F32R, e)
    stage, _ = at("stage", [P, 2, 4 + S], F32, e)
    stg, _ = at("stg", [P, 2, S], F32, e)
    rope, e = at("rope", [P, 4, HALF], F32, B)
    cos, e = at("cos", [P, S], F32, e)
    sin, e = at("sin", [P, S], F32, e)
    yr, _ = at("yr", [P, 2, KT, S], F32R, B)
    xc, e = at("xc", [P, 2, 2, S], F32, B)
    gel, e = at("gel", [P, 2, 2, S], F32, e)
    xcs, _ = at("xcs", [P, 2, 2, S], F32R, e)
    ea, e = at("ea", [P, 2, S], F32, e)
    th, e = at("th", [P, 2, S], F32, e)
    ri, e = at("ri", [P, 2, 2, S], F32, e)
    yacc, _ = at("yacc", [P, KT, S], F32, A)
    qkv, e = at("qkv", [P, 2, 1024], F32, A + 32 * K1)
    gch, e = at("gch", [P, 2, 4, CHUNK], F32, e)
    qkvs, e = at("qkvs", [P, 2, 2, 1024], F32R, e)
    ych, e = at("ych", [P, 2, 4, CHUNK], F32, e)
    stt, e = at("state", [P, 2, HALF], F32, B)
    sts, e = at("state_s", [P, 2, 2, 2, HALF], F32R, e)
    ktm, e = at("ktm", [P, 2, 2, QK], F32R, e)
    sc, e = at("sc", [P, 2, CHUNK], F32, e)
    scs, e = at("scs", [P, 2, 2, CHUNK], F32R, e)
    on, e = at("on", [P, 2, VD], F32, e)
    yh, _ = at("yh", [P, 2, 2, 4, HALF], F32R, B + 32 * K1)
    mix, _ = at("mix", [P, 2, KT, S], F32R, A + 32 * K1)
    msg, e = at("msg", [P, 4, HALF], F32, C)
    mrb, e = at("mrb", [P, 4, HALF], F32, e)
    mxf, e = at("mxf", [P, 2, HALF], F32, e)
    x1, _ = at("x1", [P, KT, D], F32, B + 32 * K1)
    xn1, _ = at("xn1", [P, KT, D], F32, A)
    hact, _ = at("hact", [P, 2, 2, 2, S], F32R, A)
    fst, e = at("fst", [P, 2, 4 + S], F32, C)
    gt, e = at("gt", [P, 2, S], F32, e)
    vt, e = at("vt", [P, 2, S], F32, e)
    gbc, _ = at("gbc", [P, D], F32, C)

    ps = nc.alloc_psum_tensor("ps", [P, 8, HALF], F32)

    scr = nc.dram_tensor("scr", [IN_W, S], F32, kind="Internal").ap()
    scr_v = nc.dram_tensor("scr_v", [S, HEADS * VD], F32, kind="Internal").ap()
    scr_y = nc.dram_tensor("scr_y", [D, S], F32, kind="Internal").ap()
    scr_r = nc.dram_tensor("scr_r", [D, S], F32, kind="Internal").ap()
    ROW_Q, ROW_K, ROW_G, ROW_XC, ROW_GR, ROW_MR, ROW_MN = 0, 1024, 4096, 6144, 7168, 8192, 9216

    names = """alone const_in cs_in xt0 xt1 xt2 xt3 xt4 xt5 xt6 xt7 raw0 raw1 whi0 whi1 wsp0 wsp1 blk0 blk1 ini
        ss_done std_done rs_done xn_done tr_ps nhi_done nsp_done
        job qk_evac v_evac evac rope_st rope_rd stage_free ost0 ost1 sto0 sto1 conv_st
        yz qr0 qr1 gr0 gr1 qhi qsp sc_ps sc_mk sc_hi sc_sp kt_ps km_hi km_done o_done u_ps t_done s_hi s_sp vhi vsp
        h_st h_ag h_var h_std h_rec h_rs h_nb on_done ont_ps y_done y_hi y_sp reto acc
        sp_st rate xg0 xg1 x_hi x_sp gw_in gw_hi gw_sp gr_ps gi_ps gr_evac gi_evac tanh_done om_done sq_done l_st
        yr_done ysto0 ysto1 ys_in0 ys_in1 ys_hi ys_sp sg_in sg_used
        mx_in0 mx_in1 mx_in2 mx_in3 mx_mul mx_f mx_hi mx_sp x_re x1_done ss2 std2 rs2 xn2 tr2_ps n2_hi n2_sp
        gv_job gv_evac conv_done f_st g_silu a_mul a_hi a_sp d_ps d_add gb_in
        ss3 std3 rs3 out_t out_done""".split()
    sem = {n: nc.alloc_semaphore(n) for n in names}
    raw_in, w_hi, w_split, blk = ([sem[n + "0"], sem[n + "1"]] for n in ("raw", "whi", "wsp", "blk"))
    ost_ready, stored = [sem["ost0"], sem["ost1"]], [sem["sto0"], sem["sto1"]]


    def load_block(sp_, pair, slot, first, second):
        sp_.wait_ge(w_split[slot], pair + 1)
        for dst, src in (first, second):
            sp_.dma_start(dst, src).then_inc(raw_in[slot], 16)

    def load_columns(sp_, pair, slot, w, col):
        r = raw[:, slot, :].rearrange("p (k c) -> p k c", k=KT)
        v = w.rearrange("(k p) n -> p k n", p=P)
        load_block(sp_, pair, slot, *((r[:, 4 * q:4 * q + 4, :], v[:, 4 * q:4 * q + 4, ds(col, BC)]) for q in range(2)))

    def load_rows(sp_, pair, slot, w, row):
        r = raw[:, slot, :].rearrange("p (k c) -> p k c", k=2)
        load_block(sp_, pair, slot, *((r[:, k, :], w[ds(row + k * P, P), :]) for k in range(2)))

    def split_hi(act, pair, slot, n=BE):
        act.wait_ge(raw_in[slot], pair * 32 + 32)
        act.wait_ge(blk[slot], pair + 1)
        act.activation(ws[:, slot, HI, 0:n], raw[:, slot, 0:n], ACT.Copy).then_inc(w_hi[slot], 1)

    def split_lo(dve, pair, slot, n=BE):
        dve.wait_ge(w_hi[slot], pair + 1)
        dve.tensor_tensor(ws[:, slot, LO, 0:n], raw[:, slot, 0:n], ws[:, slot, HI, 0:n].bitcast(F32),
                          ALU.subtract).then_inc(w_split[slot], 1)

    def alone(eng):
        eng.sem_inc(sem["alone"], 1)

    def block_ready(pe, pair, slot):
        pe.wait_ge(w_split[slot], pair + 2)

    def split_after(f, eng, pair, slot):
        f(eng, pair, 1) if slot == 0 else f(eng, pair + 1, 0)

    def mm3(pe, out, w, x, first, last):
        pe.matmul(out, w(HI), x(HI), start=first, stop=False, skip_group_check=True)
        pe.matmul(out, w(HI), x(LO), start=False, stop=False, skip_group_check=True)
        return pe.matmul(out, w(LO), x(HI), start=False, stop=last, skip_group_check=True)

    def feature_jobs(pe, slot, src, bank0, before, done, around=None):
        w = ws[:, slot, :, :].rearrange("p a (k c) -> p a k c", k=KT)
        for job in range(4):
            half, m = job // 2, job % 2
            before(job)
            for k in range(KT):
                if around:
                    around(job, k, False)
                last = mm3(pe, ps[:, bank0 + job, :], lambda q: w[:, q, k, m * P:(m + 1) * P],
                           lambda q: src[:, q, k, half * HALF:(half + 1) * HALF], k == 0, k == KT - 1)
                if k == KT - 1:
                    last.then_inc(done if job < 3 else blk[slot], 1)
                if around:
                    around(job, k, True)

    def token_jobs(pe, slot, src, bank0, before, done):
        w = ws[:, slot, :, :].rearrange("p a (k c) -> p a k c", k=KT)
        for job in range(4):
            before(job)
            for t in (2 * job, 2 * job + 1):
                for k in range(KT):
                    last = mm3(pe, ps[:, bank0 + job, (t % 2) * BC:(t % 2 + 1) * BC],
                               lambda q: src[:, q, k, t * P:(t + 1) * P], lambda q: w[:, q, k, :],
                               k == 0, k == KT - 1)
            last.then_inc(done if job < 3 else blk[slot], 1)


    def norm_scale_act(act, src, t, ss_sem, std_sem, out):
        act.activation(out[:, t, :], src[:, t, :], ACT.Square, accum_out=rms_ss[:, t:t + 1]).then_inc(ss_sem, 1)
        act.wait_ge(ss_sem, t + 1)
        act.activation(rms_rs[:, t:t + 1], rms_ss[:, t:t + 1], ACT.Sqrt, scale=1.0 / D,
                       bias=eps_norm[:, 0:1]).then_inc(std_sem, 1)

    def norm_apply_dve(dve, src, dst, t, std_sem, rs_sem, xn_sem):
        dve.wait_ge(std_sem, t + 1)
        dve.reciprocal(rms_rs[:, t:t + 1], rms_rs[:, t:t + 1]).then_inc(rs_sem, 1)
        dve.wait_ge(rs_sem, t + 1)
        dve.tensor_scalar(dst[:, t, :], src[:, t, :], rms_rs[:, t:t + 1], None, ALU.mult).then_inc(xn_sem, 1)

    def turn_bank(n):
        return n if n < 8 else 4 + n % 4

    def turn_pe(pe, jobs, src, xn_sem, ps_sem, sp_sem):
        for n in jobs:
            half, k = n // 8, n % 8
            if k == 0:
                pe.wait_ge(xn_sem, 4 * half + 4)
            if n >= 8:
                pe.wait_ge(sp_sem, n - 3)
            for t in range(4):
                last = pe.transpose(ps[:, turn_bank(n), t * P:(t + 1) * P],
                                    src[:, 4 * half + t, k * P:(k + 1) * P], ident[:, :])
            last.then_inc(ps_sem, 1)

    def first_block(pe, slot_jobs, src_turn, sems):
        def around(job, k, after):
            if job == 0 and not after:
                pe.wait_ge(sems[2], k + 1)
            if job == 2 and k == 0 and not after:
                turn_pe(pe, range(8, 12), src_turn, *sems)
            if job == 2 and not after:
                pe.wait_ge(sems[2], 9 + k)
            if job == 2 and k < 4 and after:
                turn_pe(pe, (12 + k,), src_turn, *sems)
        slot_jobs(around)

    def turn_hi(act, n, dst, g, ps_sem, hi_sem):
        half, k = n // 8, n % 8
        act.wait_ge(ps_sem, n + 1)
        act.activation(dst[:, HI, k, half * HALF:(half + 1) * HALF], ps[:, turn_bank(n), :], ACT.Copy,
                       scale=prm[:, g + k:g + k + 1]).then_inc(hi_sem, 1)

    def turn_lo(dve, n, dst, g, hi_sem, sp_sem):
        half, k = n // 8, n % 8
        cols = slice(half * HALF, (half + 1) * HALF)
        dve.wait_ge(hi_sem, n + 1)
        dve.scalar_tensor_tensor(out=dst[:, LO, k, cols], in0=ps[:, turn_bank(n), :], scalar=prm[:, g + k:g + k + 1],
                                 in1=dst[:, HI, k, cols].bitcast(F32), op0=ALU.mult, op1=ALU.subtract).then_inc(sp_sem, 1)

    eps_norm = sp[:, 6, 0:1]
    eps_gn = sp[:, 6, 1:2]
    rate = [sp[:, 3, :], sp[:, 4, :], sp[:, 5, :]]

    QK_COLS, V_COLS = slice(0, 2 * QK), slice(2 * QK, 2 * QK + VD)

    def reto_parts(h, j):
        if j == 0:
            return [(h - 1, 0, t) for t in (6, 7)]
        if j < 5:
            return [(h - 1, 1, 2 * (j - 1) + q) for q in range(2)]
        return [(h, 0, 2 * (j - 5) + q) for q in range(2)]

    def reto_number(hh, seg, t):
        return hh * 16 + (seg * 8 + t)

    def stage_base(lo):
        return 0 if lo == XR_PAIRS[0] else 4 * (G_PAIRS[0] - XR_PAIRS[1])

    def previous(h, j, n=1):
        return (h, j - n) if j >= n else (h - 1, j - n + NCH)

    block = nc.Block()
    with block:

        @block.sync
        def _(sp_):
            x_t = a["x"].rearrange("b (t p) d -> p (b t) d", p=P)
            for t in range(KT):
                sp_.dma_start(x_in[:, t, :], x_t[:, t, :]).then_inc(sem[f"xt{t}"], 16)
                if t == 1:
                    load_columns(sp_, 0, 0, a["w_in"][0], COL[XR_PAIRS])
                if t == 3:
                    for dst, src in ((prm, "prm"), (con, "con"), (ident, "ident"), (mask, "mask")):
                        sp_.dma_start(dst[:, :], a[src]).then_inc(sem["const_in"], 16)
            w_in = a["w_in"][0]

            def section(pairs, lo=None):
                with sp_.Fori(pairs[0] if lo is None else lo, pairs[1]) as i:
                    for slot in range(2):
                        load_columns(sp_, i, slot, w_in, i * (2 * BC) + (slot * BC + COL[pairs]))

            load_columns(sp_, 0, 1, w_in, COL[XR_PAIRS] + BC)
            section(XR_PAIRS, 1)
            section(GR_PAIRS)
            w_a, w_i = a["lru_w_a"][0], a["lru_w_i"][0]
            for n in range(LRU_BLOCKS):
                i, u = V_PAIRS[0] + n, n % 2
                for slot in range(2):
                    load_columns(sp_, i, slot, w_in, i * 2 * BC + slot * BC)
                sp_.wait_ge(sem["gw_sp"], n + 1)
                for q, w in enumerate((w_a, w_i)):
                    sp_.dma_start(graw[:, q * 2 * BC:(q + 1) * 2 * BC].rearrange("p (k c) -> p k c", k=2),
                                  w[n, :, :].rearrange("(k p) c -> p k c", p=P)).then_inc(sem["gw_in"], 16)
                if n == 0:
                    for slot in range(2):
                        sp_.wait_ge(stored[slot], 16 * GR_PAIRS[1])
                if n >= 2:
                    sp_.wait_ge(sem[f"ysto{u}"], 16)
                for dst, row in ((xc, ROW_XC), (gel, ROW_GR)):
                    sp_.dma_start(dst[:, u, :, :], scr[row + n * BC:row + (n + 1) * BC, :].rearrange(
                        "(m p) s -> p m s", p=P)).then_inc(sem[f"xg{u}"], 16)
            for slot in range(2):
                load_columns(sp_, QK_PAIRS[0], slot, w_in, slot * BC)
            for u in range(2):
                sp_.wait_ge(sem[f"ysto{u}"], 32)
            for dst, src in ((cos, "cos"), (sin, "sin")):
                sp_.dma_start(dst[:, :], a[src]).then_inc(sem["cs_in"], 16)
            section(QK_PAIRS, QK_PAIRS[0] + 1)
            section(G_PAIRS)
            with sp_.Fori(*M_PAIRS) as i:
                for slot in range(2):
                    load_columns(sp_, i, slot, w_in, i * (2 * BC) + slot * BC)
                    t = i * 2 + (slot - 2 * M_PAIRS[0])
                    sp_.wait_ge(sem["ys_sp"], t + 1)
                    sp_.wait_ge(sem["stage_free"], 2 + 8 + 16)
                    sp_.dma_start(stg[:, slot, :], scr_y[ds(t * P, P), :]).then_inc(sem[f"ys_in{slot}"], 16)
            w_ro = a["w_rnn_o"][0]
            for n in range(4):
                load_columns(sp_, PAIR_RNNO + n // 2, n % 2, w_ro, n * BC)
                if n == 0:
                    sp_.wait_ge(sem["ys_sp"], KT + 2)
                    for slot in range(2):
                        sp_.wait_ge(stored[slot], 16 * PAIR_RNNO)
                else:
                    sp_.wait_ge(sem["sg_used"], 4 * n)
                sp_.dma_start(stg[:, :, :], scr[ROW_MN + n * BC:ROW_MN + (n + 1) * BC, :].rearrange(
                    "(m p) s -> p m s", p=P)).then_inc(sem["sg_in"], 16)

            def load_reto(h, slot):
                rows = a["w_ret_o"][0][ds(h * VD, VD), :].rearrange("(k p) n -> p k n", p=P)
                r = raw[:, slot, :].rearrange("p (k c) -> p k c", k=4)
                load_block(sp_, PAIR_RETO + h, slot,
                           *((r[:, 2 * q:2 * q + 2, :], rows[:, 2 * q:2 * q + 2, slot * HALF:(slot + 1) * HALF])
                             for q in range(2)))

            for slot in range(2):
                sp_.wait_ge(blk[slot], PAIR_RNNO + 1)
            tokens = scr_v.rearrange("(c p) n -> p c n", p=P)

            def chunk_load(h, j):
                r = h * 8 + j
                slot = j % 2
                if not (isinstance(r, int) and r < 2):
                    sp_.wait_ge(sem["qsp"], r - 1)
                    sp_.wait_ge(sem["vsp"], r - 1)
                    sp_.wait_ge(sem["kt_ps"], r - 1)
                cols = slice(j * CHUNK, (j + 1) * CHUNK)
                for n, row in ((0, ROW_Q), (1, ROW_K)):
                    sp_.dma_start(qkv[:, slot, n * QK:(n + 1) * QK].rearrange("p (m c) -> p m c", m=2),
                                  scr[ds(h * QK + row, QK), cols].rearrange("(m p) c -> p m c", p=P)
                                  ).then_inc(sem[f"qr{slot}"], 16)
                sp_.dma_start(qkv[:, slot, 2 * QK:], tokens[:, j, ds(h * VD, VD)]).then_inc(sem[f"qr{slot}"], 16)

            def gate_load(h, j):
                r = h * 8 + j
                slot, cols = j % 2, slice(j * CHUNK, (j + 1) * CHUNK)
                if not (isinstance(r, int) and r < 2):
                    sp_.wait_ge(sem["y_done"], r - 1)
                sp_.dma_start(gch[:, slot, :, :], scr[ds(h * VD + ROW_G, VD), cols].rearrange("(m p) c -> p m c", p=P)
                              ).then_inc(sem[f"gr{slot}"], 16)

            chunk_load(0, 0)
            chunk_load(0, 1)
            for slot in range(2):
                load_reto(0, slot)
            gate_load(0, 0)
            for j in range(2, NCH):
                chunk_load(0, j)
                gate_load(0, j - 1)
            with sp_.Fori(1, HEADS) as h:
                for j in range(NCH):
                    chunk_load(h, j)
                    gate_load(*previous(h, j))
                    if j in (1, 2):
                        load_reto(h, j - 1)
            gate_load(HEADS - 1, 7)

            for slot in range(2):
                sp_.wait_ge(stored[slot], 16 * PAIR_RETO)
            w_o = a["w_out"][0]
            for n in range(16):
                half, t = n // 8, n % 8
                cols = slice(half * HALF, (half + 1) * HALF)
                if n >= 4:
                    sp_.wait_ge(sem["mx_f"], n - 3)
                for dst, src, row in ((msg, scr, ROW_MR), (mrb, scr_r, 0)):
                    sp_.dma_start(dst[:, n % 4, :], src[row + t * P:row + (t + 1) * P, cols]
                                  ).then_inc(sem[f"mx_in{n % 4}"], 16)
                if n == 3:
                    load_columns(sp_, PAIR_OUT, 0, w_o, 0)
                if n == 5:
                    load_columns(sp_, PAIR_OUT, 1, w_o, BC)
            sp_.wait_ge(sem["acc"], 16 * HEADS)
            for t in range(0, KT, 4):
                sp_.dma_start(x1[:, t:t + 4, :], x_t[:, t:t + 4, :]).then_inc(sem["x_re"], 16)
            for n in range(2, 4):
                load_columns(sp_, PAIR_OUT + 1, n % 2, w_o, n * BC)
            w_up, w_dn = a["w_up"][0], a["w_down"][0]
            load_columns(sp_, PAIR_FFN, 0, w_up, 0)
            load_columns(sp_, PAIR_FFN, 1, w_up, FFN)
            with sp_.Fori(0, (GROUPS - 1) // 2) as i:
                for c in range(6):
                    pair, slot = i * 3 + (PAIR_FFN + 1 + c // 2), c % 2
                    g = i * 2 + (1 + c // 3)
                    if c % 3 == 0:
                        load_columns(sp_, pair, slot, w_up, g * BC)
                    elif c % 3 == 1:
                        load_columns(sp_, pair, slot, w_up, g * BC + FFN)
                    else:
                        load_rows(sp_, pair, slot, w_dn, g * BC - BC)
            load_rows(sp_, PAIR_FFN + 16, 0, w_dn, (GROUPS - 1) * BC)
            sp_.wait_ge(sem["a_sp"], GROUPS)
            sp_.dma_start(gbc[:, :], a["final_g"]).then_inc(sem["gb_in"], 16)
            out_t = a["out"].rearrange("b (t p) d -> p (b t) d", p=P)
            for t in range(KT):
                sp_.wait_ge(sem["out_t"], t + 1)
                sp_.dma_start(out_t[:, t, :], x1[:, t, :]).then_inc(sem["out_done"], 16)
            sp_.wait_ge(sem["out_done"], 16 * KT)

        @block.gpsimd
        def _(pool):
            pool.memset(sp[:, 6, 0:1], NORM_EPS).then_inc(sem["ini"], 1)
            pool.memset(sp[:, 6, 1:2], GN_EPS).then_inc(sem["ini"], 1)
            def store(pair, slot, dst):
                pool.wait_ge(ost_ready[slot], pair + 1)
                pool.dma_start(dst, ost[:, slot, :, :] if len(dst.shape) == 3 and dst.shape[1] == 2 else
                               ost[:, slot, :, :].rearrange("p m (t c) -> p (m t) c", c=BC)).then_inc(stored[slot], 16)

            def rows(pairs):
                with pool.Fori(*pairs) as i:
                    for slot in range(2):
                        store(i, slot, scr[ds(i * (2 * BC) + (slot * BC + COL[pairs]), BC), :].rearrange(
                            "(m p) s -> p m s", p=P))

            rows(XR_PAIRS)
            rows(GR_PAIRS)
            tokens = scr_v.rearrange("(t p) n -> p t n", p=P)
            for i in range(*V_PAIRS):
                n = i - V_PAIRS[0]
                for slot in range(2):
                    store(i, slot, tokens[:, :, n * 2 * BC + slot * BC:n * 2 * BC + (slot + 1) * BC])
                pool.wait_ge(sem["yr_done"], n + 1)
                pool.dma_start(scr_y[n * BC:(n + 1) * BC, :].rearrange("(m p) s -> p m s", p=P), gel[:, n % 2, :, :]
                               ).then_inc(sem[f"ysto{n % 2}"], 16)
            rows(QK_PAIRS)
            rows(G_PAIRS)
            rows(M_PAIRS)
            for slot in range(2):
                pool.wait_ge(blk[slot], PAIR_RNNO + 1)
            pool.memset(yacc[:, :, :], 0.0).then_inc(sem["yz"], 1)

            def store_rnno(n):
                store(PAIR_RNNO + n // 2, n % 2, scr_r[n * BC:(n + 1) * BC, :].rearrange("(m p) s -> p m s", p=P))

            for n in range(3):
                store_rnno(n)

            def lo_parts(h, j):
                r, slot = h * 8 + j, j % 2
                for hi, lo, c in (("qhi", "qsp", QK_COLS), ("vhi", "vsp", V_COLS)):
                    if lo == "qsp" and isinstance(r, int) and r >= 2:
                        continue
                    pool.wait_ge(sem[hi], r + 1)
                    pool.tensor_tensor(qkvs[:, slot, LO, c], qkv[:, slot, c], qkvs[:, slot, HI, c].bitcast(F32),
                                       ALU.subtract).then_inc(sem[lo], 1)

            def state_lo(h, j):
                slot = j % 2
                pool.wait_ge(sem["s_hi"], h * 7 + (j + 1))
                pool.tensor_tensor(sts[:, slot, LO, :, :], stt[:, :, :], sts[:, slot, HI, :, :].bitcast(F32),
                                   ALU.subtract).then_inc(sem["s_sp"], 1)

            for j in range(NCH):
                lo_parts(0, j)
                if j == 1:
                    store_rnno(3)
                if j:
                    state_lo(0, j - 1)
            with pool.Fori(1, HEADS) as h:
                for j in range(NCH):
                    lo_parts(h, j)
                    if j:
                        state_lo(h, j - 1)
            for n in range(16):
                half, t = n // 8, n % 8
                pool.wait_ge(sem[f"mx_in{n % 4}"], 32 * (n // 4 + 1))
                pool.wait_ge(sem["acc"], 16 * (HEADS - 1) + 8 * half + t + 1)
                pool.tensor_tensor(msg[:, n % 4, :], msg[:, n % 4, :], yacc[:, t, half * HALF:(half + 1) * HALF],
                                   ALU.mult).then_inc(sem["mx_mul"], 1)

        @block.tensor
        def _(pe):
            for slot in range(2):
                pe.sem_inc(blk[slot], 1)
            pe.wait_ge(sem["const_in"], 16 * 4)
            in_sems = (sem["xn_done"], sem["tr_ps"], sem["nsp_done"])
            turn_pe(pe, range(8), xn_in, *in_sems)

            def evac_wait(pairs, i, slot):
                base = 0 if pairs in (XR_PAIRS, GR_PAIRS) else 8 * (G_PAIRS[0] - GR_PAIRS[1])
                return lambda job: pe.wait_ge(sem["evac"], i * 8 + (4 * slot + job + 1 - base))

            def section(pairs, lo=None, upper=None):
                with pe.Fori(pairs[0] if lo is None else lo, pairs[1]) as i:
                    for slot in range(2):
                        if slot and upper:
                            pe.wait_ge(*upper)
                        block_ready(pe, i, slot)
                        feature_jobs(pe, slot, actv, 4 * slot, evac_wait(pairs, i, slot), sem["job"])

            block_ready(pe, 0, 0)
            first_block(pe, lambda around: feature_jobs(pe, 0, actv, 0, lambda job: None, sem["job"], around),
                        xn_in, in_sems)
            block_ready(pe, 0, 1)
            feature_jobs(pe, 1, actv, 4, lambda job: None, sem["job"])
            section(XR_PAIRS, 1)
            section(GR_PAIRS)
            pe.wait_ge(sem["evac"], 8 * GR_PAIRS[1] + 4)

            gw = gws[:, :, :].rearrange("p a (g k c) -> p a g k c", g=2, k=2)
            with pe.Fori(*V_PAIRS) as i:
                for slot in range(2):
                    block_ready(pe, i, slot)
                    token_jobs(pe, slot, actv, 0,
                               lambda job: pe.wait_ge(sem["v_evac"], i * 8 + (4 * slot + job + 1 - 8 * V_PAIRS[0])),
                               sem["job"])
                    if slot == 1:
                        continue
                    n4 = i * 4 - 4 * V_PAIRS[0]
                    pe.wait_ge(sem["evac"], 8 * GR_PAIRS[1] + 8)
                    pe.wait_ge(sem["gw_sp"], i + (2 - V_PAIRS[0]))
                    pe.wait_ge(sem["x_sp"], i + (1 - V_PAIRS[0]))
                    for g in range(2):
                        for q in range(4):
                            m, half = q // 2, q % 2
                            pe.wait_ge(sem["gr_evac" if g else "gi_evac"], n4 + (q + 1))
                            for k in range(2):
                                last = mm3(pe, ps[:, 4 + q, :], lambda p: gw[:, p, g, k, m * P:(m + 1) * P],
                                           lambda p: xcs[:, p, k, half * HALF:(half + 1) * HALF], k == 0, k == 1)
                            last.then_inc(sem["gi_ps" if g else "gr_ps"], 1)
            pe.wait_ge(sem["v_evac"], 8 * LRU_BLOCKS + 3)
            pe.wait_ge(sem["gi_evac"], 4 * LRU_BLOCKS + 4)
            with pe.Fori(*QK_PAIRS) as i:
                for slot in range(2):
                    block_ready(pe, i, slot)

                    def before(job):
                        if slot == 0 and job == 3:
                            pe.wait_ge(sem["v_evac"], 8 * LRU_BLOCKS + 4)
                        pe.wait_ge(sem["qk_evac"], i * 4 + (2 * slot + job // 2 + 1 - 4 * QK_PAIRS[0]))
                    feature_jobs(pe, slot, actv, 4 * slot, before, sem["job"])
            pe.wait_ge(sem["qk_evac"], 4 * 4 + 2)
            section(G_PAIRS, upper=(sem["qk_evac"], 4 * 4 + 4))
            section(M_PAIRS)

            pe.wait_ge(sem["ys_sp"], KT + 2)
            for n in range(4):
                slot = n % 2
                if n < 2:
                    pe.wait_ge(sem["evac"], 8 * 12 + 4 + 4 * n)
                block_ready(pe, PAIR_RNNO + n // 2, slot)
                feature_jobs(pe, slot, yr, 4 * slot,
                             lambda job: pe.wait_ge(sem["sg_used"], 4 * n - 7 + job) if n >= 2 else None, sem["job"])
            pe.wait_ge(sem["sg_used"], 16)

            def q_(slot, m):
                return lambda p: qkvs[:, slot, p, m * P:(m + 1) * P]

            def k_(slot, m):
                return lambda p: qkvs[:, slot, p, QK + m * P:QK + (m + 1) * P]

            def v_(slot):
                return lambda p: qkvs[:, slot, p, 2 * QK:]

            def scores(h, j):
                r, slot = h * 8 + j, j % 2
                pe.wait_ge(sem["qsp"], r + 1)
                if not (isinstance(r, int) and r < 1):
                    pe.wait_ge(sem["sc_mk"], r)
                for m in range(2):
                    last = mm3(pe, ps[:, 0, slot * P:(slot + 1) * P], k_(slot, m), q_(slot, m), m == 0, m == 1)
                last.then_inc(sem["sc_ps"], 1)
                if not (isinstance(r, int) and r < 1):
                    pe.wait_ge(sem["km_done"], r)
                for m in range(2):
                    last = pe.transpose(ps[:, 1, m * P:(m + 1) * P], qkv[:, slot, QK + m * P:QK + (m + 1) * P], ident[:, :])
                last.then_inc(sem["kt_ps"], 1)

            def outs(h, j):
                r, slot = h * 8 + j, j % 2
                pe.wait_ge(sem["sc_sp"], r + 1)
                pe.wait_ge(sem["vsp"], r + 1)
                if not (isinstance(r, int) and r < 1):
                    pe.wait_ge(sem["on_done"], r)
                last = mm3(pe, ps[:, 2, :], lambda p: scs[:, slot, p, :], v_(slot), True, j == 0)
                if j:
                    pe.wait_ge(sem["s_sp"], h * 7 + j)
                    for m in range(2):
                        last = mm3(pe, ps[:, 2, :], q_(slot, m), lambda p: sts[:, 1 - slot, p, m, :], False, m == 1)
                last.then_inc(sem["o_done"], 1)

            def update(h, j):
                r, slot = h * 8 + j, j % 2
                pe.wait_ge(sem["km_done"], r + 1)
                pe.wait_ge(sem["vsp"], r + 1)
                if not (isinstance(r, int) and r < 1):
                    pe.wait_ge(sem["t_done"], h * 7 + j)
                for m in range(2):
                    last = mm3(pe, ps[:, 3 + m, :], lambda p: ktm[:, slot, p, m * P:(m + 1) * P], v_(slot), True, True)
                last.then_inc(sem["u_ps"], 1)

            def reto(hh, seg, t):
                n = reto_number(hh, seg, t)
                slot = t // 4
                if t == 0:
                    pe.wait_ge(sem["y_sp"], hh * 8 + (4 * seg + 4))
                if t % 4 == 0 and seg == 0:
                    block_ready(pe, hh + PAIR_RETO, slot)
                if not (isinstance(n, int) and n < 2):
                    pe.wait_ge(sem["acc"], n - 1)
                w = ws[:, slot, :, :].rearrange("p a (k c) -> p a k c", k=4)
                for k in range(4):
                    last = mm3(pe, ps[:, 6 + t % 2, :], lambda p: w[:, p, k, (t % 4) * P:(t % 4 + 1) * P],
                               lambda p: yh[:, seg, p, k, :], k == 0, k == 3)
                last.then_inc(blk[slot] if seg == 1 and t % 4 == 3 else sem["reto"], 1)

            def turn_out(h, j):
                r, slot = h * 8 + j, j % 2
                pe.wait_ge(sem["on_done"], r + 1)
                if not (isinstance(r, int) and r < 1):
                    pe.wait_ge(sem["y_done"], r)
                for m in range(4):
                    last = pe.transpose(ps[:, 5, m * P:(m + 1) * P], on[:, slot, m * P:(m + 1) * P], ident[:, :])
                last.then_inc(sem["ont_ps"], 1)

            def step(h, j):
                first = isinstance(h, int)
                scores(h, j)
                if not (first and j < 2):
                    turn_out(*previous(h, j, 2))
                if not (first and j == 0):
                    outs(*previous(h, j))
                if j < 7:
                    update(h, j)
                for n in [] if first and j < 5 else reto_parts(h, j):
                    reto(*n)

            for j in range(NCH):
                step(0, j)
            with pe.Fori(1, HEADS) as h:
                for j in range(NCH):
                    step(h, j)
            turn_out(HEADS - 1, 6)
            outs(HEADS - 1, 7)
            reto(HEADS - 1, 0, 6)
            turn_out(HEADS - 1, 7)
            reto(HEADS - 1, 0, 7)
            for t in range(8):
                reto(HEADS - 1, 1, t)

            for n in range(4):
                slot = n % 2
                block_ready(pe, PAIR_OUT + n // 2, slot)

                def before(job):
                    if n == 0 and job in (0, 2):
                        pe.wait_ge(sem["mx_sp"], 8 + 4 * job)
                    if n == 1 and job == 0:
                        pe.wait_ge(sem["acc"], 16 * HEADS)
                    if n >= 2:
                        pe.wait_ge(sem["x1_done"], 4 * n - 7 + job)
                token_jobs(pe, slot, mix, 4 * slot, before, sem["job"])
            ffn_sems = (sem["xn2"], sem["tr2_ps"], sem["n2_sp"])
            turn_pe(pe, range(4), xn1, *ffn_sems)
            pe.wait_ge(sem["x1_done"], 16)
            turn_pe(pe, range(4, 8), xn1, *ffn_sems)

            def up(g, pair, slot, val):
                block_ready(pe, pair, slot)

                def before(job):
                    if not (isinstance(g, int) and g < 2):
                        pe.wait_ge(sem["d_add"], g * 16 + (8 + 4 * val + job + 1 - 32))
                feature_jobs(pe, slot, mix, 4 * val, before, sem["gv_job"])

            def down(g, pair, slot, hslot):
                block_ready(pe, pair, slot)
                pe.wait_ge(sem["a_sp"], g + 1)
                w = ws[:, slot, :, :].rearrange("p a (k c) -> p a k c", k=2)
                for job in range(16):
                    t, half = job // 2, job % 2
                    if job < 8:
                        if isinstance(g, int) and g == GROUPS - 1:
                            pe.wait_ge(sem["d_add"], g * 16 - 7 + job)
                        else:
                            pe.wait_ge(sem["gv_evac"], g * 8 + (8 + job + 1))
                    else:
                        pe.wait_ge(sem["d_add"], g * 16 + (job - 7))
                    for k in range(2):
                        last = mm3(pe, ps[:, job % 8, :], lambda p: hact[:, hslot, p, k, t * P:(t + 1) * P],
                                   lambda p: w[:, p, k, half * HALF:(half + 1) * HALF], k == 0, k == 1)
                    last.then_inc(sem["d_ps"] if job < 15 else blk[slot], 1)

            def group(i, u):
                g = i * 2 + (1 + u) if not isinstance(i, int) else 2 * i + 1 + u
                c = 3 * u
                ps_ = [(i * 3 + (PAIR_FFN + 1 + (c + q) // 2), (c + q) % 2) for q in range(3)]
                up(g, *ps_[0], 0)
                up(g, *ps_[1], 1)
                down(g - 1, *ps_[2], u)

            block_ready(pe, PAIR_FFN, 0)
            first_block(pe, lambda around: feature_jobs(pe, 0, mix, 0, lambda job: None, sem["gv_job"], around),
                        xn1, ffn_sems)
            up(0, PAIR_FFN, 1, 1)
            group(0, 0)
            group(0, 1)
            with pe.Fori(1, (GROUPS - 1) // 2) as i:
                group(i, 0)
                group(i, 1)
            down(GROUPS - 1, PAIR_FFN + 16, 0, 0)

        @block.scalar
        def _(act):
            act.wait_ge(sem["ini"], 2)
            act.sem_inc(sem["evac"], 8)
            act.sem_inc(sem["v_evac"], 4)
            act.sem_inc(sem["gi_evac"], 4)
            for t in range(KT):
                act.wait_ge(sem[f"xt{t}"], 16)
                norm_scale_act(act, x_in, t, sem["ss_done"], sem["std_done"], xn_in)
                if t == 1:
                    split_hi(act, 0, 0)
                if t == 3:
                    act.wait_ge(sem["const_in"], 16 * 4)
                    for n in range(8):
                        turn_hi(act, n, actv, PRM["in_g"], sem["tr_ps"], sem["nhi_done"])
            split_hi(act, 0, 1)
            for n in range(8, 16):
                turn_hi(act, n, actv, PRM["in_g"], sem["tr_ps"], sem["nhi_done"])

            def job_wait(pair, slot, job):
                if job < 3:
                    act.wait_ge(sem["job"], pair * 6 + (3 * slot + job + 1))
                else:
                    act.wait_ge(blk[slot], pair + 2)

            def to_stage(lo, hi, func):
                def pair(i):
                    for slot in range(2):
                        if not (isinstance(i, int) and i == 0 and slot == 0):
                            split_after(split_hi, act, i, slot)
                        for job in range(4):
                            half, m = job // 2, job % 2
                            if half == 0:
                                act.wait_ge(sem["stage_free"], i * 4 + (2 * slot + m + 1 - stage_base(lo)))
                            job_wait(i, slot, job)
                            act.activation(stage[:, m, 4 + half * HALF:4 + (half + 1) * HALF], ps[:, 4 * slot + job, :],
                                           func).then_inc(sem["evac"], 1)

                if lo == 0:
                    pair(0)
                with act.Fori(max(lo, 1), hi) as i:
                    pair(i)

            def evac_ost(i, slot, func, base):
                act.wait_ge(stored[slot], i * 16)
                for job in range(4):
                    half, m = job // 2, job % 2
                    job_wait(i, slot, job)
                    act.activation(ost[:, slot, m, half * HALF:(half + 1) * HALF], ps[:, 4 * slot + job, :],
                                   func).then_inc(sem["evac"], 1)
                act.wait_ge(sem["evac"], i * 8 + (4 * slot + 4 + 8 + base))
                act.sem_inc(ost_ready[slot], 1)

            def to_ost(lo, hi, func):
                with act.Fori(lo, hi) as i:
                    for slot in range(2):
                        split_after(split_hi, act, i, slot)
                        evac_ost(i, slot, func, 0)

            to_stage(*XR_PAIRS, ACT.Copy)
            to_ost(*GR_PAIRS, ACT.Gelu_apprx_tanh)

            act.wait_ge(sem["sp_st"], 1)
            act.activation(sp[:, 1, :], sp[:, 0, :], ACT.Exp).then_inc(sem["sp_st"], 1)

            def evac_v(i, slot, jobs):
                n = i - V_PAIRS[0]
                for job in jobs:
                    job_wait(i, slot, job)
                    act.activation(ost[:, slot, job // 2, (job % 2) * HALF:(job % 2 + 1) * HALF], ps[:, job, :], ACT.Copy,
                                   scale=con[:, n:n + 1]).then_inc(sem["v_evac"], 1)
                if 3 in jobs:
                    act.wait_ge(sem["v_evac"], 8 * n + 4 * slot + 4 + 4)
                    act.sem_inc(ost_ready[slot], 1)

            for n in range(LRU_BLOCKS):
                i, u = V_PAIRS[0] + n, n % 2
                split_after(split_hi, act, i, 0)
                act.wait_ge(sem["gw_in"], 32 * n + 32)
                if n:
                    act.wait_ge(sem["gi_ps"], 4 * n)
                else:
                    act.wait_ge(sem["stage_free"], 2 + 8)
                act.activation(gws[:, HI, :], graw[:, :], ACT.Copy).then_inc(sem["gw_hi"], 1)
                act.wait_ge(sem[f"xg{u}"], 32 * (n // 2) + 32)
                if n:
                    act.wait_ge(sem["yr_done"], n)
                act.activation(xcs[:, HI, :, :], xc[:, u, :, :], ACT.Copy).then_inc(sem["x_hi"], 1)
                act.wait_ge(stored[0], 16 * i)
                evac_v(i, 0, range(4))
                for g, b in ((0, "b_a"), (1, "b_i")):
                    for q in range(4):
                        m, half = q // 2, q % 2
                        act.wait_ge(sem["gi_ps" if g else "gr_ps"], 4 * n + q + 1)
                        col = PRM[b] + 2 * n + m
                        act.activation(ri[:, g, m, half * HALF:(half + 1) * HALF], ps[:, 4 + q, :], ACT.Sigmoid,
                                       bias=prm[:, col:col + 1]).then_inc(sem["gi_evac" if g else "gr_evac"], 1)
                split_after(split_hi, act, i, 1)
                act.wait_ge(sem["gr_evac"], 4 * n + 4)
                if n == 0:
                    act.wait_ge(sem["rate"], 3)
                for m in range(2):
                    c = 2 * n + m
                    act.activation(ea[:, m, :], ri[:, 0, m, :], ACT.Exp, scale=sp[:, 3, c:c + 1])
                    act.activation(th[:, m, :], ri[:, 0, m, :], ACT.Tanh, scale=sp[:, 4, c:c + 1]).then_inc(
                        sem["tanh_done"], 1)
                    act.wait_ge(sem["tanh_done"], 4 * n + 2 * m + 1)
                    act.activation(ri[:, 0, m, :], ri[:, 0, m, :], ACT.Tanh, scale=sp[:, 5, c:c + 1]).then_inc(
                        sem["tanh_done"], 1)
                act.wait_ge(stored[1], 16 * i)
                evac_v(i, 1, range(0, 2))
                act.wait_ge(sem["om_done"], n + 1)
                act.activation(ri[:, 0, :, :], ri[:, 0, :, :], ACT.Sqrt).then_inc(sem["sq_done"], 1)
                evac_v(i, 1, range(2, 4))

            with act.Fori(*QK_PAIRS) as i:
                for slot in range(2):
                    split_after(split_hi, act, i, slot)
            to_stage(*G_PAIRS, ACT.Silu)
            with act.Fori(*M_PAIRS) as i:
                for slot in range(2):
                    split_after(split_hi, act, i, slot)
                    t = i * 2 + (slot - 2 * M_PAIRS[0])
                    act.wait_ge(sem[f"ys_in{slot}"], i * 16 + (16 - 16 * M_PAIRS[0]))
                    alone(act)
                    act.activation(yr[:, HI, ds(t, 1), :], stg[:, slot:slot + 1, :], ACT.Copy).then_inc(sem["ys_hi"], 1)
                    evac_ost(i, slot, ACT.Sigmoid, -8 * 8)
            for n in range(4):
                split_after(split_hi, act, PAIR_RNNO + n // 2, n % 2)

            def qk_hi(h, j):
                r, slot = h * 8 + j, j % 2
                act.wait_ge(sem[f"qr{slot}"], h * (48 * 4) + 48 * (j // 2 + 1))
                if not (isinstance(r, int) and r < 2):
                    act.wait_ge(sem["o_done"], r - 1)
                act.activation(qkvs[:, slot, HI, QK_COLS], qkv[:, slot, QK_COLS], ACT.Copy).then_inc(sem["qhi"], 1)

            def v_hi(h, j):
                r, slot = h * 8 + j, j % 2
                act.activation(qkvs[:, slot, HI, V_COLS], qkv[:, slot, V_COLS], ACT.Copy).then_inc(sem["vhi"], 1)

            def deviation(h, j):
                r, slot = h * 8 + j, j % 2
                act.wait_ge(sem["h_var"], r + 1)
                act.activation(hn[:, slot, 9:10], hn[:, slot, 8:9], ACT.Sqrt).then_inc(sem["h_std"], 1)

            def normalise(h, j):
                r, slot = h * 8 + j, j % 2
                if not (isinstance(r, int) and r < 2):
                    act.wait_ge(sem["ont_ps"], r - 1)
                act.wait_ge(sem["h_nb"], r + 1)
                act.activation(on[:, slot, :], ps[:, 2, :], ACT.Identity, scale=hn[:, slot, 11:12],
                               bias=hn[:, slot, 12:13]).then_inc(sem["on_done"], 1)

            def y_hi(h, j):
                r, slot = h * 8 + j, j % 2
                seg = j // 4
                act.wait_ge(sem["y_done"], r + 1)
                if j % 4 == 0 and not isinstance(h, int):
                    act.wait_ge(sem["acc"], h * 16 + (8 * seg - 8))
                if j % 4 == 0 and isinstance(h, int) and h > 0:
                    act.wait_ge(sem["acc"], h * 16 + 8 * seg - 8)
                act.activation(yh[:, seg, HI, :, (j % 4) * CHUNK:(j % 4 + 1) * CHUNK], ych[:, slot, :, :],
                               ACT.Copy).then_inc(sem["y_hi"], 1)

            def step(h, j, following):
                r, slot = h * 8 + j, j % 2
                first = isinstance(h, int)
                act.wait_ge(sem["kt_ps"], r + 1)
                act.activation(ktm[:, slot, HI, :], ps[:, 1, 0:QK], ACT.Copy).then_inc(sem["km_hi"], 1)
                act.wait_ge(sem["sc_mk"], r + 1)
                act.activation(scs[:, slot, HI, :], sc[:, slot, :], ACT.Copy).then_inc(sem["sc_hi"], 1)
                if not (first and j < 2):
                    y_hi(*previous(h, j, 2))
                if following:
                    qk_hi(*following)
                if not (first and j == 0):
                    deviation(*previous(h, j))
                if following:
                    v_hi(*following)
                if not (first and j == 0):
                    normalise(*previous(h, j))
                if (j == 3 and not first) or j == 5:
                    split_hi(act, h + PAIR_RETO, 0 if j == 3 else 1)
                if j < 7:
                    act.wait_ge(sem["t_done"], h * 7 + (j + 1))
                    act.activation(sts[:, slot, HI, :, :], stt[:, :, :], ACT.Copy).then_inc(sem["s_hi"], 1)

            for j in range(2):
                qk_hi(0, j)
                v_hi(0, j)
            for j in range(7):
                step(0, j, (0, j + 1) if j else None)
            with act.Fori(1, HEADS) as h:
                step(h - 1, 7, (h, 0))
                for j in range(7):
                    step(h, j, (h, j + 1))
            step(HEADS - 1, 7, None)
            y_hi(HEADS - 1, 6)
            deviation(HEADS - 1, 7)
            normalise(HEADS - 1, 7)

            for n in range(16):
                half, t = n // 8, n % 8
                if n == 1:
                    y_hi(HEADS - 1, 7)
                act.wait_ge(sem["mx_f"], n + 1)
                act.activation(mix[:, HI, t, half * HALF:(half + 1) * HALF], mxf[:, n % 2, :],
                               ACT.Copy).then_inc(sem["mx_hi"], 1)
                if n == 5:
                    split_hi(act, PAIR_OUT, 0)
            for n in range(4):
                split_after(split_hi, act, PAIR_OUT + n // 2, n % 2)
            for t in range(KT):
                act.wait_ge(sem["x1_done"], 12 + t // 2 + 1)
                norm_scale_act(act, x1, t, sem["ss2"], sem["std2"], xn1)
                if t == 3:
                    for n in range(8):
                        turn_hi(act, n, mix, PRM["ffn_g"], sem["tr2_ps"], sem["n2_hi"])
            split_hi(act, PAIR_FFN, 1)
            for n in range(8, 16):
                turn_hi(act, n, mix, PRM["ffn_g"], sem["tr2_ps"], sem["n2_hi"])

            def evac_up(g, pair, slot, val):
                for job in range(4):
                    half, m = job // 2, job % 2
                    if half == 0 and not (isinstance(g, int) and g == 0 and val == 0):
                        act.wait_ge(sem["conv_done"], g * 4 + (2 * val + m - 1))
                    if job < 3:
                        act.wait_ge(sem["gv_job"], g * 6 + (3 * val + job + 1))
                    else:
                        act.wait_ge(blk[slot], pair + 2)
                    act.activation(fst[:, m, 4 + half * HALF:4 + (half + 1) * HALF], ps[:, 4 * val + job, :],
                                   ACT.Copy).then_inc(sem["gv_evac"], 1)

            def silu_gate(g):
                for m in range(2):
                    act.wait_ge(sem["conv_done"], g * 4 + (m + 1))
                    act.activation(gt[:, m, :], gt[:, m, :], ACT.Silu).then_inc(sem["g_silu"], 1)

            def act_hi(g, hslot):
                act.wait_ge(sem["a_mul"], g + 1)
                if not (isinstance(g, int) and g < 2):
                    act.wait_ge(sem["d_add"], g * 16 - 16)
                act.activation(hact[:, hslot, HI, :, :], vt[:, :, :], ACT.Copy).then_inc(sem["a_hi"], 1)

            def group(i, u):
                g = i * 2 + (1 + u)
                c = 3 * u
                pp = [(i * 3 + (PAIR_FFN + 1 + (c + q) // 2), (c + q) % 2) for q in range(3)]
                split_after(split_hi, act, *pp[0])
                evac_up(g, *pp[0], 0)
                split_after(split_hi, act, *pp[1])
                silu_gate(g)
                evac_up(g, *pp[1], 1)
                split_after(split_hi, act, *pp[2])
                act_hi(g, 1 - u)

            evac_up(0, PAIR_FFN, 0, 0)
            split_hi(act, PAIR_FFN + 1, 0)
            silu_gate(0)
            evac_up(0, PAIR_FFN, 1, 1)
            act_hi(0, 0)
            group(0, 0)
            group(0, 1)
            with act.Fori(1, (GROUPS - 1) // 2) as i:
                group(i, 0)
                group(i, 1)

            def row_complete(t):
                act.wait_ge(sem["d_add"], 16 * (GROUPS - 1) + 2 * t + 2)
                if t >= 2:
                    act.wait_ge(sem["ss3"], t - 1)

            for t in range(KT):
                row_complete(t)
                act.activation(vt[:, t % 2, :], x1[:, t, :], ACT.Square, accum_out=rms_ss[:, t:t + 1]).then_inc(sem["ss3"], 1)
                act.wait_ge(sem["ss3"], t + 1)
                act.activation(rms_rs[:, t:t + 1], rms_ss[:, t:t + 1], ACT.Sqrt, scale=1.0 / D,
                               bias=eps_norm[:, 0:1]).then_inc(sem["std3"], 1)

        @block.vector
        def _(dve):
            for slot in range(2):
                dve.sem_inc(w_split[slot], 1)
            for name, n in (("qk_evac", 4), ("rope_rd", 1), ("stage_free", 2), ("gw_sp", 1), ("ys_sp", 2)):
                dve.sem_inc(sem[name], n)
            for t in range(KT):
                norm_apply_dve(dve, x_in, xn_in, t, sem["std_done"], sem["rs_done"], sem["xn_done"])
                if t == 1:
                    split_lo(dve, 0, 0)
                if t == 3:
                    dve.wait_ge(sem["const_in"], 16 * 4)
                    for n in range(8):
                        turn_lo(dve, n, actv, PRM["in_g"], sem["nhi_done"], sem["nsp_done"])
            for n in range(8, 16):
                turn_lo(dve, n, actv, PRM["in_g"], sem["nhi_done"], sem["nsp_done"])

            def job_wait(pair, slot, job):
                if job < 3:
                    dve.wait_ge(sem["job"], pair * 6 + (3 * slot + job + 1))
                else:
                    dve.wait_ge(blk[slot], pair + 2)

            def stage_ready(i, slot, m, base):
                dve.wait_ge(sem["evac"], i * 8 + (4 * slot + 3 + m + 8 - base))

            dve.memset(stage[:, :, 0:4], 0.0).then_inc(sem["conv_st"], 1)
            dve.wait_ge(sem["conv_st"], 1)

            def conv(dst, src, taps, w_col, b_col, st, st_count):
                for q in range(taps):
                    tap = taps - 1 - q
                    s_ = src[:, 4 - q:4 - q + S]
                    w = prm[:, ds(w_col + tap, 1)]
                    if q == 0:
                        ins = dve.tensor_scalar(dst, s_, w, prm[:, ds(b_col, 1)], ALU.mult, ALU.add)
                    else:
                        dve.wait_ge(st, st_count + q)
                        ins = dve.scalar_tensor_tensor(out=dst, in0=s_, scalar=w, in1=dst, op0=ALU.mult, op1=ALU.add)
                    if q < taps - 1:
                        ins.then_inc(st, 1)
                return ins

            def x_rnn(i):
                for slot in range(2):
                    split_after(split_lo, dve, i, slot)
                    if not (isinstance(i, int) and i == 0):
                        dve.wait_ge(stored[slot], i * 16)
                    for m in range(2):
                        stage_ready(i, slot, m, 0)
                        c = i * 4 + (2 * slot + m - 4 * XR_PAIRS[0])
                        conv(ost[:, slot, m, :], stage[:, m, :], 4, c * 4 + PRM["conv_w"], c + PRM["conv_b"],
                             sem["conv_st"], c * 3 + 1).then_inc(sem["stage_free"], 1)
                    dve.wait_ge(sem["stage_free"], i * 4 + (2 * slot + 4))
                    dve.sem_inc(ost_ready[slot], 1)

            x_rnn(0)
            with dve.Fori(1, XR_PAIRS[1]) as i:
                x_rnn(i)
            with dve.Fori(*GR_PAIRS) as i:
                for slot in range(2):
                    split_after(split_lo, dve, i, slot)
            a_p = prm[:, PRM["a_param"]:PRM["a_param"] + 8]
            spn = [0]

            def small(ins):
                ins.then_inc(sem["l_st"], 1)
                spn[0] += 1
                dve.wait_ge(sem["l_st"], spn[0])

            small(dve.tensor_scalar(sp[:, 2, :], a_p, -1.0, None, ALU.mult))
            dve.tensor_tensor(sp[:, 0, :], a_p, sp[:, 2, :], ALU.min).then_inc(sem["sp_st"], 1)
            dve.wait_ge(sem["sp_st"], 2)
            small(dve.tensor_scalar(sp[:, 3, :], sp[:, 1, :], 2.0, None, ALU.add))
            small(dve.reciprocal(sp[:, 3, :], sp[:, 3, :]))
            small(dve.tensor_tensor(sp[:, 1, :], sp[:, 1, :], sp[:, 3, :], ALU.mult))
            small(dve.tensor_tensor(sp[:, 4, :], sp[:, 1, :], sp[:, 1, :], ALU.mult))
            small(dve.tensor_scalar(sp[:, 5, :], sp[:, 4, :], 2.0 / 17, 2.0 / 15, ALU.mult, ALU.add))
            for odd in (13, 11, 9, 7, 5, 3, 1):
                small(dve.tensor_tensor(sp[:, 5, :], sp[:, 5, :], sp[:, 4, :], ALU.mult))
                small(dve.tensor_scalar(sp[:, 5, :], sp[:, 5, :], 2.0 / odd, None, ALU.add))
            small(dve.tensor_tensor(sp[:, 5, :], sp[:, 5, :], sp[:, 1, :], ALU.mult))
            small(dve.tensor_scalar(sp[:, 2, :], sp[:, 2, :], 0.0, None, ALU.max))
            small(dve.tensor_tensor(sp[:, 7, :], sp[:, 2, :], sp[:, 5, :], ALU.add))
            for q, f in ((3, -8.0), (4, 4.0), (5, 8.0)):
                dve.tensor_scalar(sp[:, q, :], sp[:, 7, :], f, None, ALU.mult).then_inc(sem["rate"], 1)

            for n in range(LRU_BLOCKS):
                i, u = V_PAIRS[0] + n, n % 2
                split_after(split_lo, dve, i, 0)
                dve.wait_ge(sem["gw_hi"], n + 1)
                dve.tensor_tensor(gws[:, LO, :], graw[:, :], gws[:, HI, :].bitcast(F32), ALU.subtract).then_inc(
                    sem["gw_sp"], 1)
                dve.wait_ge(sem["x_hi"], n + 1)
                dve.tensor_tensor(xcs[:, LO, :, :], xc[:, u, :, :], xcs[:, HI, :, :].bitcast(F32),
                                  ALU.subtract).then_inc(sem["x_sp"], 1)
                split_after(split_lo, dve, i, 1)
                dve.wait_ge(sem["tanh_done"], 4 * n + 4)
                small(dve.scalar_tensor_tensor(out=th[:, :, :], in0=ea[:, :, :], scalar=1.0, in1=th[:, :, :],
                                               op0=ALU.add, op1=ALU.mult))
                small(dve.tensor_scalar(ea[:, :, :], th[:, :, :], -1.0, 1.0, ALU.mult, ALU.add))
                small(dve.tensor_tensor(th[:, :, :], ea[:, :, :], ea[:, :, :], ALU.mult))
                dve.scalar_tensor_tensor(out=ri[:, 0, :, :], in0=th[:, :, :], scalar=1.0, in1=ri[:, 0, :, :],
                                         op0=ALU.add, op1=ALU.mult).then_inc(sem["om_done"], 1)
                dve.wait_ge(sem["gi_evac"], 4 * n + 4 + 4)
                small(dve.tensor_tensor(ri[:, 1, :, :], ri[:, 1, :, :], xc[:, u, :, :], ALU.mult))
                dve.wait_ge(sem["sq_done"], n + 1)
                small(dve.tensor_tensor(ri[:, 1, :, :], ri[:, 1, :, :], ri[:, 0, :, :], ALU.mult))
                dve.tensor_tensor_scan(th[:, 0, :], ea[:, 0, :], ri[:, 1, 0, :], 0.0, ALU.mult, ALU.add)
                small(dve.tensor_tensor_scan(th[:, 1, :], ea[:, 1, :], ri[:, 1, 1, :], 0.0, ALU.mult, ALU.add))
                dve.tensor_tensor(gel[:, u, :, :], gel[:, u, :, :], th[:, :, :], ALU.mult).then_inc(sem["yr_done"], 1)

            def rotary(i):
                for slot in range(2):
                    split_after(split_lo, dve, i, slot)
                    dve.wait_ge(stored[slot], i * 16)
                    for half in range(2):
                        job_wait(i, slot, 2 * half + 1)
                        dve.wait_ge(sem["rope_rd"], i * 4 + (2 * slot + half + 1 - 4 * QK_PAIRS[0]))
                        cols = slice(half * HALF, (half + 1) * HALF)
                        t1, tt2 = ps[:, 4 * slot + 2 * half, :], ps[:, 4 * slot + 2 * half + 1, :]
                        dve.tensor_tensor(rope[:, 0, :], t1, cos[:, cols], ALU.mult)
                        dve.tensor_tensor(rope[:, 1, :], tt2, sin[:, cols], ALU.mult)
                        dve.tensor_tensor(rope[:, 2, :], t1, sin[:, cols], ALU.mult).then_inc(sem["rope_st"], 1)
                        dve.tensor_tensor(rope[:, 3, :], tt2, cos[:, cols], ALU.mult).then_inc(sem["qk_evac"], 1)
                        dve.wait_ge(sem["rope_st"], i * 4 + (2 * slot + half + 1 - 4 * QK_PAIRS[0]))
                        dve.wait_ge(sem["qk_evac"], i * 4 + (2 * slot + half + 1 + 4 - 4 * QK_PAIRS[0]))
                        dve.tensor_tensor(ost[:, slot, 0, cols], rope[:, 0, :], rope[:, 1, :], ALU.subtract)
                        dve.tensor_tensor(ost[:, slot, 1, cols], rope[:, 2, :], rope[:, 3, :],
                                          ALU.add).then_inc(sem["rope_rd"], 1)
                    dve.wait_ge(sem["rope_rd"], i * 4 + (2 * slot + 3 - 4 * QK_PAIRS[0]))
                    dve.sem_inc(ost_ready[slot], 1)

            dve.wait_ge(sem["cs_in"], 32)
            with dve.Fori(*QK_PAIRS) as i:
                rotary(i)
            with dve.Fori(*G_PAIRS) as i:
                for slot in range(2):
                    split_after(split_lo, dve, i, slot)
                    dve.wait_ge(stored[slot], i * 16)
                    for m in range(2):
                        stage_ready(i, slot, m, 8 * 8)
                        dve.tensor_scalar(ost[:, slot, m, :], stage[:, m, 4:],
                                          prm[:, ds(i * 4 + (2 * slot + m + PRM["gn_g"] - 4 * G_PAIRS[0]), 1)], None,
                                          ALU.mult).then_inc(sem["stage_free"], 1)
                    dve.wait_ge(sem["stage_free"], i * 4 + (2 * slot + 4 - stage_base(G_PAIRS[0])))
                    dve.sem_inc(ost_ready[slot], 1)
            with dve.Fori(*M_PAIRS) as i:
                for slot in range(2):
                    split_after(split_lo, dve, i, slot)
                    t = i * 2 + (slot - 2 * M_PAIRS[0])
                    dve.wait_ge(sem["ys_hi"], t + 1)
                    dve.tensor_tensor(yr[:, LO, ds(t, 1), :], stg[:, slot:slot + 1, :],
                                      yr[:, HI, ds(t, 1), :].bitcast(F32), ALU.subtract).then_inc(sem["ys_sp"], 1)

            for n in range(4):
                pair, slot = PAIR_RNNO + n // 2, n % 2
                split_after(split_lo, dve, pair, slot)
                dve.wait_ge(stored[slot], 16 * pair)
                dve.wait_ge(sem["sg_in"], 16 * n + 16)
                for job in range(4):
                    half, m = job // 2, job % 2
                    cols = slice(half * HALF, (half + 1) * HALF)
                    job_wait(pair, slot, job)
                    dve.tensor_tensor(ost[:, slot, m, cols], stg[:, m, cols], ps[:, 4 * slot + job, :],
                                      ALU.mult).then_inc(sem["sg_used"], 1)
                dve.wait_ge(sem["sg_used"], 4 * n + 4)
                dve.sem_inc(ost_ready[slot], 1)

            def stats(h, j):
                r, slot = h * 8 + j, j % 2
                dve.wait_ge(sem["o_done"], r + 1)
                dve.bn_stats(hn[:, slot, 0:6], ps[:, 2, :]).then_inc(sem["h_st"], 1)
                dve.wait_ge(sem["h_st"], r + 1)
                alone(dve)
                dve.bn_aggr(hn[:, slot, 6:8], hn[:, slot, 0:6]).then_inc(sem["h_ag"], 1)
                dve.wait_ge(sem["h_ag"], r + 1)
                dve.tensor_scalar(hn[:, slot, 8:9], hn[:, slot, 7:8], con[:, ds(h + CON["gam2"], 1)], eps_gn[:, 0:1],
                                  ALU.mult, ALU.add).then_inc(sem["h_var"], 1)

            def qk_lo(h, j):
                r, slot = h * 8 + j, j % 2
                dve.wait_ge(sem["qhi"], r + 1)
                dve.tensor_tensor(qkvs[:, slot, LO, QK_COLS], qkv[:, slot, QK_COLS],
                                  qkvs[:, slot, HI, QK_COLS].bitcast(F32), ALU.subtract).then_inc(sem["qsp"], 1)

            def coefficients(h, j):
                r, slot = h * 8 + j, j % 2
                dve.wait_ge(sem["h_std"], r + 1)
                dve.reciprocal(hn[:, slot, 10:11], hn[:, slot, 9:10]).then_inc(sem["h_rec"], 1)
                dve.wait_ge(sem["h_rec"], r + 1)
                dve.tensor_scalar(hn[:, slot, 11:12], hn[:, slot, 10:11], con[:, ds(h + CON["gam"], 1)], None,
                                  ALU.mult).then_inc(sem["h_rs"], 1)
                dve.wait_ge(sem["h_rs"], r + 1)
                dve.scalar_tensor_tensor(out=hn[:, slot, 12:13], in0=hn[:, slot, 6:7], scalar=-1.0,
                                         in1=hn[:, slot, 11:12], op0=ALU.mult, op1=ALU.mult).then_inc(sem["h_nb"], 1)

            def gate(h, j):
                r, slot = h * 8 + j, j % 2
                if not (isinstance(r, int) and r < 2):
                    dve.wait_ge(sem["y_sp"], r - 1)
                dve.wait_ge(sem["ont_ps"], r + 1)
                dve.wait_ge(sem[f"gr{slot}"], h * 64 + 16 * (j // 2 + 1))
                dve.tensor_tensor(ych[:, slot, :, :], ps[:, 5, :].rearrange("p (m c) -> p m c", m=4), gch[:, slot, :, :],
                                  ALU.mult).then_inc(sem["y_done"], 1)

            def gate_lo(h, j):
                r, slot = h * 8 + j, j % 2
                seg, cols = j // 4, slice((j % 4) * CHUNK, (j % 4 + 1) * CHUNK)
                dve.wait_ge(sem["y_hi"], r + 1)
                dve.tensor_tensor(yh[:, seg, LO, :, cols], ych[:, slot, :, :], yh[:, seg, HI, :, cols].bitcast(F32),
                                  ALU.subtract).then_inc(sem["y_sp"], 1)

            def accumulate(hh, seg, t):
                if seg == 1 and t % 4 == 3:
                    dve.wait_ge(blk[t // 4], hh + (PAIR_RETO + 2))
                else:
                    dve.wait_ge(sem["reto"], hh * 14 + (8 * seg + t + 1 - (seg == 1 and t > 3)))
                cols = slice(seg * HALF, (seg + 1) * HALF)
                dve.tensor_tensor(yacc[:, t, cols], yacc[:, t, cols], ps[:, 6 + t % 2, :], ALU.add).then_inc(sem["acc"], 1)

            def step(h, j):
                r, slot = h * 8 + j, j % 2
                first = isinstance(h, int)
                parts = [] if first and j < 5 else reto_parts(h, j)
                dve.wait_ge(sem["sc_ps"], r + 1)
                if not (first and j < 2):
                    dve.wait_ge(sem["sc_sp"], r - 1)
                dve.scalar_tensor_tensor(out=sc[:, slot, :], in0=ps[:, 0, slot * P:(slot + 1) * P],
                                         scalar=con[:, ds(h + CON["unchunk"], 1)], in1=mask[:, :], op0=ALU.mult,
                                         op1=ALU.mult).then_inc(sem["sc_mk"], 1)
                if not (first and j < 2):
                    gate(*previous(h, j, 2))
                dve.wait_ge(sem["km_hi"], r + 1)
                dve.tensor_tensor(ktm[:, slot, LO, :], ps[:, 1, 0:QK], ktm[:, slot, HI, :].bitcast(F32),
                                  ALU.subtract).then_inc(sem["km_done"], 1)
                dve.wait_ge(sem["sc_hi"], r + 1)
                dve.tensor_tensor(scs[:, slot, LO, :], sc[:, slot, :], scs[:, slot, HI, :].bitcast(F32),
                                  ALU.subtract).then_inc(sem["sc_sp"], 1)
                if j in (1, 5) and not (first and j == 1):
                    gate_lo(*previous(h, j, 2))
                if not (first and j == 0):
                    stats(*previous(h, j))
                if first and 1 <= j < 7:
                    qk_lo(0, j + 1)
                if j not in (1, 5) and not (first and j == 0):
                    gate_lo(*previous(h, j, 2))
                if not (first and j == 0):
                    coefficients(*previous(h, j))
                if j < 7:
                    if not (first and j == 0):
                        dve.wait_ge(sem["s_sp"], h * 7 + j)
                    dve.wait_ge(sem["u_ps"], h * 7 + (j + 1))
                    if j:
                        for m in range(2):
                            last = dve.scalar_tensor_tensor(out=stt[:, m, :], in0=stt[:, m, :],
                                                            scalar=con[:, ds(h + CON["chunk"], 1)],
                                                            in1=ps[:, 3 + m, :], op0=ALU.mult, op1=ALU.add)
                    else:
                        last = dve.tensor_copy(stt[:, :, :], ps[:, 3:5, :])
                    last.then_inc(sem["t_done"], 1)
                for n in parts[:1]:
                    accumulate(*n)
                if (j == 3 and not first) or j == 5:
                    split_lo(dve, h + PAIR_RETO, 0 if j == 3 else 1)
                for n in parts[1:]:
                    accumulate(*n)

            dve.wait_ge(sem["yz"], 1)
            for j in range(NCH):
                step(0, j)
            with dve.Fori(1, HEADS) as h:
                for j in range(NCH):
                    step(h, j)
            def mixed(n):
                dve.wait_ge(sem["mx_mul"], n + 1)
                if n >= 2:
                    dve.wait_ge(sem["mx_sp"], n - 1)
                dve.tensor_tensor(mxf[:, n % 2, :], msg[:, n % 4, :], mrb[:, n % 4, :], ALU.add).then_inc(sem["mx_f"], 1)

            def mixed_lo(n):
                half, t = n // 8, n % 8
                cols = slice(half * HALF, (half + 1) * HALF)
                dve.wait_ge(sem["mx_hi"], n + 1)
                dve.tensor_tensor(mix[:, LO, t, cols], mxf[:, n % 2, :], mix[:, HI, t, cols].bitcast(F32),
                                  ALU.subtract).then_inc(sem["mx_sp"], 1)

            gate(HEADS - 1, 6)
            stats(HEADS - 1, 7)
            gate_lo(HEADS - 1, 6)
            coefficients(HEADS - 1, 7)
            mixed(0)
            accumulate(HEADS - 1, 0, 6)
            gate(HEADS - 1, 7)
            mixed(1)
            mixed_lo(0)
            gate_lo(HEADS - 1, 7)
            accumulate(HEADS - 1, 0, 7)
            for t in range(8):
                accumulate(HEADS - 1, 1, t)
                mixed(t + 2)
                mixed_lo(t + 1)
                if t == 4:
                    split_lo(dve, PAIR_OUT, 0)
            for n in range(10, 16):
                mixed(n)
                mixed_lo(n - 1)
            mixed_lo(15)

            dve.wait_ge(sem["x_re"], 32)
            for n in range(4):
                pair, slot = PAIR_OUT + n // 2, n % 2
                split_after(split_lo, dve, pair, slot)
                for job in range(4):
                    if job < 3:
                        dve.wait_ge(sem["job"], 6 * PAIR_RETO + 3 * n + job + 1)
                    else:
                        dve.wait_ge(blk[slot], pair + 2)
                    o = x1[:, 2 * job:2 * job + 2, n * BC:(n + 1) * BC]
                    dve.tensor_tensor(o, o, ps[:, 4 * slot + job, :].rearrange("p (t c) -> p t c", t=2),
                                      ALU.add).then_inc(sem["x1_done"], 1)
                    if n == 3 and job in (1, 2):
                        for t in (2 * job - 2, 2 * job - 1):
                            norm_apply_dve(dve, x1, xn1, t, sem["std2"], sem["rs2"], sem["xn2"])
            for t in range(3, KT):
                if t > 3:
                    norm_apply_dve(dve, x1, xn1, t, sem["std2"], sem["rs2"], sem["xn2"])
                if t == 3:
                    for n in range(8):
                        turn_lo(dve, n, mix, PRM["ffn_g"], sem["n2_hi"], sem["n2_sp"])
            for n in range(8, 16):
                turn_lo(dve, n, mix, PRM["ffn_g"], sem["n2_hi"], sem["n2_sp"])
            dve.memset(fst[:, :, 0:4], 0.0).then_inc(sem["f_st"], 1)
            dve.wait_ge(sem["f_st"], 1)

            def conv_tile(g, val, m):
                dve.wait_ge(sem["gv_evac"], g * 8 + (4 * val + 3 + m))
                c = g * 2 + (22 * val + m)
                if val == 0 and not (isinstance(g, int) and g == 0):
                    dve.wait_ge(sem["a_mul"], g)
                if val == 1 and not (isinstance(g, int) and g == 0):
                    dve.wait_ge(sem["a_sp"], g)
                conv((vt if val else gt)[:, m, :], fst[:, m, :], 3, c * 3 + PRM["fconv_w"], c + PRM["fconv_b"],
                     sem["f_st"], g * 8 + (4 * val + 2 * m + 1)).then_inc(sem["conv_done"], 1)

            def multiply(g):
                dve.wait_ge(sem["g_silu"], g * 2 + 2)
                dve.wait_ge(sem["conv_done"], g * 4 + 4)
                dve.tensor_tensor(vt[:, :, :], vt[:, :, :], gt[:, :, :], ALU.mult).then_inc(sem["a_mul"], 1)

            def act_lo(g, hslot):
                dve.wait_ge(sem["a_hi"], g + 1)
                dve.tensor_tensor(hact[:, hslot, LO, :, :], vt[:, :, :], hact[:, hslot, HI, :, :].bitcast(F32),
                                  ALU.subtract).then_inc(sem["a_sp"], 1)

            def add_down(g, pair, slot, jobs):
                for job in jobs:
                    t, half = job // 2, job % 2
                    cols = slice(half * HALF, (half + 1) * HALF)
                    if job < 15:
                        dve.wait_ge(sem["d_ps"], g * 15 + (job + 1))
                    else:
                        dve.wait_ge(blk[slot], pair + 2)
                    dve.tensor_tensor(x1[:, t, cols], x1[:, t, cols], ps[:, job % 8, :], ALU.add).then_inc(sem["d_add"], 1)

            def group(i, u):
                g = i * 2 + (1 + u)
                c = 3 * u
                pp = [(i * 3 + (PAIR_FFN + 1 + (c + q) // 2), (c + q) % 2) for q in range(3)]
                split_after(split_lo, dve, *pp[0])
                conv_tile(g, 0, 0)
                conv_tile(g, 0, 1)
                split_after(split_lo, dve, *pp[1])
                conv_tile(g, 1, 0)
                add_down(g - 1, *pp[2], range(0, 4))
                conv_tile(g, 1, 1)
                add_down(g - 1, *pp[2], range(4, 8))
                multiply(g)
                split_after(split_lo, dve, *pp[2])
                add_down(g - 1, *pp[2], range(8, 12))
                act_lo(g, 1 - u)
                add_down(g - 1, *pp[2], range(12, 16))

            split_lo(dve, PAIR_FFN, 1)
            conv_tile(0, 0, 0)
            conv_tile(0, 0, 1)
            split_lo(dve, PAIR_FFN + 1, 0)
            conv_tile(0, 1, 0)
            conv_tile(0, 1, 1)
            multiply(0)
            act_lo(0, 0)
            group(0, 0)
            group(0, 1)
            with dve.Fori(1, (GROUPS - 1) // 2) as i:
                group(i, 0)
                group(i, 1)

            def finish(t):
                dve.wait_ge(sem["std3"], t + 1)
                dve.reciprocal(rms_rs[:, t:t + 1], rms_rs[:, t:t + 1]).then_inc(sem["rs3"], 1)
                dve.wait_ge(sem["rs3"], t + 1)
                dve.scalar_tensor_tensor(out=x1[:, t, :], in0=x1[:, t, :], scalar=rms_rs[:, t:t + 1], in1=gbc[:, :],
                                         op0=ALU.mult, op1=ALU.mult).then_inc(sem["out_t"], 1)

            dve.wait_ge(sem["gb_in"], 16)
            for t in range(KT):
                add_down(GROUPS - 1, PAIR_FFN + 16, 0, (2 * t, 2 * t + 1))
                if t:
                    finish(t - 1)
            finish(KT - 1)


def kernel(**inputs):
    import numpy as np
    import concourse.bacc as bacc
    from concourse.bass_utils import run_bass_kernel_spmd

    nc = bacc.Bacc("TRN2", target_bir_lowering=False, num_devices=1)
    get = {k: np.asarray(v) for k, v in inputs.items()}
    arrays, aps = {}, {}

    def dram_in(name, array):
        arrays[name] = np.ascontiguousarray(array)
        aps[name] = nc.dram_tensor(name, array.shape, F32, kind="ExternalInput").ap()

    for name in ("x", "w_in", "w_ret_o", "lru_w_a", "lru_w_i", "w_rnn_o", "w_out", "w_up", "w_down"):
        dram_in(name, get[name])

    def columns(v):
        return v.reshape(-1, P).T

    def tap_columns(w):
        taps, ch = w.shape
        return w.reshape(taps, ch // P, P).transpose(2, 1, 0).reshape(P, -1)

    dram_in("prm", np.concatenate(
        [columns(get["in_norm_g"][0]), columns(get["ffn_norm_g"][0]), columns(get["ret_gn_g"][0]),
         tap_columns(get["lru_conv_w"][0]), columns(get["lru_conv_b"][0]), columns(get["lru_b_a"][0]),
         columns(get["lru_b_i"][0]), columns(get["lru_a_param"][0]), tap_columns(get["ffn_conv_w"][0]),
         columns(get["ffn_conv_b"][0])], axis=1))
    dram_in("final_g", np.broadcast_to(get["final_norm_g"], (P, D)))

    log_g = np.log1p(-np.exp2(-5.0 - np.arange(HEADS, dtype=np.float64)))
    pos1 = np.arange(1, CHUNK + 1, dtype=np.float64)[:, None]
    con = np.concatenate([np.exp(-log_g * pos1) / 16.0, np.exp(log_g * (pos1 + CHUNK)),
                          np.exp(2 * log_g * (pos1 + CHUNK)), np.exp(log_g * CHUNK) + 0 * pos1,
                          np.exp(-log_g * CHUNK) + 0 * pos1], axis=1)
    dram_in("con", con.astype(np.float32))
    f = np.float32
    inv_freq = f(10000.0) ** (-np.arange(0, QK, 2, dtype=f) / f(QK))
    ang = (inv_freq.astype(f)[:, None] * np.arange(S, dtype=f)[None, :]).astype(f).astype(np.float64)
    dram_in("cos", np.cos(ang).astype(f))
    dram_in("sin", np.sin(ang).astype(f))
    dram_in("ident", np.eye(P, dtype=f))
    dram_in("mask", np.triu(np.ones((P, P), dtype=f)))
    aps["out"] = nc.dram_tensor("out", (1, S, D), F32, kind="ExternalOutput").ap()

    build(nc, aps)
    r = run_bass_kernel_spmd(nc, [arrays], core_ids=[0])
    return r.results[0]["out"]
```
